# Optimizing a Trainium2 kernel written in Bass

```python
import jax, jax.numpy as jnp
from jax import lax
import numpy as np

D_MODEL = 1024
BATCH = 1
SEQ = 512
DEPTH = 2

N_MIXERS = 2
ROPE_THETA = 500000.0
RMS_EPS = 1e-6
Q_BLOCK = 128
MLA_HEADS = 16
MLA_NOPE = 128
MLA_ROPE = 64
MLA_V = 128
MLA_QK = MLA_NOPE + MLA_ROPE
MLA_Q_LORA = 384
MLA_KV_LORA = 256
MLA_IN = MLA_Q_LORA + MLA_KV_LORA + MLA_ROPE + MLA_HEADS * MLA_V
NSA_HEADS = 16
NSA_GROUPS = 4
NSA_HPG = NSA_HEADS // NSA_GROUPS
NSA_DK = 96
NSA_DV = 64
NSA_ROT = NSA_DK // 4
CMP_LEN = 32
CMP_STRIDE = 16
SEL_LEN = 64
N_SELECT = 16
WINDOW = 512
NSA_Q_BLOCK = 64
SEL_FORCE = 1e4
NSA_SIZES = (NSA_HEADS * NSA_DK,
             NSA_GROUPS * NSA_DK, NSA_GROUPS * NSA_DV,
             NSA_GROUPS * NSA_DK, NSA_GROUPS * NSA_DV,
             NSA_GROUPS * NSA_DK, NSA_GROUPS * NSA_DV,
             3 * NSA_HEADS, NSA_HEADS * NSA_DV)
NSA_IN = sum(NSA_SIZES)

kernel_name = "hybrid_mla_nsa_gated_trunk"

def rms_norm(x, g):
    xf = x.astype(jnp.float32)
    y = xf * lax.rsqrt(jnp.mean(xf * xf, axis=-1, keepdims=True) + RMS_EPS)
    return (y * g.astype(jnp.float32)).astype(x.dtype)

def rope(x, pos, rot_dim):
    half = rot_dim // 2
    inv_freq = ROPE_THETA ** (-jnp.arange(half, dtype=jnp.float32) / half)
    ang = pos.astype(jnp.float32)[:, :, None] * inv_freq
    cos = jnp.cos(ang)[:, :, None, :]
    sin = jnp.sin(ang)[:, :, None, :]
    xf = x[..., :rot_dim].astype(jnp.float32)
    x1, x2 = xf[..., :half], xf[..., half:]
    rot = jnp.concatenate([x1 * cos - x2 * sin, x2 * cos + x1 * sin], axis=-1)
    return jnp.concatenate([rot.astype(x.dtype), x[..., rot_dim:]], axis=-1)

def masked_softmax(s, mask):
    s = jnp.where(mask, s, -jnp.inf)
    m = jnp.max(s, axis=-1, keepdims=True)
    m = jnp.where(jnp.isfinite(m), m, 0.0)
    e = jnp.exp(s - m)
    d = jnp.sum(e, axis=-1, keepdims=True)
    return e / jnp.where(d > 0, d, 1.0)

def causal_block_attention(q, k, v, scale):
    S = q.shape[1]
    outs = []
    for start in range(0, S, Q_BLOCK):
        end = min(start + Q_BLOCK, S)
        s = jnp.einsum('bqhd,bkhd->bhqk', q[:, start:end], k[:, :end],
                       preferred_element_type=jnp.float32) * scale
        mask = jnp.arange(start, end)[:, None] >= jnp.arange(end)[None, :]
        p = jax.nn.softmax(jnp.where(mask, s, -jnp.inf), axis=-1)
        outs.append(jnp.einsum('bhqk,bkhd->bqhd', p.astype(v.dtype), v[:, :end]))
    return jnp.concatenate(outs, axis=1)

def mla_mixer(h, pos, w_in, g_cq, w_uq, g_ckv, w_ukv, g_q, g_k, w_out):
    B, S, _ = h.shape
    proj = h @ w_in
    c_q, c_kv, k_pe, z = jnp.split(
        proj, [MLA_Q_LORA, MLA_Q_LORA + MLA_KV_LORA, MLA_Q_LORA + MLA_KV_LORA + MLA_ROPE], axis=-1)
    q = (rms_norm(c_q, g_cq) @ w_uq).reshape(B, S, MLA_HEADS, MLA_QK)
    kv = (rms_norm(c_kv, g_ckv) @ w_ukv).reshape(B, S, MLA_HEADS, MLA_NOPE + MLA_V)
    k_nope, v = kv[..., :MLA_NOPE], kv[..., MLA_NOPE:]
    k_pe = jnp.broadcast_to(k_pe[:, :, None, :], (B, S, MLA_HEADS, MLA_ROPE))
    k = jnp.concatenate([k_pe, k_nope], axis=-1)
    q = rope(rms_norm(q, g_q), pos, MLA_ROPE)
    k = rope(rms_norm(k, g_k), pos, MLA_ROPE)
    o = causal_block_attention(q, k, v, MLA_QK ** -0.5)
    o = o.reshape(B, S, MLA_HEADS * MLA_V) * jax.nn.silu(z)
    return o @ w_out

def compress(t, tok_idx, pe, w1, w2):
    B, _, G, d = t.shape
    n, L = tok_idx.shape
    blk = t[:, tok_idx] + pe[:, None, :]
    blk = jnp.moveaxis(blk, 3, 2).reshape(B, n, G, L * d)
    return jax.nn.silu(blk @ w1) @ w2

def nsa_mixer(h, pos, w_in, g_q, g_k, pe_k, w1_k, w2_k, pe_v, w1_v, w2_v, w_out):
    B, S, _ = h.shape
    G, HPG, DK, DV = NSA_GROUPS, NSA_HPG, NSA_DK, NSA_DV
    splits = [int(c) for c in np.cumsum(NSA_SIZES)[:-1]]
    q, kc, vc, ks, vs, kw, vw, gl, z = jnp.split(h @ w_in, splits, axis=-1)
    q = rope(rms_norm(q.reshape(B, S, NSA_HEADS, DK), g_q), pos, NSA_ROT)
    ks = rope(rms_norm(ks.reshape(B, S, G, DK), g_k[1]), pos, NSA_ROT)
    kw = rope(rms_norm(kw.reshape(B, S, G, DK), g_k[2]), pos, NSA_ROT)
    vs = vs.reshape(B, S, G, DV)
    vw = vw.reshape(B, S, G, DV)
    gates = jax.nn.sigmoid(gl).reshape(B, S, NSA_HEADS, 3)
    scale = DK ** -0.5

    n_cmp = (S - CMP_LEN) // CMP_STRIDE + 1
    cmp_start = jnp.arange(n_cmp) * CMP_STRIDE
    tok_idx = cmp_start[:, None] + jnp.arange(CMP_LEN)[None, :]
    cmp_end = cmp_start + CMP_LEN - 1
    k_cmp = compress(kc.reshape(B, S, G, DK), tok_idx, pe_k, w1_k, w2_k)
    k_cmp = rope(rms_norm(k_cmp, g_k[0]), pos[:, cmp_end], NSA_ROT)
    v_cmp = compress(vc.reshape(B, S, G, DV), tok_idx, pe_v, w1_v, w2_v)

    n_sel_blk = S // SEL_LEN
    k_sel = min(N_SELECT, n_sel_blk)
    ks_blk = ks.reshape(B, n_sel_blk, SEL_LEN, G, DK).transpose(0, 3, 1, 2, 4)
    vs_blk = vs.reshape(B, n_sel_blk, SEL_LEN, G, DV).transpose(0, 3, 1, 2, 4)
    sel_start = jnp.arange(n_sel_blk) * SEL_LEN
    overlap = ((cmp_start[:, None] < sel_start[None, :] + SEL_LEN)
               & (cmp_start[:, None] + CMP_LEN > sel_start[None, :])).astype(jnp.float32)
    blk_ids = jnp.arange(n_sel_blk)
    bi = jnp.arange(B)[:, None, None, None]
    gi = jnp.arange(G)[None, :, None, None]

    kw_pad = jnp.pad(kw, ((0, 0), (WINDOW, 0), (0, 0), (0, 0)))
    vw_pad = jnp.pad(vw, ((0, 0), (WINDOW, 0), (0, 0), (0, 0)))

    Tq = NSA_Q_BLOCK
    n_chunks = S // Tq
    q_ch = jnp.moveaxis(q.reshape(B, n_chunks, Tq, G, HPG, DK), 1, 0)
    g_ch = jnp.moveaxis(gates.reshape(B, n_chunks, Tq, G, HPG, 3), 1, 0)
    starts = jnp.arange(n_chunks, dtype=jnp.int32) * Tq

    def chunk(args):
        qc, gc, start = args
        t = start + jnp.arange(Tq)
        s_c = jnp.einsum('btghd,bngd->bghtn', qc, k_cmp,
                         preferred_element_type=jnp.float32) * scale
        p_c = masked_softmax(s_c, cmp_end[None, :] <= t[:, None])
        o_c = jnp.einsum('bghtn,bngd->btghd', p_c.astype(v_cmp.dtype), v_cmp)
        imp = jnp.einsum('bgtn,nk->bgtk', p_c.sum(axis=2), overlap)
        cur = t // SEL_LEN
        valid = sel_start[None, :] <= t[:, None]
        forced = ((blk_ids[None, :] == 0) | (blk_ids[None, :] == cur[:, None])
                  | (blk_ids[None, :] == cur[:, None] - 1))
        score = jnp.where(forced, SEL_FORCE, jnp.where(valid, imp, -1.0))
        _, sel = lax.top_k(score, k_sel)
        k_g = ks_blk[bi, gi, sel].reshape(B, G, Tq, k_sel * SEL_LEN, DK)
        v_g = vs_blk[bi, gi, sel].reshape(B, G, Tq, k_sel * SEL_LEN, DV)
        key_tok = (sel[..., None] * SEL_LEN + jnp.arange(SEL_LEN)).reshape(B, G, Tq, k_sel * SEL_LEN)
        s_s = jnp.einsum('btghd,bgtkd->bghtk', qc, k_g,
                         preferred_element_type=jnp.float32) * scale
        p_s = masked_softmax(s_s, (key_tok <= t[None, None, :, None])[:, :, None])
        o_s = jnp.einsum('bghtk,bgtkd->btghd', p_s.astype(v_g.dtype), v_g)
        kb = lax.dynamic_slice_in_dim(kw_pad, start, WINDOW + Tq, axis=1)
        vb = lax.dynamic_slice_in_dim(vw_pad, start, WINDOW + Tq, axis=1)
        kt = start - WINDOW + jnp.arange(WINDOW + Tq)
        m_w = (kt[None, :] <= t[:, None]) & (kt[None, :] > t[:, None] - WINDOW) & (kt[None, :] >= 0)
        s_w = jnp.einsum('btghd,bkgd->bghtk', qc, kb,
                         preferred_element_type=jnp.float32) * scale
        p_w = masked_softmax(s_w, m_w)
        o_w = jnp.einsum('bghtk,bkgd->btghd', p_w.astype(vb.dtype), vb)
        return gc[..., 0:1] * o_c + gc[..., 1:2] * o_s + gc[..., 2:3] * o_w

    o = lax.map(chunk, (q_ch, g_ch, starts))
    o = jnp.moveaxis(o, 0, 1).reshape(B, S, NSA_HEADS * DV) * jax.nn.silu(z)
    return o @ w_out

def setup_inputs(seed: int = 0) -> dict:
    key = jax.random.key(seed)
    k = jax.random.split(key, 24)
    n_mla = (DEPTH + N_MIXERS - 1) // N_MIXERS
    n_nsa = (DEPTH + N_MIXERS - 2) // N_MIXERS

    def dense(kk, shape):
        return jax.random.normal(kk, shape, jnp.float32) * shape[-2] ** -0.5

    def gain(kk, shape):
        return 1.0 + 0.05 * jax.random.normal(kk, shape, jnp.float32)

    x = jax.random.normal(k[0], (BATCH, SEQ, D_MODEL), jnp.float32)
    offsets = jax.random.randint(k[1], (BATCH, 1), 0, 1024, dtype=jnp.int32)
    positions = offsets + jnp.arange(SEQ, dtype=jnp.int32)[None, :]
    return {
        "x": x,
        "positions": positions,
        "norm_g": gain(k[2], (DEPTH, D_MODEL)),
        "mla_w_in": dense(k[3], (n_mla, D_MODEL, MLA_IN)),
        "mla_g_cq": gain(k[4], (n_mla, MLA_Q_LORA)),
        "mla_w_uq": dense(k[5], (n_mla, MLA_Q_LORA, MLA_HEADS * MLA_QK)),
        "mla_g_ckv": gain(k[6], (n_mla, MLA_KV_LORA)),
        "mla_w_ukv": dense(k[7], (n_mla, MLA_KV_LORA, MLA_HEADS * (MLA_NOPE + MLA_V))),
        "mla_g_q": gain(k[8], (n_mla, MLA_QK)),
        "mla_g_k": gain(k[9], (n_mla, MLA_QK)),
        "mla_w_out": dense(k[10], (n_mla, MLA_HEADS * MLA_V, D_MODEL)),
        "nsa_w_in": dense(k[11], (n_nsa, D_MODEL, NSA_IN)),
        "nsa_g_q": gain(k[12], (n_nsa, NSA_DK)),
        "nsa_g_k": gain(k[13], (n_nsa, 3, NSA_DK)),
        "nsa_pe_k": 0.02 * jax.random.normal(k[14], (n_nsa, CMP_LEN, NSA_DK), jnp.float32),
        "nsa_w1_k": dense(k[15], (n_nsa, CMP_LEN * NSA_DK, NSA_DK)),
        "nsa_w2_k": dense(k[16], (n_nsa, NSA_DK, NSA_DK)),
        "nsa_pe_v": 0.02 * jax.random.normal(k[17], (n_nsa, CMP_LEN, NSA_DV), jnp.float32),
        "nsa_w1_v": dense(k[18], (n_nsa, CMP_LEN * NSA_DV, NSA_DV)),
        "nsa_w2_v": dense(k[19], (n_nsa, NSA_DV, NSA_DV)),
        "nsa_w_out": dense(k[20], (n_nsa, NSA_HEADS * NSA_DV, D_MODEL)),
    }

def reference(x, positions, norm_g, mla_w_in, mla_g_cq, mla_w_uq, mla_g_ckv, mla_w_ukv,
              mla_g_q, mla_g_k, mla_w_out, nsa_w_in, nsa_g_q, nsa_g_k, nsa_pe_k, nsa_w1_k,
              nsa_w2_k, nsa_pe_v, nsa_w1_v, nsa_w2_v, nsa_w_out):
    for i in range(DEPTH):
        h = rms_norm(x, norm_g[i])
        j = i // N_MIXERS
        if i % N_MIXERS == 0:
            y = mla_mixer(h, positions, mla_w_in[j], mla_g_cq[j], mla_w_uq[j], mla_g_ckv[j],
                          mla_w_ukv[j], mla_g_q[j], mla_g_k[j], mla_w_out[j])
        else:
            y = nsa_mixer(h, positions, nsa_w_in[j], nsa_g_q[j], nsa_g_k[j], nsa_pe_k[j],
                          nsa_w1_k[j], nsa_w2_k[j], nsa_pe_v[j], nsa_w1_v[j], nsa_w2_v[j],
                          nsa_w_out[j])
        x = x + y
    return x


_drawn_inputs = setup_inputs


def setup_inputs(seed=0):
    import zlib

    import numpy as np

    out = dict(_drawn_inputs(seed))
    spreads = {}
    factors = {'norm_g': 3.798,
     'mla_g_cq': 8.0,
     'mla_g_ckv': 7.961,
     'mla_g_q': 8.0,
     'mla_g_k': 8.0,
     'nsa_g_q': 8.0,
     'nsa_g_k': 8.0,
     'nsa_pe_k': 8.0,
     'nsa_pe_v': 64.0}
    for name, (base, spread) in spreads.items():
        noise = np.random.default_rng([zlib.crc32(name.encode()), seed]).standard_normal(out[name].shape)
        drawn = base * np.exp(spread * noise) if base else spread * noise
        out[name] = __import__('jax').numpy.asarray(drawn.astype(out[name].dtype))
    for name, factor in factors.items():
        out[name] = (out[name] * factor).astype(out[name].dtype)
    return out
```

```python
from contextlib import ExitStack

import numpy as np
import concourse.bass as bass
from concourse import mybir

F32 = mybir.dt.float32
F32R = mybir.dt.float32r
BF16 = mybir.dt.bfloat16
I32 = mybir.dt.int32
ACT = mybir.ActivationFunctionType
ALU = mybir.AluOpType
AX = mybir.AxisListType

P = 128
SEQ, DM = 512, 1024
NT = SEQ // P
EPS = 1e-6
THETA = 500000.0
NEG = -1e30
FLOOR = -1e20

H = 16
NOPE, ROPE, DV0 = 128, 64, 128
QK = NOPE + ROPE
HQK = QK // 2
CQ, CKV = 384, 256
KQ, KKV = CQ // P, CKV // P
CC = CQ + CKV + ROPE
ZZ = H * DV0
HALF0 = ROPE // 2
WQ, WKV = QK, NOPE + DV0

G, HPG, DK, DV = 4, 4, 96, 64
ROT = DK // 4
HALF1 = ROT // 2
LCMP, STRIDE = 32, 16
NCMP = (SEQ - LCMP) // STRIDE + 1
NC = 32
QW = H * DK
KVW = 3 * G * (DK + DV)
KC, VC, KS, VS, KW, VW = 0, 384, 640, 1024, 1280, 1664
GW = 3 * H
Z1 = H * DV
FREQS = HALF0 + HALF1

KP = 4
CW = 512
TWO_PI = 2 * np.pi
C1 = 6.28125
C2 = float(np.floor((TWO_PI - C1) * 2**17) / 2**17)
C3 = float(TWO_PI - C1 - C2)
ROUND = 1.5 * 2**23


class Order:

    def __init__(self, eng, sem):
        self.eng, self.sem, self.n, self.base = eng, sem, 0, 0

    def link(self, ins):
        ins.then_inc(self.sem, 1)
        self.n += 1
        self.eng.wait_ge(self.sem, self.base + self.n)

    def enter(self, i, steps):
        self.start, self.steps = self.base + self.n, steps
        self.base, self.n = self.start + i * steps, 0

    def leave(self, trips):
        assert self.n == self.steps, (self.n, self.steps)
        self.base, self.n = self.start + trips * self.steps, 0


def mm3(nc, out, a, b, start, stop):
    nc.tensor.matmul(out, a[0], b[0], start=start, stop=False)
    nc.tensor.matmul(out, a[0], b[1], start=False, stop=False)
    return nc.tensor.matmul(out, a[1], b[0], start=False, stop=stop)


def trunk(nc, x, positions, inv_freq, norm_g, mla_w_in, mla_g_cq, mla_w_uq, mla_g_ckv, mla_w_ukv,
          mla_g_q, mla_g_k, mla_w_out, nsa_w_in, nsa_g_q, nsa_g_k, nsa_pe_k, nsa_w1_k, nsa_w2_k,
          nsa_pe_v, nsa_w1_v, nsa_w2_v, nsa_w_out, out):
    with ExitStack() as whole:
        names = set()

        def sem(name):
            assert name not in names
            names.add(name)
            return whole.enter_context(nc.semaphore(name))

        def sb(ctx, name, shape, dt=F32):
            return ctx.enter_context(nc.sbuf_tensor(name, shape, dt))

        keep = lambda name, shape, dt=F32: sb(whole, name, shape, dt)
        whole.enter_context(nc.allow_non_contiguous_dma(reason="gains and positions are short"))
        bank = [whole.enter_context(nc.psum_tensor(f"bank{b}", [P, 512], F32)) for b in range(8)]

        x_sb = keep("x_sb", [P, NT, DM])
        ident = keep("ident", [P, P])
        identb = keep("identb", [P, P], BF16)
        causal = keep("causal", [P, P], BF16)
        cmask = keep("cmask", [P, NT, NC])
        zeros = keep("zeros", [P, NT * NC])
        minus_half = keep("minus_half", [P, 16])
        tcos = keep("tcos", [P, NT + 1, FREQS])
        tsin = keep("tsin", [P, NT + 1, FREQS])
        g_x = keep("g_x", [P, 2, DM // P])
        g_c = keep("g_c", [P, KQ + KKV])
        gq0 = keep("gq0", [P, QK])
        gk0 = keep("gk0", [P, QK])
        gq1 = keep("gq1", [P, DK])
        gk1 = keep("gk1", [P, 3, DK])

        w_raw = [keep(f"w_raw{s}", [P, KP, CW]) for s in range(2)]
        w_landed = [sem(f"w_landed{s}") for s in range(2)]
        w_hi_made, w_lo_made, w_used = sem("w_hi_made"), sem("w_lo_made"), sem("w_used")
        acc_done, acc_free = sem("acc_done"), sem("acc_free")
        piece_base, acc_base = [0], [0]

        def stream(ctx, loops, act_hi, act_lo, evacuate):
            at = piece_base[0]
            w_hi = [sb(ctx, f"w_hi{s}_{at}", [P, KP, CW], F32R) for s in range(2)]
            w_lo = [sb(ctx, f"w_lo{s}_{at}", [P, KP, CW], F32R) for s in range(2)]
            plan = []
            for w, col0, width, chunks, what in loops:
                kt = w.shape[0] // P
                plan.append((w, col0, width, chunks, what, kt // KP, piece_base[0], acc_base[0]))
                piece_base[0] += kt // KP * chunks
                acc_base[0] += NT * chunks
            assert piece_base[0] % 2 == 0

            def load(sp):
                for w, col0, width, chunks, what, ppc, p0, a0 in plan:
                    rows = w.rearrange("(k p) c -> p k c", p=P)

                    def chunk(c):
                        for j in range(ppc):
                            g = p0 + c * ppc + j
                            if not isinstance(g, int) or g >= 2:
                                sp.wait_ge(w_lo_made, g - 1)
                            sp.dma_start(w_raw[j % 2][:, :, 0:width],
                                         rows[:, j * KP:(j + 1) * KP, bass.ds(col0 + c * width, width)]
                                         ).then_inc(w_landed[j % 2], 16)
                    first = 1 if p0 == 0 else 0
                    if first:
                        chunk(0)
                    if chunks > first:
                        with sp.Fori(first, chunks) as c:
                            chunk(c)

            def split_hi(act, extra):
                for w, col0, width, chunks, what, ppc, p0, a0 in plan:
                    def chunk(c):
                        for j in range(ppc):
                            g = p0 + c * ppc + j
                            act.wait_ge(w_landed[j % 2], (p0 // 2 + c * (ppc // 2) + j // 2 + 1) * 16)
                            if not isinstance(g, int) or g >= 2:
                                act.wait_ge(w_used, g - 1)
                            nc.scalar.activation(w_hi[j % 2][:, :, 0:width], w_raw[j % 2][:, :, 0:width],
                                                 ACT.Copy).then_inc(w_hi_made, 1)
                            if j == 0:
                                extra(act, what, c, a0, width)
                    first = 1 if p0 == 0 else 0
                    if first:
                        chunk(0)
                    if chunks > first:
                        with act.Fori(first, chunks) as c:
                            chunk(c)

            def split_lo(pool):
                for w, col0, width, chunks, what, ppc, p0, a0 in plan:
                    with pool.Fori(0, chunks) as c:
                        for j in range(ppc):
                            pool.wait_ge(w_hi_made, p0 + c * ppc + j + 1)
                            nc.gpsimd.tensor_tensor(
                                w_lo[j % 2][:, :, 0:width], w_raw[j % 2][:, :, 0:width],
                                w_hi[j % 2][:, :, 0:width].bitcast(F32), ALU.subtract).then_inc(w_lo_made, 1)

            def products(pe):
                for w, col0, width, chunks, what, ppc, p0, a0 in plan:
                    def chunk(c):
                        for j in range(ppc):
                            pe.wait_ge(w_lo_made, p0 + c * ppc + j + 1)
                            for t in range(NT):
                                a = a0 + c * NT + t
                                if j == 0 and (not isinstance(a, int) or a >= NT):
                                    pe.wait_ge(acc_free, a - NT + 1)
                                for k in range(KP):
                                    kt = j * KP + k
                                    tok = slice(t * P, (t + 1) * P)
                                    last = mm3(nc, bank[t][:, 0:width],
                                               (act_hi[:, kt, tok], act_lo[:, kt, tok]),
                                               (w_hi[j % 2][:, k, 0:width], w_lo[j % 2][:, k, 0:width]),
                                               start=kt == 0, stop=kt == ppc * KP - 1)
                                if j == ppc - 1:
                                    last.then_inc(acc_done, 1)
                            nc.tensor.matmul(bank[4][:, 0:P], identb[:, :], identb[:, :], start=True,
                                             stop=True).then_inc(w_used, 1)
                    first = 1 if a0 == 0 else 0
                    if first:
                        chunk(0)
                    if chunks > first:
                        with pe.Fori(first, chunks) as c:
                            chunk(c)

            def evacuation(eng):
                for w, col0, width, chunks, what, ppc, p0, a0 in plan:
                    with eng.Fori(0, chunks) as c:
                        for t in range(NT):
                            eng.wait_ge(acc_done, a0 + c * NT + t + 1)
                            evacuate(what, t, c * width, width, bank[t][:, 0:width]).then_inc(acc_free, 1)

            return load, split_hi, split_lo, products, evacuation

        with ExitStack() as ctx:
            pos_i = sb(ctx, "pos_i", [P, NT + 1], I32)
            pos_f = sb(ctx, "pos_f", [P, NT + 1])
            freq = sb(ctx, "freq", [P, FREQS])
            ang = sb(ctx, "ang", [P, (NT + 1) * FREQS])
            turns = sb(ctx, "turns", [P, (NT + 1) * FREQS])
            red = sb(ctx, "red", [P, (NT + 1) * FREQS])
            quarter = sb(ctx, "quarter", [P, (NT + 1) * FREQS])
            loaded, pos_clear = sem("loaded"), sem("pos_clear")
            made, table_ready, dve_order = sem("made"), sem("table_ready"), sem("dve_order0")
            pool_order, tables_done = sem("pool_order0"), sem("tables_done")
            block = ctx.enter_context(nc.Block())

            @block.sync
            def _(sp):
                sp.wait_ge(pos_clear, 1)
                row = lambda ap: ap.rearrange("(a d) -> a d", a=1)
                pieces = [
                    (pos_i[:, 0:NT], positions[0].rearrange("(t p) -> p t", p=P)),
                    (pos_i[0:NCMP, NT:NT + 1],
                     positions[0, LCMP - 1:SEQ].rearrange("(n s) -> n s", n=1).rearrange("n s -> s n")[0:SEQ - LCMP + 1:STRIDE, :]),
                    (freq[:, :], row(inv_freq).to_broadcast([P, FREQS])),
                    (g_x[:, :, :], norm_g.rearrange("l (k p) -> p l k", p=P)),
                    (g_c[:, 0:KQ], mla_g_cq[0].rearrange("(k p) -> p k", p=P)),
                    (g_c[:, KQ:KQ + KKV], mla_g_ckv[0].rearrange("(k p) -> p k", p=P)),
                    (gq0[:, :], row(mla_g_q[0]).to_broadcast([P, QK])),
                    (gk0[:, :], row(mla_g_k[0]).to_broadcast([P, QK])),
                    (gq1[:, :], row(nsa_g_q[0]).to_broadcast([P, DK])),
                ] + [(gk1[:, b, :], row(nsa_g_k[0, b]).to_broadcast([P, DK])) for b in range(3)]
                for dst, src in pieces:
                    sp.dma_start(dst, src).then_inc(loaded, 16)
                for t in range(NT):
                    sp.dma_start(x_sb[:, t, :], x[0, t * P:(t + 1) * P, :]).then_inc(loaded, 16)
                sp.wait_ge(loaded, 16 * (len(pieces) + NT))

            @block.gpsimd
            def _(pool):
                o = Order(pool, pool_order)
                nc.gpsimd.memset(pos_i[:, :], 0).then_inc(pos_clear, 1)
                nc.gpsimd.memset(minus_half[:, :], -0.5)
                o.link(nc.gpsimd.memset(zeros[:, :], 0.0))
                z = zeros[:, 0:P]
                o.link(nc.gpsimd.affine_select(out=ident[:, :], in_=z, compare_op=ALU.not_equal, fill=1.0,
                                               base=0, pattern=[[-1, P]], channel_multiplier=1))
                nc.gpsimd.affine_select(out=identb[:, :], in_=z, compare_op=ALU.not_equal, fill=1.0,
                                        base=0, pattern=[[-1, P]], channel_multiplier=1)
                nc.gpsimd.affine_select(out=causal[:, :], in_=z, compare_op=ALU.is_ge, fill=NEG,
                                        base=0, pattern=[[-1, P]], channel_multiplier=1)
                nc.gpsimd.affine_select(out=cmask[:, :, :], in_=z.rearrange("p (i n) -> p i n", n=NC),
                                        compare_op=ALU.is_ge, fill=NEG, base=-(LCMP - 1),
                                        pattern=[[P, NT], [-STRIDE, NC]], channel_multiplier=1
                                        ).then_inc(made, 1)

            @block.vector
            def _(dve):
                o = Order(dve, dve_order)
                dve.wait_ge(loaded, 16 * (12 + NT))
                o.link(nc.vector.tensor_copy(pos_f[:, :], pos_i[:, :]))
                for t in range(NT + 1):
                    last = nc.vector.tensor_scalar(ang[:, t * FREQS:(t + 1) * FREQS], freq[:, :],
                                                   pos_f[:, t:t + 1], None, ALU.mult)
                o.link(last)
                o.link(nc.vector.tensor_scalar(turns[:, :], ang[:, :], 1 / TWO_PI, ROUND, ALU.mult, ALU.add))
                o.link(nc.vector.tensor_scalar(turns[:, :], turns[:, :], -ROUND, None, ALU.add))
                o.link(nc.vector.scalar_tensor_tensor(ang[:, :], turns[:, :], -C1, ang[:, :], ALU.mult, ALU.add))
                o.link(nc.vector.scalar_tensor_tensor(ang[:, :], turns[:, :], -C2, ang[:, :], ALU.mult, ALU.add))
                o.link(nc.vector.scalar_tensor_tensor(ang[:, :], turns[:, :], -C3, ang[:, :], ALU.mult, ALU.add))
                pi = float(np.nextafter(np.float32(np.pi), np.float32(0)))
                o.link(nc.vector.tensor_scalar(red[:, :], ang[:, :], pi, -pi, ALU.min, ALU.max))
                o.link(nc.vector.scalar_tensor_tensor(quarter[:, :], red[:, :], -1.0, red[:, :], ALU.mult, ALU.max))
                nc.vector.tensor_scalar(quarter[:, :], quarter[:, :], -1.0, float(np.pi / 2), ALU.mult,
                                        ALU.add).then_inc(table_ready, 1)
                nc.vector.tensor_scalar(gq0[:, :], gq0[:, :], float(QK) ** -0.5, None, ALU.mult)
                nc.vector.tensor_scalar(gq1[:, :], gq1[:, :], float(DK) ** -0.5, None, ALU.mult)

            @block.scalar
            def _(act):
                act.wait_ge(table_ready, 1)
                nc.scalar.activation(tsin[:, :, :].rearrange("p t f -> p (t f)"), red[:, :], ACT.Sin)
                nc.scalar.activation(tcos[:, :, :].rearrange("p t f -> p (t f)"), quarter[:, :],
                                     ACT.Sin).then_inc(tables_done, 1)
                act.wait_ge(tables_done, 1)

        def transpose_block(ctx, tag, src, kt, gain, dst_hi, dst_lo, norm=None, before=None):
            norm = norm or []
            normed = sb(ctx, f"normed_{tag}", [P, NT, kt * P]) if norm else src
            junk = sb(ctx, f"junk_{tag}", [P, DM if norm else 2])
            ms = sb(ctx, f"ms_{tag}", [P, NT, 2])
            squared, factor, scaled = sem(f"squared_{tag}"), sem(f"factor_{tag}"), sem(f"scaled_{tag}")
            turned, hi_made, lo_made = sem(f"turned_{tag}"), sem(f"hi_{tag}"), sem(f"lo_{tag}")
            pool_o, act_o = sem(f"pool_o_{tag}"), sem(f"act_o_{tag}")
            block = ctx.enter_context(nc.Block())

            @block.scalar
            def _(act):
                o = Order(act, act_o)
                for t in range(NT if norm else 0):
                    for s, (c0, width) in enumerate(norm):
                        o.link(nc.scalar.activation(junk[:, 0:width], src[:, t, c0:c0 + width], ACT.Square,
                                                    scale=float(width) ** -0.5, accum_out=ms[:, t, s:s + 1]))
                for k in range(kt):
                    act.wait_ge(turned, k + 1)
                    nc.scalar.activation(dst_hi[:, k, :], bank[k % 8][:, :], ACT.Copy,
                                         scale=gain[:, k:k + 1] if gain is not None else 1.0
                                         ).then_inc(hi_made, 1)

            @block.gpsimd
            def _(pool):
                o = Order(pool, pool_o)
                for t in range(NT if norm else 0):
                    n = len(norm)
                    pool.wait_ge(act_o, n * (t + 1))
                    o.link(nc.gpsimd.tensor_scalar(ms[:, t, 0:n], ms[:, t, 0:n], EPS, None, ALU.add))
                    nc.gpsimd.tensor_tensor(ms[:, t, 0:n], ms[:, t, 0:n], minus_half[:, 0:n],
                                            ALU.pow).then_inc(factor, 1)
                if before:
                    before(pool)

            @block.vector
            def _(dve):
                for t in range(NT if norm else 0):
                    dve.wait_ge(factor, t + 1)
                    for s, (c0, width) in enumerate(norm):
                        last = nc.vector.tensor_scalar(normed[:, t, c0:c0 + width], src[:, t, c0:c0 + width],
                                                       ms[:, t, s:s + 1], None, ALU.mult)
                    last.then_inc(scaled, 1)
                for k in range(kt):
                    dve.wait_ge(hi_made, k + 1)
                    g = gain[:, k:k + 1] if gain is not None else 1.0
                    nc.vector.scalar_tensor_tensor(dst_lo[:, k, :], bank[k % 8][:, :], g,
                                                   dst_hi[:, k, :].bitcast(F32), ALU.mult,
                                                   ALU.subtract).then_inc(lo_made, 1)

            @block.tensor
            def _(pe):
                if norm:
                    pe.wait_ge(scaled, NT)
                for k in range(kt):
                    if k >= 8:
                        pe.wait_ge(lo_made, k - 7)
                    for t in range(NT):
                        last = nc.tensor.transpose(bank[k % 8][:, t * P:(t + 1) * P],
                                                   normed[:, t, k * P:(k + 1) * P], ident[:, :])
                    last.then_inc(turned, 1)

        def run_stream(ctx, loops, act_hi, act_lo, evacuate, evac_engine):
            load, split_hi, split_lo, products, evacuation = stream(ctx, loops, act_hi, act_lo, evacuate)
            block = ctx.enter_context(nc.Block())

            @block.sync
            def _(sp):
                load(sp)

            @block.scalar
            def _(act):
                split_hi(act, lambda *a: None)

            @block.gpsimd
            def _(pool):
                split_lo(pool)

            @block.tensor
            def _(pe):
                products(pe)

            @block.vector
            def _(dve):
                evacuation(dve)

        with ExitStack() as layer:
            z_sb = sb(layer, "z_sb", [P, NT, ZZ])
            silu_done = sem("silu_done0")
            with ExitStack() as proj:
                c_hi = sb(layer, "c_hi", [P, KQ + KKV, SEQ], F32R)
                c_lo = sb(layer, "c_lo", [P, KQ + KKV, SEQ], F32R)
                kpe_sb = sb(layer, "kpe_sb", [P, NT, ROPE])
                kpe_ms = sb(layer, "kpe_ms", [P, NT, 2])
                c_sb = sb(proj, "c_sb", [P, NT, CC])
                with ExitStack() as ph:
                    h_hi = sb(ph, "h_hi", [P, DM // P, SEQ], F32R)
                    h_lo = sb(ph, "h_lo", [P, DM // P, SEQ], F32R)
                    with ExitStack() as ctx:
                        transpose_block(ctx, "x0", x_sb, DM // P, g_x[:, 0, :], h_hi, h_lo, norm=[(0, DM)])
                    with ExitStack() as ctx:
                        def evacuate(what, t, c0, width, acc):
                            dst = {"c": c_sb, "z": z_sb}[what]
                            return nc.vector.tensor_copy(dst[:, t, bass.ds(c0, width)], acc)
                        run_stream(ctx, [(mla_w_in[0], 0, CC // 2, 2, "c"), (mla_w_in[0], CC, CW, ZZ // CW, "z")],
                                   h_hi, h_lo, evacuate, "dve")

                with ExitStack() as ctx:
                    rot = sb(ctx, "rot0", [P, 4, NT, HALF0])
                    junk = sb(ctx, "junk_pe", [P, ROPE])
                    dve_o, kpe_sq = sem("dve_o_pe"), sem("kpe_sq")
                    block = ctx.enter_context(nc.Block())

                    @block.scalar
                    def _(act):
                        for t in range(NT):
                            nc.scalar.activation(junk[:, :], c_sb[:, t, CQ + CKV:CC], ACT.Square,
                                                 scale=float(QK) ** -0.5, accum_out=kpe_ms[:, t, 1:2]
                                                 ).then_inc(kpe_sq, 1)
                            act.wait_ge(kpe_sq, t + 1)
                        for t in range(NT):
                            nc.scalar.activation(z_sb[:, t, :], z_sb[:, t, :], ACT.Silu).then_inc(silu_done, 1)

                    @block.vector
                    def _(dve):
                        o = Order(dve, dve_o)
                        o.link(nc.vector.memset(kpe_ms[:, :, 0:1], EPS))
                        pe_in = c_sb[:, :, CQ + CKV:CC]
                        dve.wait_ge(kpe_sq, NT)
                        for t in range(NT):
                            last = nc.vector.tensor_tensor(pe_in[:, t, :], pe_in[:, t, :], gk0[:, 0:ROPE], ALU.mult)
                        o.link(last)
                        x1, x2 = pe_in[:, :, 0:HALF0], pe_in[:, :, HALF0:ROPE]
                        cos, sin = tcos[:, 0:NT, 0:HALF0], tsin[:, 0:NT, 0:HALF0]
                        nc.vector.tensor_tensor(rot[:, 0], x1, cos, ALU.mult)
                        nc.vector.tensor_tensor(rot[:, 1], x2, sin, ALU.mult)
                        nc.vector.tensor_tensor(rot[:, 2], x2, cos, ALU.mult)
                        o.link(nc.vector.tensor_tensor(rot[:, 3], x1, sin, ALU.mult))
                        nc.vector.tensor_tensor(kpe_sb[:, :, 0:HALF0], rot[:, 0], rot[:, 1], ALU.subtract)
                        nc.vector.tensor_tensor(kpe_sb[:, :, HALF0:ROPE], rot[:, 2], rot[:, 3], ALU.add)
                        nc.vector.tensor_scalar(kpe_ms[:, :, 1:2], kpe_ms[:, :, 1:2], EPS, None, ALU.add)
                with ExitStack() as ctx:
                    transpose_block(ctx, "c", c_sb, KQ + KKV, g_c, c_hi, c_lo, norm=[(0, CQ), (CQ, CKV)])

            with ExitStack() as ctx:
                v_all = sb(ctx, "v_all", [P, NT, ZZ])
                wh_raw = sb(ctx, "wh_raw", [P, KQ * WQ + KKV * WKV])
                wh_hi = sb(ctx, "wh_hi", [P, KQ * WQ + KKV * WKV], F32R)
                wh_lo = sb(ctx, "wh_lo", [P, KQ * WQ + KKV * WKV], F32R)
                qn = sb(ctx, "qn", [P, NT, QK])
                kn = sb(ctx, "kn", [P, NT, QK])
                rot = sb(ctx, "rotq", [P, 4, 2, HALF0])
                sq_junk = sb(ctx, "sq_junk", [P, QK + NOPE])
                ms = sb(ctx, "ms_qk", [P, NT, 2])
                qkT_hi = sb(ctx, "qkT_hi", [HQK, 4, SEQ], F32R)
                qkT_lo = sb(ctx, "qkT_lo", [HQK, 4, SEQ], F32R)
                prob = sb(ctx, "prob", [P, 2, SEQ])
                probT = sb(ctx, "probT", [P, 2, SEQ])
                negmax = sb(ctx, "negmax", [P, NT])
                rowsum = sb(ctx, "rowsum", [P, NT])
                rinv = sb(ctx, "rinv", [P, NT])
                score_bank, pt_bank, o_bank, px_bank = [bank[0], bank[1]], bank[2], bank[3], bank[4:8]
                wh_landed, wh_hi_made, wh_ready = sem("wh_landed"), sem("wh_hi_made"), sem("wh_ready")
                p_done, squares, factors = sem("p_done"), sem("squares"), sem("factors")
                qk_scaled, qk_turned_ok, px_free = sem("qk_scaled"), sem("qk_rotated"), sem("px_free")
                x_done, x_hi = sem("x_done"), sem("x_hi")
                s_done, max_done, exp_done = sem("s_done"), sem("max_done"), sem("exp_done")
                t_done, pt_ready, pv_done, o_free = sem("t_done"), sem("pt_ready"), sem("pv_done"), sem("o_free")
                act_sem, dve_sem, pool_sem = sem("act_o_mla"), sem("dve_o_mla"), sem("pool_o_mla")
                wq_of = lambda w, k: w[:, k * WQ:(k + 1) * WQ]
                wkv_of = lambda w, k: w[:, KQ * WQ + k * WKV:KQ * WQ + (k + 1) * WKV]
                block = ctx.enter_context(nc.Block())

                def positive(v):
                    return not isinstance(v, int) or v > 0

                @block.sync
                def _(sp):
                    def load(n):
                        if positive(n):
                            sp.wait_ge(wh_ready, n)
                        sp.dma_start(wh_raw[:, 0:KQ * WQ].rearrange("p (k c) -> p k c", k=KQ),
                                     mla_w_uq[0].rearrange("(k p) c -> p k c", p=P)[:, :, bass.ds(n * WQ, WQ)]
                                     ).then_inc(wh_landed, 16)
                        sp.dma_start(wh_raw[:, KQ * WQ:].rearrange("p (k c) -> p k c", k=KKV),
                                     mla_w_ukv[0].rearrange("(k p) c -> p k c", p=P)[:, :, bass.ds(n * WKV, WKV)]
                                     ).then_inc(wh_landed, 16)
                    load(0)
                    with sp.Fori(1, H) as n:
                        load(n)

                @block.tensor
                def _(pe):
                    def project(n, t):
                        if t == 0:
                            pe.wait_ge(wh_ready, n + 1)
                        if positive(8 * n + t - 3):
                            pe.wait_ge(px_free, 8 * n + t - 3)
                        tok = slice(t * P, (t + 1) * P)
                        for k in range(KQ):
                            mm3(nc, px_bank[t][:, 0:WQ], (c_hi[:, k, tok], c_lo[:, k, tok]),
                                (wq_of(wh_hi, k), wq_of(wh_lo, k)), start=k == 0, stop=k == KQ - 1)
                        for k in range(KKV):
                            last = mm3(nc, px_bank[t][:, WQ:WQ + WKV], (c_hi[:, KQ + k, tok], c_lo[:, KQ + k, tok]),
                                       (wkv_of(wh_hi, k), wkv_of(wh_lo, k)), start=k == 0, stop=k == KKV - 1)
                        last.then_inc(p_done, 1)

                    def turn(n, t):
                        if t % 2 == 0:
                            pe.wait_ge(qk_turned_ok, 2 * n + t // 2 + 1)
                        if positive(8 * n + 4 + t - 3):
                            pe.wait_ge(px_free, 8 * n + 4 + t - 3)
                        for part in range(4):
                            src = (qn, kn)[part // 2][:, t, (part % 2) * HQK:(part % 2 + 1) * HQK]
                            last = nc.tensor.transpose(px_bank[t][0:HQK, part * P:(part + 1) * P], src, ident[:, :])
                        last.then_inc(x_done, 1)

                    def scores(h, i):
                        if i == 0:
                            pe.wait_ge(px_free, 8 * h + 8)
                        tok, keys = slice(i * P, (i + 1) * P), (i + 1) * P
                        dst = score_bank[i % 2]
                        for part in range(2):
                            mm3(nc, dst[:, 0:keys], (qkT_hi[:, part, tok], qkT_lo[:, part, tok]),
                                (qkT_hi[:, 2 + part, 0:keys], qkT_lo[:, 2 + part, 0:keys]),
                                start=part == 0, stop=False)
                        nc.tensor.matmul(dst[:, tok], identb[:, :], causal[:, :], start=False,
                                         stop=True).then_inc(s_done, 1)

                    def turn_probs(h, i):
                        pe.wait_ge(exp_done, 4 * h + i + 1)
                        for j in range(i + 1):
                            last = nc.tensor.transpose(pt_bank[:, j * P:(j + 1) * P],
                                                       prob[:, i % 2, j * P:(j + 1) * P], ident[:, :])
                        last.then_inc(t_done, 1)

                    def values(h, i):
                        pe.wait_ge(pt_ready, 4 * h + i + 1)
                        pe.wait_ge(o_free, 4 * h + i + 1)
                        for j in range(i + 1):
                            last = nc.tensor.matmul(o_bank[:, 0:DV0], probT[:, i % 2, j * P:(j + 1) * P],
                                                    v_all[:, j, bass.ds(h * DV0, DV0)],
                                                    start=j == 0, stop=j == i)
                        last.then_inc(pv_done, 1)

                    def step(h, n):
                        prj = (lambda t: project(n, t)) if n is not None else (lambda t: None)
                        trn = (lambda t: turn(n, t)) if n is not None else (lambda t: None)
                        prj(0); scores(h, 0); prj(1); scores(h, 1); turn_probs(h, 0)
                        prj(2); scores(h, 2); values(h, 0); turn_probs(h, 1)
                        prj(3); scores(h, 3); values(h, 1); turn_probs(h, 2)
                        trn(0); trn(1); values(h, 2); turn_probs(h, 3)
                        trn(2); trn(3); values(h, 3)

                    for t in range(NT):
                        project(0, t)
                    for t in range(NT):
                        turn(0, t)
                    with pe.Fori(0, H - 1) as h:
                        step(h, h + 1)
                    step(H - 1, None)

                @block.scalar
                def _(act):
                    def split_weights(n):
                        act.wait_ge(wh_landed, 32 * n + 32)
                        if positive(n):
                            act.wait_ge(p_done, 4 * n)
                        nc.scalar.activation(wh_hi[:, :], wh_raw[:, :], ACT.Copy).then_inc(wh_hi_made, 1)

                    def stats(n, t):
                        act.wait_ge(p_done, 4 * n + t + 1)
                        if t or positive(n):
                            act.wait_ge(squares, 4 * n + t)
                        src = px_bank[t]
                        nc.scalar.activation(sq_junk[:, 0:QK], src[:, 0:QK], ACT.Square, scale=float(QK) ** -0.5,
                                             accum_out=ms[:, t, 0:1])
                        nc.scalar.activation(v_all[:, t, bass.ds(n * DV0, DV0)], src[:, QK + NOPE:QK + NOPE + DV0],
                                             ACT.Copy)
                        nc.scalar.activation(sq_junk[:, QK:], src[:, QK:QK + NOPE], ACT.Square,
                                             scale=float(QK) ** -0.5, accum_out=ms[:, t, 1:2]).then_inc(squares, 1)

                    def high(n, t):
                        act.wait_ge(x_done, 4 * n + t + 1)
                        nc.scalar.activation(qkT_hi[:, :, t * P:(t + 1) * P],
                                             px_bank[t][0:HQK, :].rearrange("p (a t) -> p a t", a=4),
                                             ACT.Copy).then_inc(x_hi, 1)

                    def exponential(h, i):
                        act.wait_ge(max_done, 4 * h + i + 1)
                        if i == 0 and positive(h):
                            act.wait_ge(o_free, 4 * h + 1)
                        keys = (i + 1) * P
                        nc.scalar.activation(prob[:, i % 2, 0:keys], score_bank[i % 2][:, 0:keys], ACT.Exp,
                                             bias=negmax[:, i:i + 1], accum_out=rowsum[:, i:i + 1]
                                             ).then_inc(exp_done, 1)

                    def probs_out(h, i):
                        act.wait_ge(t_done, 4 * h + i + 1)
                        nc.scalar.activation(probT[:, i % 2, 0:(i + 1) * P], pt_bank[:, 0:(i + 1) * P],
                                             ACT.Copy).then_inc(pt_ready, 1)

                    def step(h, n, more):
                        st = (lambda t: stats(n, t)) if n is not None else (lambda t: None)
                        hi = (lambda t: high(n, t)) if n is not None else (lambda t: None)
                        st(0); exponential(h, 0); st(1); exponential(h, 1); st(2); exponential(h, 2)
                        probs_out(h, 1); st(3); exponential(h, 3); probs_out(h, 2)
                        if more:
                            split_weights(n + 1)
                        hi(0); hi(1); hi(2); hi(3)

                    split_weights(0)
                    for t in range(NT):
                        stats(0, t)
                    split_weights(1)
                    for t in range(NT):
                        high(0, t)
                    with act.Fori(0, H - 2) as h:
                        step(h, h + 1, True)
                    step(H - 2, H - 1, False)
                    step(H - 1, None, False)

                @block.gpsimd
                def _(pool):
                    o = Order(pool, pool_sem)

                    def factor(n, t):
                        pool.wait_ge(squares, 4 * n + t + 1)
                        o.link(nc.gpsimd.tensor_tensor(ms[:, t, :], ms[:, t, :], kpe_ms[:, t, :], ALU.add))
                        nc.gpsimd.tensor_tensor(ms[:, t, :], ms[:, t, :], minus_half[:, 0:2],
                                                ALU.pow).then_inc(factors, 1)
                        pool.wait_ge(factors, 4 * n + t + 1)
                        nc.gpsimd.tensor_tensor(kn[:, t, 0:ROPE], kpe_sb[:, t, :],
                                                ms[:, t, 1:2].to_broadcast([P, ROPE]), ALU.mult)

                    def rotate(n, a):
                        pool.wait_ge(qk_scaled, 4 * n + 2 * a + 2)
                        tt = slice(2 * a, 2 * a + 2)
                        x1, x2 = qn[:, tt, 0:HALF0], qn[:, tt, HALF0:ROPE]
                        cos, sin = tcos[:, tt, 0:HALF0], tsin[:, tt, 0:HALF0]
                        nc.gpsimd.tensor_tensor(rot[:, 0], x1, cos, ALU.mult)
                        nc.gpsimd.tensor_tensor(rot[:, 1], x2, sin, ALU.mult)
                        nc.gpsimd.tensor_tensor(rot[:, 2], x2, cos, ALU.mult)
                        o.link(nc.gpsimd.tensor_tensor(rot[:, 3], x1, sin, ALU.mult))
                        nc.gpsimd.tensor_tensor(x1, rot[:, 0], rot[:, 1], ALU.subtract)
                        nc.gpsimd.tensor_tensor(x2, rot[:, 2], rot[:, 3], ALU.add).then_inc(qk_turned_ok, 1)
                        pool.wait_ge(qk_turned_ok, 2 * n + a + 1)

                    def head(n):
                        for a in range(2):
                            factor(n, 2 * a)
                            factor(n, 2 * a + 1)
                            rotate(n, a)

                    with pool.Fori(0, H) as n:
                        o.enter(n, 6)
                        head(n)
                        o.leave(H)

                @block.vector
                def _(dve):
                    o = Order(dve, dve_sem)

                    def split_weights(n):
                        dve.wait_ge(wh_hi_made, n + 1)
                        nc.vector.tensor_tensor(wh_lo[:, :], wh_raw[:, :], wh_hi[:, :].bitcast(F32),
                                                ALU.subtract).then_inc(wh_ready, 1)

                    def scale(n, t):
                        dve.wait_ge(factors, 4 * n + t + 1)
                        nc.vector.scalar_tensor_tensor(qn[:, t, :], px_bank[t][:, 0:QK], ms[:, t, 0:1], gq0[:, :],
                                                       ALU.mult, ALU.mult).then_inc(qk_scaled, 1)
                        nc.vector.scalar_tensor_tensor(kn[:, t, ROPE:QK], px_bank[t][:, QK:QK + NOPE],
                                                       ms[:, t, 1:2], gk0[:, ROPE:QK], ALU.mult,
                                                       ALU.mult).then_inc(px_free, 1)

                    def low(n, t):
                        dve.wait_ge(x_hi, 4 * n + t + 1)
                        at = slice(t * P, (t + 1) * P)
                        nc.vector.tensor_tensor(qkT_lo[:, :, at],
                                                px_bank[t][0:HQK, :].rearrange("p (a t) -> p a t", a=4),
                                                qkT_hi[:, :, at].bitcast(F32), ALU.subtract).then_inc(px_free, 1)

                    def maximum(h, i):
                        dve.wait_ge(s_done, 4 * h + i + 1)
                        nc.vector.tensor_reduce(negmax[:, i:i + 1], score_bank[i % 2][:, 0:(i + 1) * P], AX.X,
                                                ALU.max, negate=True).then_inc(max_done, 1)

                    def probs_out(h, i):
                        dve.wait_ge(t_done, 4 * h + i + 1)
                        nc.vector.tensor_copy(probT[:, i % 2, 0:(i + 1) * P],
                                              pt_bank[:, 0:(i + 1) * P]).then_inc(pt_ready, 1)

                    def gate(h, i):
                        o.link(nc.vector.reciprocal(rinv[:, i:i + 1], rowsum[:, i:i + 1]))
                        dve.wait_ge(pv_done, 4 * h + i + 1)
                        at = z_sb[:, i, bass.ds(h * DV0, DV0)]
                        nc.vector.scalar_tensor_tensor(at, o_bank[:, 0:DV0], rinv[:, i:i + 1], at, ALU.mult,
                                                       ALU.mult).then_inc(o_free, 1)

                    def step(h, n, more):
                        sc = (lambda t: scale(n, t)) if n is not None else (lambda t: None)
                        lo = (lambda t: low(n, t)) if n is not None else (lambda t: None)
                        sc(0); maximum(h, 0); sc(1); maximum(h, 1); probs_out(h, 0)
                        sc(2); maximum(h, 2); gate(h, 0); sc(3); maximum(h, 3); gate(h, 1)
                        if more:
                            split_weights(n + 1)
                        lo(0); lo(1); gate(h, 2); probs_out(h, 3)
                        lo(2); lo(3); gate(h, 3)

                    nc.vector.memset(rinv[:, :], 1.0).then_inc(o_free, 1)
                    dve.wait_ge(o_free, 1)
                    split_weights(0)
                    for t in range(NT):
                        scale(0, t)
                    split_weights(1)
                    for t in range(NT):
                        low(0, t)
                    with dve.Fori(0, H - 2) as h:
                        o.enter(h, NT)
                        step(h, h + 1, True)
                        o.leave(H - 2)
                    step(H - 2, H - 1, False)
                    step(H - 1, None, False)

            with ExitStack() as ph:
                o_hi = sb(ph, "o_hi", [P, ZZ // P, SEQ], F32R)
                o_lo = sb(ph, "o_lo", [P, ZZ // P, SEQ], F32R)
                with ExitStack() as ctx:
                    transpose_block(ctx, "o0", z_sb, ZZ // P, None, o_hi, o_lo)
                with ExitStack() as ctx:
                    def evacuate(what, t, c0, width, acc):
                        at = x_sb[:, t, bass.ds(c0, width)]
                        return nc.vector.tensor_tensor(at, acc, at, ALU.add)
                    run_stream(ctx, [(mla_w_out[0], 0, CW, DM // CW, "x")], o_hi, o_lo, evacuate, "dve")

        with ExitStack() as layer:
            z_sb = sb(layer, "z1_sb", [P, NT, Z1])
            mixer = ExitStack()
            qs = sb(mixer, "qs", [P, NT, QW + DK])
            kv = sb(mixer, "kv", [P, NT, KVW])
            gates = sb(mixer, "gates", [P, NT, GW])
            with ExitStack() as ph:
                h_hi = sb(ph, "h1_hi", [P, DM // P, SEQ], F32R)
                h_lo = sb(ph, "h1_lo", [P, DM // P, SEQ], F32R)
                with ExitStack() as ctx:
                    transpose_block(ctx, "x1", x_sb, DM // P, g_x[:, 1, :], h_hi, h_lo, norm=[(0, DM)])
                with ExitStack() as ctx:
                    def evacuate(what, t, c0, width, acc):
                        dst = {"q": qs, "kv": kv, "g": gates, "z": z_sb}[what]
                        return nc.vector.tensor_copy(dst[:, t, bass.ds(c0, width)], acc)
                    w = nsa_w_in[0]
                    run_stream(ctx, [(w, 0, CW, QW // CW, "q"), (w, QW, G * DK, KVW // (G * DK), "kv"),
                                     (w, QW + KVW, GW, 1, "g"), (w, QW + KVW + GW, CW, Z1 // CW, "z")],
                               h_hi, h_lo, evacuate, "dve")

            kT_hi = sb(mixer, "kT_hi", [DK, 2, G, SEQ], F32R)
            kT_lo = sb(mixer, "kT_lo", [DK, 2, G, SEQ], F32R)
            kcT_hi = sb(mixer, "kcT_hi", [DK, G, NC], F32R)
            kcT_lo = sb(mixer, "kcT_lo", [DK, G, NC], F32R)
            v_diag = sb(mixer, "v_diag", [P, G, NT, DV])

            with ExitStack() as ctx:
                sq = sb(ctx, "sq1", [P, QW])
                mean = sb(ctx, "mean1", [P, 16])
                rot = sb(ctx, "rot1", [P, 4, 16, HALF1])
                kcT = sb(ctx, "kcT", [DK, G, SEQ])
                vcT = sb(ctx, "vcT", [DV, G, SEQ])
                w1k = sb(ctx, "w1k", [DK, LCMP, DK])
                w1v = sb(ctx, "w1v", [DV, LCMP, DV])
                w2k, w2v = sb(ctx, "w2k", [DK, DK]), sb(ctx, "w2v", [DV, DV])
                pek, pev = sb(ctx, "pek", [LCMP, DK]), sb(ctx, "pev", [LCMP, DV])
                pekT, pevT = sb(ctx, "pekT", [DK, LCMP]), sb(ctx, "pevT", [DV, LCMP])
                biask, biasv = sb(ctx, "biask", [DK, 1]), sb(ctx, "biasv", [DV, 1])
                hidk, hidv = sb(ctx, "hidk", [DK, G, NC]), sb(ctx, "hidv", [DV, G, NC])
                kcmp, vcmp = sb(ctx, "kcmp", [NC, G, DK]), sb(ctx, "vcmp", [NC, G, DV])
                loaded1, dve_s, mean_ready, factor1 = sem("loaded1"), sem("dve_o1"), sem("mean_ready1"), sem("factor1")
                normed_b, turned1, copied1 = sem("normed1"), sem("turned1"), sem("copied1")
                hi1, silu1, gate1, pool_s, spread = sem("hi1"), sem("silu1"), sem("gate1"), sem("pool_o1"), sem("spread1")
                block = ctx.enter_context(nc.Block())
                work = []
                for t in range(NT):
                    work.append((lambda t=t: qs[:, t, 0:QW].rearrange("p (h d) -> p h d", d=DK), H, gq1[:, :], t))
                    for b, c0 in ((1, KS), (2, KW)):
                        work.append((lambda t=t, c0=c0: kv[:, t, c0:c0 + G * DK].rearrange("p (h d) -> p h d", d=DK),
                                     G, gk1[:, b, :], t))
                LOADS = 8

                def norm_rotate(dve, o, view, heads, gain, t, rows, number):
                    x = view[0:rows]
                    s = sq[0:rows, 0:heads * DK].rearrange("p (h d) -> p h d", d=DK)
                    o.link(nc.vector.tensor_tensor(s, x, x, ALU.mult))
                    nc.vector.tensor_reduce(mean[0:rows, 0:heads], s, AX.X, ALU.add).then_inc(mean_ready, 1)
                    dve.wait_ge(factor1, number)
                    wide = lambda a: a.to_broadcast([rows, heads, DK])
                    o.link(nc.vector.tensor_tensor(x, x, mean[0:rows, 0:heads].unsqueeze(2).to_broadcast([rows, heads, DK]), ALU.mult))
                    o.link(nc.vector.tensor_tensor(x, x, gain[0:rows].unsqueeze(1).to_broadcast([rows, heads, DK]), ALU.mult))
                    x1, x2 = x[:, :, 0:HALF1], x[:, :, HALF1:ROT]
                    cos = tcos[0:rows, t, HALF0:FREQS].unsqueeze(1).to_broadcast([rows, heads, HALF1])
                    sin = tsin[0:rows, t, HALF0:FREQS].unsqueeze(1).to_broadcast([rows, heads, HALF1])
                    r = [rot[0:rows, a, 0:heads, :] for a in range(4)]
                    nc.vector.tensor_tensor(r[0], x1, cos, ALU.mult)
                    nc.vector.tensor_tensor(r[1], x2, sin, ALU.mult)
                    nc.vector.tensor_tensor(r[2], x2, cos, ALU.mult)
                    o.link(nc.vector.tensor_tensor(r[3], x1, sin, ALU.mult))
                    nc.vector.tensor_tensor(x1, r[0], r[1], ALU.subtract)
                    nc.vector.tensor_tensor(x2, r[2], r[3], ALU.add).then_inc(normed_b, 1)
                    dve.wait_ge(normed_b, number)

                @block.sync
                def _(sp):
                    for dst, src in ((w1k[:, :, :], nsa_w1_k[0].rearrange("(l d) e -> d l e", d=DK)),
                                     (w1v[:, :, :], nsa_w1_v[0].rearrange("(l d) e -> d l e", d=DV)),
                                     (w2k[:, :], nsa_w2_k[0]), (w2v[:, :], nsa_w2_v[0]),
                                     (pek[:, :], nsa_pe_k[0]), (pev[:, :], nsa_pe_v[0])):
                        sp.dma_start(dst, src).then_inc(loaded1, 16)
                    sp.wait_ge(spread, 2)
                    for i in range(NT):
                        sp.dma_start(v_diag[i * NC:(i + 1) * NC, :, i, :], vcmp[:, :, :]).then_inc(loaded1, 16)
                    sp.wait_ge(loaded1, 16 * (6 + NT))

                @block.tensor
                def _(pe):
                    for g in range(G):
                        for t in range(NT):
                            last = nc.tensor.transpose(bank[g][0:DK, t * P:(t + 1) * P],
                                                       kv[:, t, KC + g * DK:KC + (g + 1) * DK], ident[:, :])
                        last.then_inc(turned1, 1)
                    for g in range(G):
                        for t in range(NT):
                            last = nc.tensor.transpose(bank[4 + g][0:DV, t * P:(t + 1) * P],
                                                       kv[:, t, VC + g * DV:VC + (g + 1) * DV], ident[:, :])
                        last.then_inc(turned1, 1)
                    pe.wait_ge(loaded1, 16 * 6)
                    pe.wait_ge(copied1, 1)
                    nc.tensor.transpose(bank[0][0:DK, 0:LCMP], pek[:, :], ident[0:LCMP, 0:LCMP])
                    nc.tensor.transpose(bank[0][0:DV, LCMP:2 * LCMP], pev[:, :],
                                        ident[0:LCMP, 0:LCMP]).then_inc(turned1, 1)
                    pe.wait_ge(copied1, 9)
                    for w1, srcT, peT, bb, bh, d in ((w1k, kcT, pekT, 1, 2, DK), (w1v, vcT, pevT, 3, 4, DV)):
                        for l in range(LCMP):
                            nc.tensor.matmul(bank[bb][0:d, 0:1], w1[:, l, :], peT[:, l:l + 1],
                                             start=l == 0, stop=l == LCMP - 1)
                        for l in range(LCMP):
                            rhs = srcT[:, :, l:l + (NCMP - 1) * STRIDE + 1:STRIDE]
                            last = nc.tensor.matmul(bank[bh][0:d, 0:G * NCMP].rearrange("p (g n) -> p g n", g=G),
                                                    w1[:, l, :], rhs, start=l == 0, stop=l == LCMP - 1)
                        last.then_inc(turned1, 1)
                    pe.wait_ge(silu1, 2)
                    for g in range(G):
                        last = nc.tensor.matmul(bank[5][0:NC, g * DK:(g + 1) * DK], hidk[:, g, :], w2k[:, :],
                                                start=True, stop=True)
                    last.then_inc(turned1, 1)
                    for g in range(G):
                        last = nc.tensor.matmul(bank[6][0:NC, g * DV:(g + 1) * DV], hidv[:, g, :], w2v[:, :],
                                                start=True, stop=True)
                    last.then_inc(turned1, 1)
                    pe.wait_ge(normed_b, 1)
                    for g in range(G):
                        last = nc.tensor.transpose(bank[7][0:DK, g * NC:(g + 1) * NC], kcmp[:, g, :],
                                                   ident[0:NC, 0:NC])
                    last.then_inc(turned1, 1)
                    pe.wait_ge(normed_b, 1 + len(work))
                    for b, c0 in enumerate((KS, KW)):
                        for g in range(G):
                            u = b * G + g
                            if u >= 4:
                                pe.wait_ge(hi1, u - 4 + 1 + 1)
                                pe.wait_ge(copied1, 12 + u - 4 + 1)
                            for t in range(NT):
                                last = nc.tensor.transpose(bank[u % 4][0:DK, t * P:(t + 1) * P],
                                                           kv[:, t, c0 + g * DK:c0 + (g + 1) * DK], ident[:, :])
                            last.then_inc(turned1, 1)

                @block.scalar
                def _(act):
                    nc.scalar.activation(gates[:, :, :], gates[:, :, :], ACT.Sigmoid)
                    for t in range(NT):
                        nc.scalar.activation(z_sb[:, t, :], z_sb[:, t, :], ACT.Silu).then_inc(gate1, 1)
                    act.wait_ge(turned1, 11)
                    act.wait_ge(copied1, 11)
                    nc.scalar.activation(hidk[:, :, 0:NCMP], bank[2][0:DK, 0:G * NCMP].rearrange("p (g n) -> p g n", g=G),
                                         ACT.Silu, bias=biask[:, 0:1]).then_inc(silu1, 1)
                    nc.scalar.activation(hidv[:, :, 0:NCMP], bank[4][0:DV, 0:G * NCMP].rearrange("p (g n) -> p g n", g=G),
                                         ACT.Silu, bias=biasv[:, 0:1]).then_inc(silu1, 1)
                    act.wait_ge(turned1, 14)
                    nc.scalar.activation(kcT_hi[:, :, :], bank[7][0:DK, 0:G * NC].rearrange("p (g n) -> p g n", g=G),
                                         ACT.Copy).then_inc(hi1, 1)
                    for u in range(2 * G):
                        act.wait_ge(turned1, 15 + u)
                        nc.scalar.activation(kT_hi[:, u // G, u % G, :], bank[u % 4][0:DK, :],
                                             ACT.Copy).then_inc(hi1, 1)

                @block.gpsimd
                def _(pool):
                    o = Order(pool, pool_s)
                    nc.gpsimd.memset(hidk[:, :, :], 0.0)
                    nc.gpsimd.memset(hidv[:, :, :], 0.0)
                    nc.gpsimd.memset(v_diag[:, :, :, :], 0.0)
                    nc.gpsimd.memset(qs[:, :, QW:QW + DK], 0.0).then_inc(spread, 1)
                    for number, (rows, heads) in enumerate([(NC, G)] + [(P, w[1]) for w in work]):
                        pool.wait_ge(mean_ready, number + 1)
                        m = mean[0:rows, 0:heads]
                        o.link(nc.gpsimd.tensor_scalar(m, m, 1.0 / DK, EPS, ALU.mult, ALU.add))
                        nc.gpsimd.tensor_tensor(m, m, minus_half[0:rows, 0:heads], ALU.pow).then_inc(factor1, 1)

                @block.vector
                def _(dve):
                    o = Order(dve, dve_s)
                    for g in range(G):
                        dve.wait_ge(turned1, g + 1)
                        nc.vector.tensor_copy(kcT[:, g, :], bank[g][0:DK, :]).then_inc(copied1, 1)
                    for g in range(G):
                        dve.wait_ge(turned1, G + g + 1)
                        nc.vector.tensor_copy(vcT[:, g, :], bank[4 + g][0:DV, :]).then_inc(copied1, 1)
                    dve.wait_ge(turned1, 9)
                    nc.vector.tensor_copy(pekT[:, :], bank[0][0:DK, 0:LCMP])
                    nc.vector.tensor_copy(pevT[:, :], bank[0][0:DV, LCMP:2 * LCMP]).then_inc(copied1, 1)
                    dve.wait_ge(turned1, 11)
                    dve.wait_ge(spread, 1)
                    nc.vector.tensor_copy(biask[:, :], bank[1][0:DK, 0:1]).then_inc(copied1, 1)
                    nc.vector.tensor_copy(biasv[:, :], bank[3][0:DV, 0:1]).then_inc(copied1, 1)
                    dve.wait_ge(turned1, 13)
                    nc.vector.tensor_copy(vcmp[:, :, :], bank[6][0:NC, 0:G * DV].rearrange("p (g d) -> p g d", g=G)
                                          ).then_inc(spread, 1)
                    o.link(nc.vector.tensor_copy(kcmp[:, :, :],
                                                 bank[5][0:NC, 0:G * DK].rearrange("p (g d) -> p g d", g=G)))
                    norm_rotate(dve, o, kcmp[:, :, :], G, gk1[:, 0, :], NT, NC, 1)
                    dve.wait_ge(hi1, 1)
                    nc.vector.tensor_tensor(kcT_lo[:, :, :], bank[7][0:DK, 0:G * NC].rearrange("p (g n) -> p g n", g=G),
                                            kcT_hi[:, :, :].bitcast(F32), ALU.subtract).then_inc(copied1, 1)
                    for number, (view, heads, gain, t) in enumerate(work):
                        norm_rotate(dve, o, view(), heads, gain, t, P, number + 2)
                    for u in range(2 * G):
                        dve.wait_ge(hi1, 2 + u)
                        nc.vector.tensor_tensor(kT_lo[:, u // G, u % G, :], bank[u % 4][0:DK, :],
                                                kT_hi[:, u // G, u % G, :].bitcast(F32),
                                                ALU.subtract).then_inc(copied1, 1)

            with ExitStack() as ctx:
                U = 2 * NT
                q_stage = sb(ctx, "q_stage", [P, NT, DK])
                qT_hi = sb(ctx, "qT_hi", [DK, SEQ], F32R)
                qT_lo = sb(ctx, "qT_lo", [DK, SEQ], F32R)
                prob = sb(ctx, "prob1", [P, 3, SEQ])
                probT = sb(ctx, "probT1", [P, 2, SEQ])
                negmax = sb(ctx, "negmax1", [P, U])
                sums = sb(ctx, "sums1", [P, U])
                coef = sb(ctx, "coef1", [P, U])
                c_s = sb(ctx, "c_s", [P, NT, NC])
                c_e = sb(ctx, "c_e", [P, NT, NC])
                c_eT = sb(ctx, "c_eT", [P, P])
                c_max = sb(ctx, "c_max", [P, NT])
                c_sum = sb(ctx, "c_sum", [P, NT])
                c_coef = sb(ctx, "c_coef", [P, NT])
                o_sw = sb(ctx, "o_sw", [P, NT, 2, DV])
                o_c = sb(ctx, "o_c", [P, NT, DV])
                score_bank, pt_bank, o_bank, c_bank, x_bank = bank[0:3], bank[3:5], bank[5], bank[6], bank[7]
                x_done, x_hi, q_ready = sem("x_done1"), sem("x_hi1"), sem("q_ready1")
                s_done, max_done, exp_done = sem("s_done1"), sem("max_done1"), sem("exp_done1")
                t_done, pt_ready, pv_done = sem("t_done1"), sem("pt_ready1"), sem("pv_done1")
                pt_ready_act = sem("pt_ready_act1")
                c_done, c_shift, c_exp, ct_done, ct_ready, cv_done = (sem(n) for n in (
                    "c_done", "c_shift", "c_exp", "ct_done", "ct_ready", "cv_done"))
                o_left, mixed, dve_s, pool_s = sem("o_left"), sem("mixed"), sem("dve_o2"), sem("pool_o2")
                coef_done, q_staged = sem("coef_done"), sem("q_staged")
                block = ctx.enter_context(nc.Block())
                positive = lambda v: not isinstance(v, int) or v > 0
                by_act = (1, 2, 5, 6)
                n_act, n_dve = len(by_act), U - len(by_act)

                @block.tensor
                def _(pe):
                    def turn_q(n):
                        pe.wait_ge(q_staged, n + 1)
                        for t in range(NT):
                            last = nc.tensor.transpose(x_bank[0:DK, t * P:(t + 1) * P],
                                                       q_stage[:, t, :], ident[:, :])
                        last.then_inc(x_done, 1)

                    def scores(h, g, u):
                        i, b = u // 2, u % 2
                        tok, keys = slice(i * P, (i + 1) * P), (i + 1) * P
                        dst = score_bank[u % 3]
                        mm3(nc, dst[:, 0:keys], (qT_hi[:, tok], qT_lo[:, tok]),
                            (kT_hi[:, b, g, 0:keys], kT_lo[:, b, g, 0:keys]), start=True, stop=False)
                        nc.tensor.matmul(dst[:, tok], identb[:, :], causal[:, :], start=False,
                                         stop=True).then_inc(s_done, 1)

                    def turn_probs(h, u):
                        pe.wait_ge(exp_done, U * h + u + 1)
                        i = u // 2
                        for j in range(i + 1):
                            last = nc.tensor.transpose(pt_bank[u % 2][:, j * P:(j + 1) * P],
                                                       prob[:, u % 3, j * P:(j + 1) * P], ident[:, :])
                        last.then_inc(t_done, 1)

                    def values(h, g, u):
                        i, b = u // 2, u % 2
                        if u in by_act:
                            pe.wait_ge(pt_ready_act, n_act * h + by_act.index(u) + 1)
                        else:
                            pe.wait_ge(pt_ready, n_dve * h + u + 1 - sum(a < u for a in by_act))
                        if u == 0:
                            pe.wait_ge(o_left, h + 1)
                        for j in range(i + 1):
                            c0 = (VS, VW)[b]
                            last = nc.tensor.matmul(o_bank[:, u * DV:(u + 1) * DV], probT[:, u % 2, j * P:(j + 1) * P],
                                                    kv[:, j, bass.ds(c0 + g * DV, DV)], start=j == 0, stop=j == i)
                        last.then_inc(pv_done, 1)

                    turn_q(0)
                    with pe.Fori(0, G) as g:
                        with pe.Fori(0, HPG) as hh:
                            h = g * HPG + hh
                            pe.wait_ge(q_ready, h + 1)
                            pe.wait_ge(o_left, h + 1)
                            for i in range(NT):
                                tok = slice(i * P, (i + 1) * P)
                                last = mm3(nc, c_bank[:, i * NC:(i + 1) * NC], (qT_hi[:, tok], qT_lo[:, tok]),
                                           (kcT_hi[:, g, :], kcT_lo[:, g, :]), start=True, stop=True)
                            last.then_inc(c_done, 1)
                            for u in range(U + 3):
                                if u < U:
                                    scores(h, g, u)
                                if u == U:
                                    turn_q(h + 1)
                                if 2 <= u < U + 2:
                                    turn_probs(h, u - 2)
                                if u >= 3:
                                    values(h, g, u - 3)
                                if u == 4:
                                    pe.wait_ge(c_exp, h + 1)
                                    nc.tensor.transpose(c_bank[:, 0:P], c_e[:, :, :].rearrange("p i n -> p (i n)"),
                                                        ident[:, :]).then_inc(ct_done, 1)
                                if u == 6:
                                    pe.wait_ge(ct_ready, h + 1)
                                    nc.tensor.matmul(c_bank[:, 0:NT * DV], c_eT[:, :],
                                                     v_diag[:, g, :, :].rearrange("p i d -> p (i d)"),
                                                     start=True, stop=True).then_inc(cv_done, 1)

                @block.scalar
                def _(act):
                    def high(n):
                        act.wait_ge(x_done, n + 1)
                        nc.scalar.activation(qT_hi[:, :], x_bank[0:DK, :], ACT.Copy).then_inc(x_hi, 1)

                    high(0)
                    with act.Fori(0, H) as h:
                        for u in range(U + 2):
                            if u < U:
                                act.wait_ge(max_done, U * h + u + 1)
                                keys = (u // 2 + 1) * P
                                nc.scalar.activation(prob[:, u % 3, 0:keys], score_bank[u % 3][:, 0:keys], ACT.Exp,
                                                     bias=negmax[:, u:u + 1], accum_out=sums[:, u:u + 1]
                                                     ).then_inc(exp_done, 1)
                            if u == 1:
                                act.wait_ge(c_shift, h + 1)
                                nc.scalar.activation(c_e[:, :, :], c_s[:, :, :], ACT.Exp).then_inc(c_exp, 1)
                            if u - 2 in by_act:
                                if u - 2 == by_act[-1]:
                                    high(h + 1)
                                act.wait_ge(t_done, U * h + u - 2 + 1)
                                keys = ((u - 2) // 2 + 1) * P
                                nc.scalar.activation(probT[:, (u - 2) % 2, 0:keys], pt_bank[(u - 2) % 2][:, 0:keys],
                                                     ACT.Copy).then_inc(pt_ready_act, 1)

                @block.gpsimd
                def _(pool):
                    o = Order(pool, pool_s)

                    def stage(n):
                        nc.gpsimd.tensor_copy(q_stage[:, :, :], qs[:, :, bass.ds(n * DK, DK)]).then_inc(q_staged, 1)

                    stage(0)
                    nc.gpsimd.memset(o_c[:, :, :], 0.0).then_inc(mixed, 1)
                    with pool.Fori(0, H) as h:
                        o.enter(h, 2)
                        pool.wait_ge(x_done, h + 1)
                        stage(h + 1)
                        pool.wait_ge(o_left, h + 2)
                        o.link(nc.gpsimd.tensor_tensor(o_c[:, :, :], o_c[:, :, :], o_sw[:, :, 0, :], ALU.add))
                        o.link(nc.gpsimd.tensor_tensor(o_c[:, :, :], o_c[:, :, :], o_sw[:, :, 1, :], ALU.add))
                        at = z_sb[:, :, bass.ds(h * DV, DV)]
                        nc.gpsimd.tensor_tensor(at, o_c[:, :, :], at, ALU.mult).then_inc(mixed, 1)
                        o.leave(H)

                @block.vector
                def _(dve):
                    o = Order(dve, dve_s)

                    def low(n):
                        dve.wait_ge(x_hi, n + 1)
                        nc.vector.tensor_tensor(qT_lo[:, :], x_bank[0:DK, :], qT_hi[:, :].bitcast(F32),
                                                ALU.subtract).then_inc(q_ready, 1)

                    nc.vector.memset(coef[:, :], 0.0).then_inc(o_left, 1)
                    dve.wait_ge(o_left, 1)
                    low(0)
                    with dve.Fori(0, H) as h:
                        o.enter(h, 7)
                        gate = gates[:, :, bass.ds(h * 3, 3)]
                        dve.wait_ge(c_done, h + 1)
                        o.link(nc.vector.tensor_tensor(c_s[:, :, :], c_bank[:, 0:NT * NC].rearrange("p (i n) -> p i n", n=NC),
                                                       cmask[:, :, :], ALU.add))
                        o.link(nc.vector.tensor_reduce(c_max[:, :], c_s[:, :, :], AX.X, ALU.max))
                        o.link(nc.vector.tensor_scalar(c_max[:, :], c_max[:, :], FLOOR, None, ALU.max))
                        nc.vector.tensor_tensor(c_s[:, :, :], c_s[:, :, :],
                                                c_max[:, :].unsqueeze(2).to_broadcast([P, NT, NC]),
                                                ALU.subtract).then_inc(c_shift, 1)
                        for u in range(U + 2):
                            if u < U:
                                dve.wait_ge(s_done, U * h + u + 1)
                                nc.vector.tensor_reduce(negmax[:, u:u + 1], score_bank[u % 3][:, 0:(u // 2 + 1) * P],
                                                        AX.X, ALU.max, negate=True).then_inc(max_done, 1)
                            if u == 3:
                                dve.wait_ge(c_exp, h + 1)
                                o.link(nc.vector.tensor_reduce(c_sum[:, :], c_e[:, :, :], AX.X, ALU.add))
                                o.link(nc.vector.tensor_scalar(c_sum[:, :], c_sum[:, :], 1e-30, None, ALU.max))
                                o.link(nc.vector.reciprocal(c_coef[:, :], c_sum[:, :]))
                                nc.vector.tensor_tensor(c_coef[:, :], c_coef[:, :], gate[:, :, 0], ALU.mult)
                            if u == 5:
                                dve.wait_ge(ct_done, h + 1)
                                nc.vector.tensor_copy(c_eT[:, :], c_bank[:, 0:P]).then_inc(ct_ready, 1)
                            if 0 <= u - 2 and u - 2 not in by_act:
                                if u - 2 == U - 1:
                                    low(h + 1)
                                dve.wait_ge(t_done, U * h + u - 2 + 1)
                                keys = ((u - 2) // 2 + 1) * P
                                nc.vector.tensor_copy(probT[:, (u - 2) % 2, 0:keys],
                                                      pt_bank[(u - 2) % 2][:, 0:keys]).then_inc(pt_ready, 1)
                        o.link(nc.vector.reciprocal(coef[:, :], sums[:, :]))
                        nc.vector.tensor_tensor(coef[:, :].rearrange("p (i b) -> p i b", b=2),
                                                coef[:, :].rearrange("p (i b) -> p i b", b=2), gate[:, :, 1:3], ALU.mult
                                                ).then_inc(coef_done, 1)
                        dve.wait_ge(coef_done, h + 1)
                        dve.wait_ge(cv_done, h + 1)
                        dve.wait_ge(mixed, h + 1)
                        nc.vector.tensor_tensor(o_c[:, :, :], c_bank[:, 0:NT * DV].rearrange("p (i d) -> p i d", d=DV),
                                                c_coef[:, :].unsqueeze(2).to_broadcast([P, NT, DV]), ALU.mult)
                        dve.wait_ge(pv_done, U * h + U)
                        nc.vector.tensor_tensor(o_sw[:, :, :, :].rearrange("p i b d -> p (i b) d"),
                                                o_bank[:, :].rearrange("p (u d) -> p u d", d=DV),
                                                coef[:, :].unsqueeze(2).to_broadcast([P, U, DV]),
                                                ALU.mult).then_inc(o_left, 1)
                        o.leave(H)

            mixer.close()

            with ExitStack() as ph:
                o_hi = sb(ph, "o1_hi", [P, Z1 // P, SEQ], F32R)
                o_lo = sb(ph, "o1_lo", [P, Z1 // P, SEQ], F32R)
                with ExitStack() as ctx:
                    transpose_block(ctx, "o1", z_sb, Z1 // P, None, o_hi, o_lo)
                with ExitStack() as ctx:
                    def evacuate(what, t, c0, width, acc):
                        at = x_sb[:, t, bass.ds(c0, width)]
                        return nc.vector.tensor_tensor(at, acc, at, ALU.add)
                    run_stream(ctx, [(nsa_w_out[0], 0, CW, DM // CW, "x")], o_hi, o_lo, evacuate, "dve")
                with ExitStack() as ctx:
                    stored = sem("stored")
                    block = ctx.enter_context(nc.Block())

                    @block.sync
                    def _(sp):
                        for t in range(NT):
                            sp.dma_start(out[0, t * P:(t + 1) * P, :], x_sb[:, t, :]).then_inc(stored, 16)
                        sp.wait_ge(stored, 16 * NT)


_INS = ["x", "positions", "inv_freq", "norm_g", "mla_w_in", "mla_g_cq", "mla_w_uq", "mla_g_ckv", "mla_w_ukv",
        "mla_g_q", "mla_g_k", "mla_w_out", "nsa_w_in", "nsa_g_q", "nsa_g_k", "nsa_pe_k", "nsa_w1_k",
        "nsa_w2_k", "nsa_pe_v", "nsa_w1_v", "nsa_w2_v", "nsa_w_out"]


def kernel(**inputs):
    import concourse.bacc as bacc
    from concourse.bass_utils import run_bass_kernel_spmd

    inputs["inv_freq"] = np.concatenate(
        [THETA ** (-np.arange(half) / half) for half in (HALF0, HALF1)]).astype(np.float32)
    nc = bacc.Bacc("TRN2", target_bir_lowering=False, num_devices=1)
    arrays, args = {}, []
    for name in _INS:
        a = np.ascontiguousarray(inputs[name])
        arrays[f"in_{name}"] = a
        args.append(nc.dram_tensor(f"in_{name}", a.shape, mybir.dt.from_np(a.dtype), kind="ExternalInput").ap())
    out = nc.dram_tensor("out_0", (1, SEQ, DM), F32, kind="ExternalOutput").ap()
    trunk(nc, *args, out)
    r = run_bass_kernel_spmd(nc, [arrays], core_ids=[0])
    return r.results[0]["out_0"]
```

```python
from contextlib import ExitStack

import numpy as np
import concourse.bass as bass
from concourse import mybir

F32 = mybir.dt.float32
F32R = mybir.dt.float32r
BF16 = mybir.dt.bfloat16
I32 = mybir.dt.int32
ACT = mybir.ActivationFunctionType
ALU = mybir.AluOpType
AX = mybir.AxisListType

P = 128
SEQ, DM = 512, 1024
NT = SEQ // P
EPS = 1e-6
THETA = 500000.0
NEG = -1e30
FLOOR = -1e20

H = 16
NOPE, ROPE, DV0 = 128, 64, 128
QK = NOPE + ROPE
HQK = QK // 2
CQ, CKV = 384, 256
KQ, KKV = CQ // P, CKV // P
CC = CQ + CKV + ROPE
ZZ = H * DV0
HALF0 = ROPE // 2
WQ, WKV = QK, NOPE + DV0

G, HPG, DK, DV = 4, 4, 96, 64
ROT = DK // 4
HALF1 = ROT // 2
LCMP, STRIDE = 32, 16
NCMP = (SEQ - LCMP) // STRIDE + 1
NC = 32
QW = H * DK
KVW = 3 * G * (DK + DV)
KC, VC, KS, VS, KW, VW = 0, 384, 640, 1024, 1280, 1664
GW = 3 * H
Z1 = H * DV
FREQS = HALF0 + HALF1

KP = 4
CW = 512
TWO_PI = 2 * np.pi
C1 = 6.28125
C2 = float(np.floor((TWO_PI - C1) * 2**17) / 2**17)
C3 = float(TWO_PI - C1 - C2)
ROUND = 1.5 * 2**23


class Order:

    def __init__(self, eng, sem):
        self.eng, self.sem, self.n, self.base = eng, sem, 0, 0

    def link(self, ins):
        ins.then_inc(self.sem, 1)
        self.n += 1
        self.eng.wait_ge(self.sem, self.base + self.n)

    def enter(self, i, steps):
        self.start, self.steps = self.base + self.n, steps
        self.base, self.n = self.start + i * steps, 0

    def leave(self, trips):
        assert self.n == self.steps, (self.n, self.steps)
        self.base, self.n = self.start + trips * self.steps, 0


def mm3(nc, out, a, b, start, stop):
    nc.tensor.matmul(out, a[0], b[0], start=start, stop=False)
    nc.tensor.matmul(out, a[0], b[1], start=False, stop=False)
    return nc.tensor.matmul(out, a[1], b[0], start=False, stop=stop)


def trunk(nc, x, positions, inv_freq, norm_g, mla_w_in, mla_g_cq, mla_w_uq, mla_g_ckv, mla_w_ukv,
          mla_g_q, mla_g_k, mla_w_out, nsa_w_in, nsa_g_q, nsa_g_k, nsa_pe_k, nsa_w1_k, nsa_w2_k,
          nsa_pe_v, nsa_w1_v, nsa_w2_v, nsa_w_out, out):
    with ExitStack() as whole:
        names = set()

        def sem(name):
            assert name not in names
            names.add(name)
            return whole.enter_context(nc.semaphore(name))

        def sb(ctx, name, shape, dt=F32):
            return ctx.enter_context(nc.sbuf_tensor(name, shape, dt))

        keep = lambda name, shape, dt=F32: sb(whole, name, shape, dt)
        whole.enter_context(nc.allow_non_contiguous_dma(reason="gains and positions are short"))
        bank = [whole.enter_context(nc.psum_tensor(f"bank{b}", [P, 512], F32)) for b in range(8)]

        x_sb = keep("x_sb", [P, NT, DM])
        ident = keep("ident", [P, P])
        identb = keep("identb", [P, P], BF16)
        causal = keep("causal", [P, P], BF16)
        cmask = keep("cmask", [P, NT, NC])
        zeros = keep("zeros", [P, NT * NC])
        minus_half = keep("minus_half", [P, 16])
        tcos = keep("tcos", [P, NT + 1, FREQS])
        tsin = keep("tsin", [P, NT + 1, FREQS])
        g_x = keep("g_x", [P, 2, DM // P])
        g_c = keep("g_c", [P, KQ + KKV])
        gq0 = keep("gq0", [P, QK])
        gk0 = keep("gk0", [P, QK])
        gq1 = keep("gq1", [P, DK])
        gk1 = keep("gk1", [P, 3, DK])

        w_raw = [keep(f"w_raw{s}", [P, KP, CW]) for s in range(2)]
        w_landed = [sem(f"w_landed{s}") for s in range(2)]
        w_hi_made, w_lo_made, w_used = sem("w_hi_made"), sem("w_lo_made"), sem("w_used")
        acc_done, acc_free = sem("acc_done"), sem("acc_free")
        piece_base, acc_base = [0], [0]

        def stream(ctx, loops, act_hi, act_lo, evacuate):
            at = piece_base[0]
            w_hi = [sb(ctx, f"w_hi{s}_{at}", [P, KP, CW], F32R) for s in range(2)]
            w_lo = [sb(ctx, f"w_lo{s}_{at}", [P, KP, CW], F32R) for s in range(2)]
            plan = []
            for w, col0, width, chunks, what in loops:
                kt = w.shape[0] // P
                plan.append((w, col0, width, chunks, what, kt // KP, piece_base[0], acc_base[0]))
                piece_base[0] += kt // KP * chunks
                acc_base[0] += NT * chunks
            assert piece_base[0] % 2 == 0

            def load(sp):
                for w, col0, width, chunks, what, ppc, p0, a0 in plan:
                    rows = w.rearrange("(k p) c -> p k c", p=P)

                    def chunk(c):
                        for j in range(ppc):
                            g = p0 + c * ppc + j
                            if not isinstance(g, int) or g >= 2:
                                sp.wait_ge(w_lo_made, g - 1)
                            sp.dma_start(w_raw[j % 2][:, :, 0:width],
                                         rows[:, j * KP:(j + 1) * KP, bass.ds(col0 + c * width, width)]
                                         ).then_inc(w_landed[j % 2], 16)
                    first = 1 if p0 == 0 else 0
                    if first:
                        chunk(0)
                    if chunks > first:
                        with sp.Fori(first, chunks) as c:
                            chunk(c)

            def split_hi(act, extra):
                for w, col0, width, chunks, what, ppc, p0, a0 in plan:
                    def chunk(c):
                        for j in range(ppc):
                            g = p0 + c * ppc + j
                            act.wait_ge(w_landed[j % 2], (p0 // 2 + c * (ppc // 2) + j // 2 + 1) * 16)
                            if not isinstance(g, int) or g >= 2:
                                act.wait_ge(w_used, g - 1)
                            nc.scalar.activation(w_hi[j % 2][:, :, 0:width], w_raw[j % 2][:, :, 0:width],
                                                 ACT.Copy).then_inc(w_hi_made, 1)
                            if j == 0:
                                extra(act, what, c, a0, width)
                    first = 1 if p0 == 0 else 0
                    if first:
                        chunk(0)
                    if chunks > first:
                        with act.Fori(first, chunks) as c:
                            chunk(c)

            def split_lo(pool):
                for w, col0, width, chunks, what, ppc, p0, a0 in plan:
                    with pool.Fori(0, chunks) as c:
                        for j in range(ppc):
                            pool.wait_ge(w_hi_made, p0 + c * ppc + j + 1)
                            nc.gpsimd.tensor_tensor(
                                w_lo[j % 2][:, :, 0:width], w_raw[j % 2][:, :, 0:width],
                                w_hi[j % 2][:, :, 0:width].bitcast(F32), ALU.subtract).then_inc(w_lo_made, 1)

            def products(pe):
                for w, col0, width, chunks, what, ppc, p0, a0 in plan:
                    def chunk(c):
                        for j in range(ppc):
                            pe.wait_ge(w_lo_made, p0 + c * ppc + j + 1)
                            for t in range(NT):
                                a = a0 + c * NT + t
                                if j == 0 and (not isinstance(a, int) or a >= NT):
                                    pe.wait_ge(acc_free, a - NT + 1)
                                for k in range(KP):
                                    kt = j * KP + k
                                    tok = slice(t * P, (t + 1) * P)
                                    last = mm3(nc, bank[t][:, 0:width],
                                               (act_hi[:, kt, tok], act_lo[:, kt, tok]),
                                               (w_hi[j % 2][:, k, 0:width], w_lo[j % 2][:, k, 0:width]),
                                               start=kt == 0, stop=kt == ppc * KP - 1)
                                if j == ppc - 1:
                                    last.then_inc(acc_done, 1)
                            nc.tensor.matmul(bank[4][:, 0:P], identb[:, :], identb[:, :], start=True,
                                             stop=True).then_inc(w_used, 1)
                    first = 1 if a0 == 0 else 0
                    if first:
                        chunk(0)
                    if chunks > first:
                        with pe.Fori(first, chunks) as c:
                            chunk(c)

            def evacuation(eng):
                for w, col0, width, chunks, what, ppc, p0, a0 in plan:
                    with eng.Fori(0, chunks) as c:
                        for t in range(NT):
                            eng.wait_ge(acc_done, a0 + c * NT + t + 1)
                            evacuate(what, t, c * width, width, bank[t][:, 0:width]).then_inc(acc_free, 1)

            return load, split_hi, split_lo, products, evacuation

        with ExitStack() as ctx:
            pos_i = sb(ctx, "pos_i", [P, NT + 1], I32)
            pos_f = sb(ctx, "pos_f", [P, NT + 1])
            freq = sb(ctx, "freq", [P, FREQS])
            ang = sb(ctx, "ang", [P, (NT + 1) * FREQS])
            turns = sb(ctx, "turns", [P, (NT + 1) * FREQS])
            red = sb(ctx, "red", [P, (NT + 1) * FREQS])
            quarter = sb(ctx, "quarter", [P, (NT + 1) * FREQS])
            loaded, pos_clear = sem("loaded"), sem("pos_clear")
            made, table_ready, dve_order = sem("made"), sem("table_ready"), sem("dve_order0")
            pool_order, tables_done = sem("pool_order0"), sem("tables_done")
            block = ctx.enter_context(nc.Block())

            @block.sync
            def _(sp):
                sp.wait_ge(pos_clear, 1)
                row = lambda ap: ap.rearrange("(a d) -> a d", a=1)
                pieces = [
                    (pos_i[:, 0:NT], positions[0].rearrange("(t p) -> p t", p=P)),
                    (pos_i[0:NCMP, NT:NT + 1],
                     positions[0, LCMP - 1:SEQ].rearrange("(n s) -> n s", n=1).rearrange("n s -> s n")[0:SEQ - LCMP + 1:STRIDE, :]),
                    (freq[:, :], row(inv_freq).to_broadcast([P, FREQS])),
                    (g_x[:, :, :], norm_g.rearrange("l (k p) -> p l k", p=P)),
                    (g_c[:, 0:KQ], mla_g_cq[0].rearrange("(k p) -> p k", p=P)),
                    (g_c[:, KQ:KQ + KKV], mla_g_ckv[0].rearrange("(k p) -> p k", p=P)),
                    (gq0[:, :], row(mla_g_q[0]).to_broadcast([P, QK])),
                    (gk0[:, :], row(mla_g_k[0]).to_broadcast([P, QK])),
                    (gq1[:, :], row(nsa_g_q[0]).to_broadcast([P, DK])),
                ] + [(gk1[:, b, :], row(nsa_g_k[0, b]).to_broadcast([P, DK])) for b in range(3)]
                for dst, src in pieces:
                    sp.dma_start(dst, src).then_inc(loaded, 16)
                for t in range(NT):
                    sp.dma_start(x_sb[:, t, :], x[0, t * P:(t + 1) * P, :]).then_inc(loaded, 16)
                sp.wait_ge(loaded, 16 * (len(pieces) + NT))

            @block.gpsimd
            def _(pool):
                o = Order(pool, pool_order)
                nc.gpsimd.memset(pos_i[:, :], 0).then_inc(pos_clear, 1)
                nc.gpsimd.memset(minus_half[:, :], -0.5)
                o.link(nc.gpsimd.memset(zeros[:, :], 0.0))
                z = zeros[:, 0:P]
                o.link(nc.gpsimd.affine_select(out=ident[:, :], in_=z, compare_op=ALU.not_equal, fill=1.0,
                                               base=0, pattern=[[-1, P]], channel_multiplier=1))
                nc.gpsimd.affine_select(out=identb[:, :], in_=z, compare_op=ALU.not_equal, fill=1.0,
                                        base=0, pattern=[[-1, P]], channel_multiplier=1)
                nc.gpsimd.affine_select(out=causal[:, :], in_=z, compare_op=ALU.is_ge, fill=NEG,
                                        base=0, pattern=[[-1, P]], channel_multiplier=1)
                nc.gpsimd.affine_select(out=cmask[:, :, :], in_=z.rearrange("p (i n) -> p i n", n=NC),
                                        compare_op=ALU.is_ge, fill=NEG, base=-(LCMP - 1),
                                        pattern=[[P, NT], [-STRIDE, NC]], channel_multiplier=1
                                        ).then_inc(made, 1)

            @block.vector
            def _(dve):
                o = Order(dve, dve_order)
                dve.wait_ge(loaded, 16 * (12 + NT))
                o.link(nc.vector.tensor_copy(pos_f[:, :], pos_i[:, :]))
                for t in range(NT + 1):
                    last = nc.vector.tensor_scalar(ang[:, t * FREQS:(t + 1) * FREQS], freq[:, :],
                                                   pos_f[:, t:t + 1], None, ALU.mult)
                o.link(last)
                o.link(nc.vector.tensor_scalar(turns[:, :], ang[:, :], 1 / TWO_PI, ROUND, ALU.mult, ALU.add))
                o.link(nc.vector.tensor_scalar(turns[:, :], turns[:, :], -ROUND, None, ALU.add))
                o.link(nc.vector.scalar_tensor_tensor(ang[:, :], turns[:, :], -C1, ang[:, :], ALU.mult, ALU.add))
                o.link(nc.vector.scalar_tensor_tensor(ang[:, :], turns[:, :], -C2, ang[:, :], ALU.mult, ALU.add))
                o.link(nc.vector.scalar_tensor_tensor(ang[:, :], turns[:, :], -C3, ang[:, :], ALU.mult, ALU.add))
                pi = float(np.nextafter(np.float32(np.pi), np.float32(0)))
                o.link(nc.vector.tensor_scalar(red[:, :], ang[:, :], pi, -pi, ALU.min, ALU.max))
                o.link(nc.vector.scalar_tensor_tensor(quarter[:, :], red[:, :], -1.0, red[:, :], ALU.mult, ALU.max))
                nc.vector.tensor_scalar(quarter[:, :], quarter[:, :], -1.0, float(np.pi / 2), ALU.mult,
                                        ALU.add).then_inc(table_ready, 1)
                nc.vector.tensor_scalar(gq0[:, :], gq0[:, :], float(QK) ** -0.5, None, ALU.mult)
                nc.vector.tensor_scalar(gq1[:, :], gq1[:, :], float(DK) ** -0.5, None, ALU.mult)

            @block.scalar
            def _(act):
                act.wait_ge(table_ready, 1)
                nc.scalar.activation(tsin[:, :, :].rearrange("p t f -> p (t f)"), red[:, :], ACT.Sin)
                nc.scalar.activation(tcos[:, :, :].rearrange("p t f -> p (t f)"), quarter[:, :],
                                     ACT.Sin).then_inc(tables_done, 1)
                act.wait_ge(tables_done, 1)

        def transpose_block(ctx, tag, src, kt, gain, dst_hi, dst_lo, norm=None, before=None):
            norm = norm or []
            normed = sb(ctx, f"normed_{tag}", [P, NT, kt * P]) if norm else src
            junk = sb(ctx, f"junk_{tag}", [P, DM if norm else 2])
            ms = sb(ctx, f"ms_{tag}", [P, NT, 2])
            squared, factor, scaled = sem(f"squared_{tag}"), sem(f"factor_{tag}"), sem(f"scaled_{tag}")
            turned, hi_made, lo_made = sem(f"turned_{tag}"), sem(f"hi_{tag}"), sem(f"lo_{tag}")
            pool_o, act_o = sem(f"pool_o_{tag}"), sem(f"act_o_{tag}")
            block = ctx.enter_context(nc.Block())

            @block.scalar
            def _(act):
                o = Order(act, act_o)
                for t in range(NT if norm else 0):
                    for s, (c0, width) in enumerate(norm):
                        o.link(nc.scalar.activation(junk[:, 0:width], src[:, t, c0:c0 + width], ACT.Square,
                                                    scale=float(width) ** -0.5, accum_out=ms[:, t, s:s + 1]))
                for k in range(kt):
                    act.wait_ge(turned, k + 1)
                    nc.scalar.activation(dst_hi[:, k, :], bank[k % 8][:, :], ACT.Copy,
                                         scale=gain[:, k:k + 1] if gain is not None else 1.0
                                         ).then_inc(hi_made, 1)

            @block.gpsimd
            def _(pool):
                o = Order(pool, pool_o)
                for t in range(NT if norm else 0):
                    n = len(norm)
                    pool.wait_ge(act_o, n * (t + 1))
                    o.link(nc.gpsimd.tensor_scalar(ms[:, t, 0:n], ms[:, t, 0:n], EPS, None, ALU.add))
                    nc.gpsimd.tensor_tensor(ms[:, t, 0:n], ms[:, t, 0:n], minus_half[:, 0:n],
                                            ALU.pow).then_inc(factor, 1)
                if before:
                    before(pool)

            @block.vector
            def _(dve):
                for t in range(NT if norm else 0):
                    dve.wait_ge(factor, t + 1)
                    for s, (c0, width) in enumerate(norm):
                        last = nc.vector.tensor_scalar(normed[:, t, c0:c0 + width], src[:, t, c0:c0 + width],
                                                       ms[:, t, s:s + 1], None, ALU.mult)
                    last.then_inc(scaled, 1)
                for k in range(kt):
                    dve.wait_ge(hi_made, k + 1)
                    g = gain[:, k:k + 1] if gain is not None else 1.0
                    nc.vector.scalar_tensor_tensor(dst_lo[:, k, :], bank[k % 8][:, :], g,
                                                   dst_hi[:, k, :].bitcast(F32), ALU.mult,
                                                   ALU.subtract).then_inc(lo_made, 1)

            @block.tensor
            def _(pe):
                if norm:
                    pe.wait_ge(scaled, NT)
                for k in range(kt):
                    if k >= 8:
                        pe.wait_ge(lo_made, k - 7)
                    for t in range(NT):
                        last = nc.tensor.transpose(bank[k % 8][:, t * P:(t + 1) * P],
                                                   normed[:, t, k * P:(k + 1) * P], ident[:, :])
                    last.then_inc(turned, 1)

        def run_stream(ctx, loops, act_hi, act_lo, evacuate, evac_engine):
            load, split_hi, split_lo, products, evacuation = stream(ctx, loops, act_hi, act_lo, evacuate)
            block = ctx.enter_context(nc.Block())

            @block.sync
            def _(sp):
                load(sp)

            @block.scalar
            def _(act):
                split_hi(act, lambda *a: None)

            @block.gpsimd
            def _(pool):
                split_lo(pool)

            @block.tensor
            def _(pe):
                products(pe)

            @block.vector
            def _(dve):
                evacuation(dve)

        with ExitStack() as layer:
            z_sb = sb(layer, "z_sb", [P, NT, ZZ])
            silu_done = sem("silu_done0")
            with ExitStack() as proj:
                c_hi = sb(layer, "c_hi", [P, KQ + KKV, SEQ], F32R)
                c_lo = sb(layer, "c_lo", [P, KQ + KKV, SEQ], F32R)
                kpe_sb = sb(layer, "kpe_sb", [P, NT, ROPE])
                kpe_ms = sb(layer, "kpe_ms", [P, NT, 2])
                c_sb = sb(proj, "c_sb", [P, NT, CC])
                with ExitStack() as ph:
                    h_hi = sb(ph, "h_hi", [P, DM // P, SEQ], F32R)
                    h_lo = sb(ph, "h_lo", [P, DM // P, SEQ], F32R)
                    with ExitStack() as ctx:
                        transpose_block(ctx, "x0", x_sb, DM // P, g_x[:, 0, :], h_hi, h_lo, norm=[(0, DM)])
                    with ExitStack() as ctx:
                        def evacuate(what, t, c0, width, acc):
                            dst = {"c": c_sb, "z": z_sb}[what]
                            return nc.vector.tensor_copy(dst[:, t, bass.ds(c0, width)], acc)
                        run_stream(ctx, [(mla_w_in[0], 0, CC // 2, 2, "c"), (mla_w_in[0], CC, CW, ZZ // CW, "z")],
                                   h_hi, h_lo, evacuate, "dve")

                with ExitStack() as ctx:
                    rot = sb(ctx, "rot0", [P, 4, NT, HALF0])
                    junk = sb(ctx, "junk_pe", [P, ROPE])
                    dve_o, kpe_sq = sem("dve_o_pe"), sem("kpe_sq")
                    block = ctx.enter_context(nc.Block())

                    @block.scalar
                    def _(act):
                        for t in range(NT):
                            nc.scalar.activation(junk[:, :], c_sb[:, t, CQ + CKV:CC], ACT.Square,
                                                 scale=float(QK) ** -0.5, accum_out=kpe_ms[:, t, 1:2]
                                                 ).then_inc(kpe_sq, 1)
                            act.wait_ge(kpe_sq, t + 1)
                        for t in range(NT):
                            nc.scalar.activation(z_sb[:, t, :], z_sb[:, t, :], ACT.Silu).then_inc(silu_done, 1)

                    @block.vector
                    def _(dve):
                        o = Order(dve, dve_o)
                        o.link(nc.vector.memset(kpe_ms[:, :, 0:1], EPS))
                        pe_in = c_sb[:, :, CQ + CKV:CC]
                        dve.wait_ge(kpe_sq, NT)
                        for t in range(NT):
                            last = nc.vector.tensor_tensor(pe_in[:, t, :], pe_in[:, t, :], gk0[:, 0:ROPE], ALU.mult)
                        o.link(last)
                        x1, x2 = pe_in[:, :, 0:HALF0], pe_in[:, :, HALF0:ROPE]
                        cos, sin = tcos[:, 0:NT, 0:HALF0], tsin[:, 0:NT, 0:HALF0]
                        nc.vector.tensor_tensor(rot[:, 0], x1, cos, ALU.mult)
                        nc.vector.tensor_tensor(rot[:, 1], x2, sin, ALU.mult)
                        nc.vector.tensor_tensor(rot[:, 2], x2, cos, ALU.mult)
                        o.link(nc.vector.tensor_tensor(rot[:, 3], x1, sin, ALU.mult))
                        nc.vector.tensor_tensor(kpe_sb[:, :, 0:HALF0], rot[:, 0], rot[:, 1], ALU.subtract)
                        nc.vector.tensor_tensor(kpe_sb[:, :, HALF0:ROPE], rot[:, 2], rot[:, 3], ALU.add)
                        nc.vector.tensor_scalar(kpe_ms[:, :, 1:2], kpe_ms[:, :, 1:2], EPS, None, ALU.add)
                with ExitStack() as ctx:
                    transpose_block(ctx, "c", c_sb, KQ + KKV, g_c, c_hi, c_lo, norm=[(0, CQ), (CQ, CKV)])

            with ExitStack() as ctx:
                v_all = sb(ctx, "v_all", [P, NT, ZZ])
                wh_raw = sb(ctx, "wh_raw", [P, KQ * WQ + KKV * WKV])
                wh_hi = [sb(ctx, f"wh_hi{a}", [P, KQ * WQ + KKV * WKV], F32R) for a in range(2)]
                wh_lo = [sb(ctx, f"wh_lo{a}", [P, KQ * WQ + KKV * WKV], F32R) for a in range(2)]
                qn = sb(ctx, "qn", [P, NT, QK])
                kn = sb(ctx, "kn", [P, NT, QK])
                rot = sb(ctx, "rotq", [P, 4, 2, HALF0])
                sq_junk = sb(ctx, "sq_junk", [P, QK + NOPE])
                ms = sb(ctx, "ms_qk", [P, NT, 2])
                qkT_hi = [sb(ctx, f"qkT_hi{a}", [HQK, 4, SEQ], F32R) for a in range(2)]
                qkT_lo = [sb(ctx, f"qkT_lo{a}", [HQK, 4, SEQ], F32R) for a in range(2)]
                prob = sb(ctx, "prob", [P, 2, SEQ])
                probT = sb(ctx, "probT", [P, 2, SEQ])
                negmax = sb(ctx, "negmax", [P, 2, NT])
                rowsum = sb(ctx, "rowsum", [P, 2, NT])
                rinv = sb(ctx, "rinv", [P, NT])
                score_bank, pt_bank, o_bank = [bank[0], bank[1]], bank[2], bank[3]
                p_bank, x_bank = [bank[4], bank[5]], [bank[6], bank[7]]
                wh_landed, wh_hi_made, wh_ready = sem("wh_landed"), sem("wh_hi_made"), sem("wh_ready")
                p_done, squares, factors = sem("p_done"), sem("squares"), sem("factors")
                qk_scaled, qk_rotated, p_free = sem("qk_scaled"), sem("qk_rotated"), sem("p_free")
                x_free, v_out = sem("x_free"), sem("v_out")
                x_done, x_hi = sem("x_done"), sem("x_hi")
                s_done, max_done, exp_done = sem("s_done"), sem("max_done"), sem("exp_done")
                t_done, pt_ready, pv_done, o_free = sem("t_done"), sem("pt_ready"), sem("pv_done"), sem("o_free")
                act_sem, dve_sem, pool_sem = sem("act_o_mla"), sem("dve_o_mla"), sem("pool_o_mla")
                wq_of = lambda w, k: w[:, k * WQ:(k + 1) * WQ]
                wkv_of = lambda w, k: w[:, KQ * WQ + k * WKV:KQ * WQ + (k + 1) * WKV]
                block = ctx.enter_context(nc.Block())

                def positive(v):
                    return not isinstance(v, int) or v > 0

                @block.sync
                def _(sp):
                    def load(n):
                        if positive(n):
                            sp.wait_ge(wh_ready, n)
                        sp.dma_start(wh_raw[:, 0:KQ * WQ].rearrange("p (k c) -> p k c", k=KQ),
                                     mla_w_uq[0].rearrange("(k p) c -> p k c", p=P)[:, :, bass.ds(n * WQ, WQ)]
                                     ).then_inc(wh_landed, 16)
                        sp.dma_start(wh_raw[:, KQ * WQ:].rearrange("p (k c) -> p k c", k=KKV),
                                     mla_w_ukv[0].rearrange("(k p) c -> p k c", p=P)[:, :, bass.ds(n * WKV, WKV)]
                                     ).then_inc(wh_landed, 16)
                    load(0)
                    with sp.Fori(1, H) as n:
                        load(n)

                def heads(eng, step):
                    with eng.Fori(0, H - 4, 2) as h:
                        step(h, 0, True, True)
                        step(h + 1, 1, True, True)
                    for h in range(H - 4, H):
                        step(h, h % 2, h + 1 < H, h + 2 < H)

                @block.tensor
                def _(pe):
                    def project(n, a, t):
                        if t == 0:
                            pe.wait_ge(wh_ready, n + 1)
                        if positive(4 * n + t - 1):
                            pe.wait_ge(p_free, 4 * n + t - 1)
                        tok = slice(t * P, (t + 1) * P)
                        for k in range(KQ):
                            mm3(nc, p_bank[t % 2][:, 0:WQ], (c_hi[:, k, tok], c_lo[:, k, tok]),
                                (wq_of(wh_hi[a], k), wq_of(wh_lo[a], k)), start=k == 0, stop=k == KQ - 1)
                        for k in range(KKV):
                            last = mm3(nc, p_bank[t % 2][:, WQ:WQ + WKV],
                                       (c_hi[:, KQ + k, tok], c_lo[:, KQ + k, tok]),
                                       (wkv_of(wh_hi[a], k), wkv_of(wh_lo[a], k)), start=k == 0, stop=k == KKV - 1)
                        last.then_inc(p_done, 1)

                    def turn(n, t):
                        if t % 2 == 0:
                            pe.wait_ge(qk_rotated, 2 * n + t // 2 + 1)
                        if positive(4 * n + t - 1):
                            pe.wait_ge(x_free, 4 * n + t - 1)
                        for part in range(4):
                            src = (qn, kn)[part // 2][:, t, (part % 2) * HQK:(part % 2 + 1) * HQK]
                            last = nc.tensor.transpose(x_bank[t % 2][0:HQK, part * P:(part + 1) * P], src, ident[:, :])
                        last.then_inc(x_done, 1)

                    def scores(h, a, i):
                        if i == 0:
                            pe.wait_ge(x_free, 4 * h + 4)
                        tok, keys = slice(i * P, (i + 1) * P), (i + 1) * P
                        dst = score_bank[i % 2]
                        for part in range(2):
                            mm3(nc, dst[:, 0:keys], (qkT_hi[a][:, part, tok], qkT_lo[a][:, part, tok]),
                                (qkT_hi[a][:, 2 + part, 0:keys], qkT_lo[a][:, 2 + part, 0:keys]),
                                start=part == 0, stop=False)
                        nc.tensor.matmul(dst[:, tok], identb[:, :], causal[:, :], start=False,
                                         stop=True).then_inc(s_done, 1)

                    def turn_probs(h, i):
                        pe.wait_ge(exp_done, 4 * h + i + 1)
                        if i == NT - 1:
                            pe.wait_ge(pt_ready, 4 * h + i)
                        for j in range(i + 1):
                            last = nc.tensor.transpose(pt_bank[:, j * P:(j + 1) * P],
                                                       prob[:, i % 2, j * P:(j + 1) * P], ident[:, :])
                        last.then_inc(t_done, 1)

                    def values(h, i):
                        pe.wait_ge(pt_ready, 4 * h + i + 1)
                        pe.wait_ge(o_free, 4 * h + i + 1)
                        for j in range(i + 1):
                            last = nc.tensor.matmul(o_bank[:, 0:DV0], probT[:, i % 2, j * P:(j + 1) * P],
                                                    v_all[:, j, bass.ds(h * DV0, DV0)],
                                                    start=j == 0, stop=j == i)
                        last.then_inc(pv_done, 1)

                    def step(h, a, x, p):
                        for i in range(NT):
                            scores(h, a, i)
                            if x:
                                turn(h + 1, i)
                            if i >= 2:
                                values(h, i - 2)
                            if i >= 1:
                                turn_probs(h, i - 1)
                            if p:
                                project(h + 2, a, i)
                        turn_probs(h, 3)
                        values(h, 2)
                        values(h, 3)

                    for t in range(NT):
                        project(0, 0, t)
                    for t in range(NT):
                        turn(0, t)
                        project(1, 1, t)
                    heads(pe, step)

                @block.scalar
                def _(act):
                    def split_weights(n, a):
                        act.wait_ge(wh_landed, 32 * n + 32)
                        if positive(n - 1):
                            act.wait_ge(p_done, 4 * n - 4)
                        nc.scalar.activation(wh_hi[a][:, :], wh_raw[:, :], ACT.Copy).then_inc(wh_hi_made, 1)

                    def stats(n, t):
                        act.wait_ge(p_done, 4 * n + t + 1)
                        if t or positive(n):
                            act.wait_ge(squares, 4 * n + t)
                        src = p_bank[t % 2]
                        nc.scalar.activation(sq_junk[:, 0:QK], src[:, 0:QK], ACT.Square, scale=float(QK) ** -0.5,
                                             accum_out=ms[:, t, 0:1])
                        nc.scalar.activation(sq_junk[:, QK:], src[:, QK:QK + NOPE], ACT.Square,
                                             scale=float(QK) ** -0.5, accum_out=ms[:, t, 1:2]).then_inc(squares, 1)
                        nc.scalar.activation(v_all[:, t, bass.ds(n * DV0, DV0)], src[:, QK + NOPE:QK + NOPE + DV0],
                                             ACT.Copy).then_inc(v_out, 1)

                    def high(n, a, t):
                        act.wait_ge(x_done, 4 * n + t + 1)
                        nc.scalar.activation(qkT_hi[a][:, :, t * P:(t + 1) * P],
                                             x_bank[t % 2][0:HQK, :].rearrange("p (a t) -> p a t", a=4),
                                             ACT.Copy).then_inc(x_hi, 1)

                    def exponential(h, a, i):
                        act.wait_ge(max_done, 4 * h + i + 1)
                        keys = (i + 1) * P
                        nc.scalar.activation(prob[:, i % 2, 0:keys], score_bank[i % 2][:, 0:keys], ACT.Exp,
                                             bias=negmax[:, a, i:i + 1], accum_out=rowsum[:, a, i:i + 1]
                                             ).then_inc(exp_done, 1)

                    def probs_out(h, i):
                        act.wait_ge(t_done, 4 * h + i + 1)
                        nc.scalar.activation(probT[:, i % 2, 0:(i + 1) * P], pt_bank[:, 0:(i + 1) * P],
                                             ACT.Copy).then_inc(pt_ready, 1)

                    def step(h, a, x, p):
                        for i in range(NT):
                            exponential(h, a, i)
                            if x:
                                high(h + 1, 1 - a, i)
                            if i == 0 and (not isinstance(h, int) or h + 3 < H):
                                split_weights(h + 3, 1 - a)
                            if i >= 2:
                                probs_out(h, i - 1)
                            if p:
                                stats(h + 2, i)

                    split_weights(0, 0)
                    split_weights(1, 1)
                    for t in range(NT):
                        stats(0, t)
                    split_weights(2, 0)
                    for t in range(NT):
                        high(0, 0, t)
                        stats(1, t)
                    heads(act, step)

                @block.gpsimd
                def _(pool):
                    o = Order(pool, pool_sem)

                    def factor(n, t):
                        pool.wait_ge(squares, 4 * n + t + 1)
                        o.link(nc.gpsimd.tensor_tensor(ms[:, t, :], ms[:, t, :], kpe_ms[:, t, :], ALU.add))
                        nc.gpsimd.tensor_tensor(ms[:, t, :], ms[:, t, :], minus_half[:, 0:2],
                                                ALU.pow).then_inc(factors, 1)
                        pool.wait_ge(factors, 4 * n + t + 1)
                        nc.gpsimd.tensor_tensor(kn[:, t, 0:ROPE], kpe_sb[:, t, :],
                                                ms[:, t, 1:2].to_broadcast([P, ROPE]), ALU.mult)

                    def rotate(n, a):
                        pool.wait_ge(qk_scaled, 4 * n + 2 * a + 2)
                        tt = slice(2 * a, 2 * a + 2)
                        x1, x2 = qn[:, tt, 0:HALF0], qn[:, tt, HALF0:ROPE]
                        cos, sin = tcos[:, tt, 0:HALF0], tsin[:, tt, 0:HALF0]
                        nc.gpsimd.tensor_tensor(rot[:, 0], x1, cos, ALU.mult)
                        nc.gpsimd.tensor_tensor(rot[:, 1], x2, sin, ALU.mult)
                        nc.gpsimd.tensor_tensor(rot[:, 2], x2, cos, ALU.mult)
                        o.link(nc.gpsimd.tensor_tensor(rot[:, 3], x1, sin, ALU.mult))
                        nc.gpsimd.tensor_tensor(x1, rot[:, 0], rot[:, 1], ALU.subtract)
                        nc.gpsimd.tensor_tensor(x2, rot[:, 2], rot[:, 3], ALU.add).then_inc(qk_rotated, 1)
                        pool.wait_ge(qk_rotated, 2 * n + a + 1)

                    with pool.Fori(0, H) as n:
                        o.enter(n, 6)
                        for a in range(2):
                            factor(n, 2 * a)
                            factor(n, 2 * a + 1)
                            rotate(n, a)
                        o.leave(H)

                @block.vector
                def _(dve):
                    o = Order(dve, dve_sem)

                    def split_weights(n, a):
                        dve.wait_ge(wh_hi_made, n + 1)
                        nc.vector.tensor_tensor(wh_lo[a][:, :], wh_raw[:, :], wh_hi[a][:, :].bitcast(F32),
                                                ALU.subtract).then_inc(wh_ready, 1)

                    def scale(n, t):
                        dve.wait_ge(v_out, 4 * n + t + 1)
                        dve.wait_ge(factors, 4 * n + t + 1)
                        src = p_bank[t % 2]
                        nc.vector.scalar_tensor_tensor(qn[:, t, :], src[:, 0:QK], ms[:, t, 0:1], gq0[:, :],
                                                       ALU.mult, ALU.mult).then_inc(qk_scaled, 1)
                        nc.vector.scalar_tensor_tensor(kn[:, t, ROPE:QK], src[:, QK:QK + NOPE],
                                                       ms[:, t, 1:2], gk0[:, ROPE:QK], ALU.mult,
                                                       ALU.mult).then_inc(p_free, 1)

                    def low(n, a, t):
                        dve.wait_ge(x_hi, 4 * n + t + 1)
                        at = slice(t * P, (t + 1) * P)
                        nc.vector.tensor_tensor(qkT_lo[a][:, :, at],
                                                x_bank[t % 2][0:HQK, :].rearrange("p (a t) -> p a t", a=4),
                                                qkT_hi[a][:, :, at].bitcast(F32), ALU.subtract).then_inc(x_free, 1)

                    def maximum(h, a, i):
                        dve.wait_ge(s_done, 4 * h + i + 1)
                        nc.vector.tensor_reduce(negmax[:, a, i:i + 1], score_bank[i % 2][:, 0:(i + 1) * P], AX.X,
                                                ALU.max, negate=True).then_inc(max_done, 1)

                    def probs_out(h, i):
                        dve.wait_ge(t_done, 4 * h + i + 1)
                        nc.vector.tensor_copy(probT[:, i % 2, 0:(i + 1) * P],
                                              pt_bank[:, 0:(i + 1) * P]).then_inc(pt_ready, 1)

                    def gate(h, a, i):
                        o.link(nc.vector.reciprocal(rinv[:, i:i + 1], rowsum[:, a, i:i + 1]))
                        dve.wait_ge(pv_done, 4 * h + i + 1)
                        at = z_sb[:, i, bass.ds(h * DV0, DV0)]
                        nc.vector.scalar_tensor_tensor(at, o_bank[:, 0:DV0], rinv[:, i:i + 1], at, ALU.mult,
                                                       ALU.mult).then_inc(o_free, 1)

                    def step(h, a, x, p):
                        for i in range(NT):
                            maximum(h, a, i)
                            if x:
                                low(h + 1, 1 - a, i)
                            if i == 0 and (not isinstance(h, int) or h + 3 < H):
                                split_weights(h + 3, 1 - a)
                            if i == 1:
                                probs_out(h, 0)
                            if i >= 2:
                                gate(h, a, i - 2)
                            if p and i >= 1:
                                scale(h + 2, i - 1)
                        probs_out(h, 3)
                        gate(h, a, 2)
                        if p:
                            scale(h + 2, 3)
                        gate(h, a, 3)

                    nc.vector.memset(rinv[:, :], 1.0).then_inc(o_free, 1)
                    dve.wait_ge(o_free, 1)
                    split_weights(0, 0)
                    split_weights(1, 1)
                    for t in range(NT):
                        scale(0, t)
                    split_weights(2, 0)
                    for t in range(NT):
                        low(0, 0, t)
                        scale(1, t)
                    with dve.Fori(0, H - 4, 2) as h:
                        o.base, o.n = h * NT, 0
                        step(h, 0, True, True)
                        step(h + 1, 1, True, True)
                    o.base, o.n = (H - 4) * NT, 0
                    for h in range(H - 4, H):
                        step(h, h % 2, h + 1 < H, h + 2 < H)

            with ExitStack() as ph:
                o_hi = sb(ph, "o_hi", [P, ZZ // P, SEQ], F32R)
                o_lo = sb(ph, "o_lo", [P, ZZ // P, SEQ], F32R)
                with ExitStack() as ctx:
                    transpose_block(ctx, "o0", z_sb, ZZ // P, None, o_hi, o_lo)
                with ExitStack() as ctx:
                    def evacuate(what, t, c0, width, acc):
                        at = x_sb[:, t, bass.ds(c0, width)]
                        return nc.vector.tensor_tensor(at, acc, at, ALU.add)
                    run_stream(ctx, [(mla_w_out[0], 0, CW, DM // CW, "x")], o_hi, o_lo, evacuate, "dve")

        with ExitStack() as layer:
            z_sb = sb(layer, "z1_sb", [P, NT, Z1])
            mixer = ExitStack()
            qs = sb(mixer, "qs", [P, NT, QW])
            kv = sb(mixer, "kv", [P, NT, KVW])
            gates = sb(mixer, "gates", [P, NT, GW])
            kcT_hi = sb(mixer, "kcT_hi", [DK, G, NC], F32R)
            kcT_lo = sb(mixer, "kcT_lo", [DK, G, NC], F32R)
            vcmp = sb(mixer, "vcmp", [NC, G, DV])
            with ExitStack() as ph:
                h_hi = sb(ph, "h1_hi", [P, DM // P, SEQ], F32R)
                h_lo = sb(ph, "h1_lo", [P, DM // P, SEQ], F32R)
                with ExitStack() as ctx:
                    transpose_block(ctx, "x1", x_sb, DM // P, g_x[:, 1, :], h_hi, h_lo, norm=[(0, DM)])
                with ExitStack() as ctx:
                    def evacuate(what, t, c0, width, acc):
                        dst = {"q": qs, "kv": kv, "g": gates}[what]
                        return nc.vector.tensor_copy(dst[:, t, bass.ds(c0, width)], acc)
                    w = nsa_w_in[0]
                    run_stream(ctx, [(w, 0, CW, QW // CW, "q"), (w, QW, G * DK, KVW // (G * DK), "kv"),
                                     (w, QW + KVW, GW, 1, "g")],
                               h_hi, h_lo, evacuate, "dve")

                with ExitStack() as ctx:
                    w_hi = [sb(ctx, f"w_hi{s}_z", [P, KP, CW], F32R) for s in range(2)]
                    w_lo = [sb(ctx, f"w_lo{s}_z", [P, KP, CW], F32R) for s in range(2)]
                    sq = [sb(ctx, f"sq1_{s}", [P, G * DK]) for s in range(2)]
                    rot = sb(ctx, "rot1", [P, 4, G, HALF1])
                    ct = sb(ctx, "ct", [DK, G, SEQ])
                    w1 = sb(ctx, "w1", [DK, LCMP, DK])
                    w1v = w1[:, :, :].rearrange("d l e -> d (l e)")[0:DV, 0:LCMP * DV].rearrange("d (l e) -> d l e", e=DV)
                    w2k, w2v = sb(ctx, "w2k", [DK, DK]), sb(ctx, "w2v", [DV, DV])
                    pek, pev = sb(ctx, "pek", [LCMP, DK]), sb(ctx, "pev", [LCMP, DV])
                    pekT, pevT = sb(ctx, "pekT", [DK, LCMP]), sb(ctx, "pevT", [DV, LCMP])
                    biask, biasv = sb(ctx, "biask", [DK, 1]), sb(ctx, "biasv", [DV, 1])
                    hidk, hidv = sb(ctx, "hidk", [DK, G, NC]), sb(ctx, "hidv", [DV, G, NC])
                    kcmp = sb(ctx, "kcmp", [NC, G, DK])
                    item = []
                    for t in range(NT):
                        for b, c0 in ((1, KS), (2, KW)):
                            item.append((kv[:, t, c0:c0 + G * DK], gk1[:, b, :], t, P))
                    for t in range(NT):
                        for c0 in range(0, QW, G * DK):
                            item.append((qs[:, t, c0:c0 + G * DK], gq1[:, :], t, P))
                    KCMP = 16
                    item.insert(KCMP, (kcmp[:, :, :].rearrange("p g d -> p (g d)"), gk1[:, 0, :], NT, NC))
                    mean = sb(ctx, "mean1", [P, len(item), G])
                    small_in, w1_in, squared, averaged, factor1 = (sem(n) for n in (
                        "small_in", "w1_in", "squared1", "averaged1", "factor1"))
                    dve_s, pool_s, normed1, turned1, copied1 = (sem(n) for n in (
                        "dve_o1", "pool_o1", "normed1", "turned1", "copied1"))
                    hidden, hid_clear, kc_hi, gate_act, cmp_out = (sem(n) for n in (
                        "hidden", "hid_clear", "kc_hi", "gate_act", "cmp_out"))
                    p0, a0 = piece_base[0], acc_base[0]
                    CHUNKS = Z1 // CW
                    piece_base[0] += 2 * CHUNKS
                    acc_base[0] += NT * CHUNKS
                    wz = nsa_w_in[0].rearrange("(k p) c -> p k c", p=P)
                    block = ctx.enter_context(nc.Block())

                    T_KC, T_PE, T_HIDK, T_VC, T_HIDV, T_CMP, T_KCT = 4, 5, 6, 10, 11, 12, 13
                    C_KC, C_PE, C_BIASK, C_VC, C_BIASV = 4, 5, 6, 10, 11

                    @block.sync
                    def _(sp):
                        def load(g):
                            sp.wait_ge(w_lo_made, p0 + g - 1)
                            c0 = QW + KVW + GW + g // 2 * CW
                            sp.dma_start(w_raw[g % 2][:, :, :], wz[:, g % 2 * KP:(g % 2 + 1) * KP, c0:c0 + CW]
                                         ).then_inc(w_landed[g % 2], 16)
                        load(0)
                        load(1)
                        sp.dma_start(w1[:, :, :], nsa_w1_k[0].rearrange("(l d) e -> d l e", d=DK)).then_inc(w1_in, 16)
                        for dst, src in ((w2k[:, :], nsa_w2_k[0]), (w2v[:, :], nsa_w2_v[0]),
                                         (pek[:, :], nsa_pe_k[0]), (pev[:, :], nsa_pe_v[0])):
                            sp.dma_start(dst, src).then_inc(small_in, 16)
                        load(2)
                        load(3)
                        sp.wait_ge(turned1, T_HIDK)
                        sp.dma_start(w1v, nsa_w1_v[0].rearrange("(l d) e -> d l e", d=DV)).then_inc(w1_in, 16)

                    @block.tensor
                    def _(pe):
                        def turn_c(c0, width, g, b):
                            for t in range(NT):
                                last = nc.tensor.transpose(bank[b][0:width, t * P:(t + 1) * P],
                                                           kv[:, t, c0 + g * width:c0 + (g + 1) * width], ident[:, :])
                            last.then_inc(turned1, 1)

                        def turn_kc():
                            for g in range(G):
                                turn_c(KC, DK, g, 4 + g)

                        def turn_pe():
                            pe.wait_ge(small_in, 64)
                            pe.wait_ge(copied1, 1)
                            nc.tensor.transpose(bank[4][0:DK, 0:LCMP], pek[:, :], ident[0:LCMP, 0:LCMP])
                            nc.tensor.transpose(bank[4][0:DV, LCMP:2 * LCMP], pev[:, :],
                                                ident[0:LCMP, 0:LCMP]).then_inc(turned1, 1)

                        def bias(w, peT, d, b, copies):
                            pe.wait_ge(copied1, copies)
                            for l in range(LCMP):
                                nc.tensor.matmul(bank[b][0:d, 0:1], w[:, l, :], peT[:, l:l + 1],
                                                 start=l == 0, stop=l == LCMP - 1)

                        def hidden_layer(w, d, b):
                            for l in range(LCMP):
                                rhs = ct[0:d, :, l:l + (NCMP - 1) * STRIDE + 1:STRIDE]
                                last = nc.tensor.matmul(bank[b][0:d, 0:G * NCMP].rearrange("p (g n) -> p g n", g=G),
                                                        w[:, l, :], rhs, start=l == 0, stop=l == LCMP - 1)
                            last.then_inc(turned1, 1)

                        def bias_k():
                            pe.wait_ge(w1_in, 16)
                            bias(w1, pekT, DK, 5, C_PE)

                        def turn_vc(half):
                            if half:
                                pe.wait_ge(copied1, C_BIASK + 2)
                            turn_c(VC, DV, 2 * half, 4)
                            turn_c(VC, DV, 2 * half + 1, 7)

                        def bias_v():
                            pe.wait_ge(w1_in, 32)
                            bias(w1v, pevT, DV, 4, C_VC)

                        def second_layers():
                            pe.wait_ge(hidden, 2)
                            for g in range(G):
                                nc.tensor.matmul(bank[5][0:NC, g * DK:(g + 1) * DK], hidk[:, g, :], w2k[:, :],
                                                 start=True, stop=True)
                            for g in range(G):
                                last = nc.tensor.matmul(bank[6][0:NC, g * DV:(g + 1) * DV], hidv[:, g, :], w2v[:, :],
                                                        start=True, stop=True)
                            last.then_inc(turned1, 1)

                        def turn_k_cmp():
                            pe.wait_ge(normed1, KCMP + 1)
                            for g in range(G):
                                last = nc.tensor.transpose(bank[7][0:DK, g * NC:(g + 1) * NC], kcmp[:, g, :],
                                                           ident[0:NC, 0:NC])
                            last.then_inc(turned1, 1)

                        beside = {0: turn_kc, 1: turn_pe, 2: bias_k, 3: lambda: hidden_layer(w1, DK, 6),
                                  4: lambda: turn_vc(0), 5: lambda: turn_vc(1), 6: bias_v,
                                  7: lambda: hidden_layer(w1v, DV, 7), 10: second_layers, 15: turn_k_cmp}
                        slot = 0
                        for c in range(CHUNKS):
                            for j in range(2):
                                pe.wait_ge(w_lo_made, p0 + 2 * c + j + 1)
                                for t in range(NT):
                                    if j == 0 and c > 0:
                                        pe.wait_ge(acc_free, a0 + NT * (c - 1) + t + 1)
                                    tok = slice(t * P, (t + 1) * P)
                                    for k in range(KP):
                                        kt = j * KP + k
                                        last = mm3(nc, bank[t][:, :], (h_hi[:, kt, tok], h_lo[:, kt, tok]),
                                                   (w_hi[j][:, k, :], w_lo[j][:, k, :]),
                                                   start=kt == 0, stop=kt == DM // P - 1)
                                    if j:
                                        last.then_inc(acc_done, 1)
                                    elif t == NT - 1:
                                        last.then_inc(w_used, 1)
                                    if slot in beside:
                                        beside[slot]()
                                    slot += 1
                                if j:
                                    nc.tensor.matmul(bank[5][0:1, 0:2], identb[:, 0:1], identb[:, 0:2], start=True,
                                                     stop=True).then_inc(w_used, 1)

                    @block.scalar
                    def _(act):
                        def high(g):
                            act.wait_ge(w_landed[g % 2], ((p0 + g) // 2 + 1) * 16)
                            act.wait_ge(w_used, p0 + g - 1)
                            nc.scalar.activation(w_hi[g % 2][:, :, :], w_raw[g % 2][:, :, :],
                                                 ACT.Copy).then_inc(w_hi_made, 1)

                        def square(n):
                            if n >= 2:
                                act.wait_ge(averaged, n - 1)
                            if n == KCMP:
                                act.wait_ge(cmp_out, 1)
                            src, _, _, rows = item[n]
                            nc.scalar.activation(sq[n % 2][0:rows, :], src, ACT.Square).then_inc(squared, 1)

                        def silu_z(c, t):
                            act.wait_ge(acc_done, a0 + NT * c + t + 1)
                            nc.scalar.activation(z_sb[:, t, c * CW:(c + 1) * CW], bank[t][:, :],
                                                 ACT.Silu).then_inc(acc_free, 1)

                        high(0)
                        high(1)
                        nc.scalar.activation(gates[:, :, :], gates[:, :, :], ACT.Tanh, scale=0.5).then_inc(gate_act, 1)
                        for n in range(6):
                            square(n)
                        high(2)
                        for n in range(6, 9):
                            square(n)
                        for t in range(NT):
                            silu_z(0, t)
                            square(9 + t)
                        high(3)
                        act.wait_ge(hid_clear, 1)
                        for hid, bi, d, b, t_at, c_at in ((hidk, biask, DK, 6, T_HIDK, C_BIASK),
                                                          (hidv, biasv, DV, 7, T_HIDV, C_BIASV)):
                            act.wait_ge(turned1, t_at)
                            act.wait_ge(copied1, c_at)
                            nc.scalar.activation(hid[:, :, 0:NCMP],
                                                 bank[b][0:d, 0:G * NCMP].rearrange("p (g n) -> p g n", g=G),
                                                 ACT.Silu, bias=bi[:, 0:1]).then_inc(hidden, 1)
                        for n in range(9 + NT, len(item)):
                            square(n)
                        for t in range(NT):
                            silu_z(1, t)
                        act.wait_ge(turned1, T_KCT)
                        nc.scalar.activation(kcT_hi[:, :, :], bank[7][0:DK, 0:G * NC].rearrange("p (g n) -> p g n", g=G),
                                             ACT.Copy).then_inc(kc_hi, 1)

                    @block.gpsimd
                    def _(pool):
                        o = Order(pool, pool_s)

                        def low(g):
                            pool.wait_ge(w_hi_made, p0 + g + 1)
                            nc.gpsimd.tensor_tensor(w_lo[g % 2][:, :, :], w_raw[g % 2][:, :, :],
                                                    w_hi[g % 2][:, :, :].bitcast(F32), ALU.subtract).then_inc(w_lo_made, 1)

                        def factor(n):
                            pool.wait_ge(averaged, n + 1)
                            m = mean[0:item[n][3], n, :]
                            o.link(nc.gpsimd.tensor_scalar(m, m, 1.0 / DK, EPS, ALU.mult, ALU.add))
                            nc.gpsimd.tensor_tensor(m, m, minus_half[0:item[n][3], 0:G], ALU.pow).then_inc(factor1, 1)

                        low(0)
                        low(1)
                        nc.gpsimd.memset(hidk[:, :, :], 0.0)
                        nc.gpsimd.memset(hidv[:, :, :], 0.0).then_inc(hid_clear, 1)
                        for n in range(6):
                            factor(n)
                        low(2)
                        for n in range(6, 12):
                            factor(n)
                        low(3)
                        for n in range(12, len(item)):
                            factor(n)

                    @block.vector
                    def _(dve):
                        o = Order(dve, dve_s)

                        def average(n):
                            rows = item[n][3]
                            dve.wait_ge(squared, n + 1)
                            nc.vector.tensor_reduce(mean[0:rows, n, :], sq[n % 2][0:rows, :].rearrange("p (g d) -> p g d", g=G),
                                                    AX.X, ALU.add).then_inc(averaged, 1)

                        def norm_rotate(n):
                            src, gain, t, rows = item[n]
                            dve.wait_ge(factor1, n + 1)
                            for g in range(G):
                                x = src[:, g * DK:(g + 1) * DK]
                                last = nc.vector.scalar_tensor_tensor(x, x, mean[0:rows, n, g:g + 1], gain[0:rows],
                                                                      ALU.mult, ALU.mult)
                            o.link(last)
                            x = src.rearrange("p (g d) -> p g d", g=G)
                            x1, x2 = x[:, :, 0:HALF1], x[:, :, HALF1:ROT]
                            cos = tcos[0:rows, t, HALF0:FREQS].unsqueeze(1).to_broadcast([rows, G, HALF1])
                            sin = tsin[0:rows, t, HALF0:FREQS].unsqueeze(1).to_broadcast([rows, G, HALF1])
                            ro = [rot[0:rows, a] for a in range(4)]
                            nc.vector.tensor_tensor(ro[0], x1, cos, ALU.mult)
                            nc.vector.tensor_tensor(ro[1], x2, sin, ALU.mult)
                            nc.vector.tensor_tensor(ro[2], x2, cos, ALU.mult)
                            o.link(nc.vector.tensor_tensor(ro[3], x1, sin, ALU.mult))
                            nc.vector.tensor_tensor(x1, ro[0], ro[1], ALU.subtract)
                            nc.vector.tensor_tensor(x2, ro[2], ro[3], ALU.add).then_inc(normed1, 1)
                            dve.wait_ge(normed1, n + 1)

                        def copy_out(dst, b, rows, c0=0, c1=512):
                            nc.vector.tensor_copy(dst, bank[b][0:rows, c0:c1]).then_inc(copied1, 1)

                        def copies_k():
                            for g in range(G):
                                dve.wait_ge(turned1, g + 1)
                                copy_out(ct[:, g, :], 4 + g, DK)
                            dve.wait_ge(turned1, T_PE)
                            nc.vector.tensor_copy(pekT[:, :], bank[4][0:DK, 0:LCMP])
                            copy_out(pevT[:, :], 4, DV, LCMP, 2 * LCMP)

                        def bias_k():
                            dve.wait_ge(turned1, T_HIDK)
                            copy_out(biask[:, :], 5, DK, 0, 1)

                        def copies_v():
                            for g in range(G):
                                dve.wait_ge(turned1, T_HIDK + g + 1)
                                copy_out(ct[0:DV, g, :], (4, 7)[g % 2], DV)

                        def bias_v():
                            dve.wait_ge(turned1, T_HIDV)
                            copy_out(biasv[:, :], 4, DV, 0, 1)

                        def compressed():
                            dve.wait_ge(turned1, T_CMP)
                            nc.vector.tensor_copy(vcmp[:, :, :], bank[6][0:NC, 0:G * DV].rearrange("p (g d) -> p g d", g=G))
                            nc.vector.tensor_copy(kcmp[:, :, :], bank[5][0:NC, 0:G * DK].rearrange("p (g d) -> p g d", g=G)
                                                  ).then_inc(cmp_out, 1)

                        before = {2: copies_k, 8: bias_k, 10: copies_v, 13: bias_v, KCMP: compressed}
                        for n in range(len(item)):
                            if n in before:
                                before[n]()
                            average(n)
                            if n:
                                norm_rotate(n - 1)
                        norm_rotate(len(item) - 1)
                        dve.wait_ge(gate_act, 1)
                        nc.vector.tensor_scalar(gates[:, :, :], gates[:, :, :], 0.5, 0.5, ALU.mult, ALU.add)
                        dve.wait_ge(kc_hi, 1)
                        nc.vector.tensor_tensor(kcT_lo[:, :, :], bank[7][0:DK, 0:G * NC].rearrange("p (g n) -> p g n", g=G),
                                                kcT_hi[:, :, :].bitcast(F32), ALU.subtract)

            kT_hi = sb(mixer, "kT_hi", [DK, 2, G, SEQ], F32R)
            kT_lo = sb(mixer, "kT_lo", [DK, 2, G, SEQ], F32R)
            v_diag = sb(mixer, "v_diag", [P, G, NT, DV])

            with ExitStack() as ctx:
                kt_turned, kt_hi, kt_lo, spread, clear = (sem(n) for n in (
                    "kt_turned", "kt_hi", "kt_lo", "spread", "v_clear"))
                block = ctx.enter_context(nc.Block())

                @block.sync
                def _(sp):
                    sp.wait_ge(clear, 1)
                    for i in range(NT):
                        sp.dma_start(v_diag[i * NC:(i + 1) * NC, :, i, :], vcmp[:, :, :]).then_inc(spread, 16)
                    sp.wait_ge(spread, 16 * NT)

                @block.gpsimd
                def _(pool):
                    nc.gpsimd.memset(v_diag[:, :, :, :], 0.0).then_inc(clear, 1)

                @block.tensor
                def _(pe):
                    for u in range(2 * G):
                        c0, g = (KS, KW)[u // G], u % G
                        for t in range(NT):
                            last = nc.tensor.transpose(bank[u][0:DK, t * P:(t + 1) * P],
                                                       kv[:, t, c0 + g * DK:c0 + (g + 1) * DK], ident[:, :])
                        last.then_inc(kt_turned, 1)

                @block.scalar
                def _(act):
                    for u in range(2 * G):
                        act.wait_ge(kt_turned, u + 1)
                        nc.scalar.activation(kT_hi[:, u // G, u % G, :], bank[u][0:DK, :], ACT.Copy).then_inc(kt_hi, 1)

                @block.vector
                def _(dve):
                    for u in range(2 * G):
                        dve.wait_ge(kt_hi, u + 1)
                        nc.vector.tensor_tensor(kT_lo[:, u // G, u % G, :], bank[u][0:DK, :],
                                                kT_hi[:, u // G, u % G, :].bitcast(F32), ALU.subtract).then_inc(kt_lo, 1)

            with ExitStack() as ctx:
                U = 2 * NT
                q_stage = sb(ctx, "q_stage", [P, NT, DK])
                qT_hi = [sb(ctx, f"qT_hi{a}", [DK, SEQ], F32R) for a in range(2)]
                qT_lo = [sb(ctx, f"qT_lo{a}", [DK, SEQ], F32R) for a in range(2)]
                prob = sb(ctx, "prob1", [P, 3, SEQ])
                probT = sb(ctx, "probT1", [P, 2, SEQ])
                negmax = sb(ctx, "negmax1", [P, 2, U])
                sums = sb(ctx, "sums1", [P, 2, U])
                coef = sb(ctx, "coef1", [P, U])
                c_s = sb(ctx, "c_s", [P, NT, NC])
                c_e = sb(ctx, "c_e", [P, NT, NC])
                c_eT = sb(ctx, "c_eT", [P, P])
                c_max = sb(ctx, "c_max", [P, NT])
                c_sum = sb(ctx, "c_sum", [P, NT])
                c_coef = sb(ctx, "c_coef", [P, NT])
                o_sw = sb(ctx, "o_sw", [P, NT, 2, DV])
                o_c = sb(ctx, "o_c", [P, NT, DV])
                score_bank, pt_bank, o_bank, c_bank = bank[0:3], bank[3:5], bank[5:7], bank[7]
                x_done, x_hi, q_ready, q_staged = sem("x_done1"), sem("x_hi1"), sem("q_ready1"), sem("q_staged")
                s_done, max_done, exp_done = sem("s_done1"), sem("max_done1"), sem("exp_done1")
                t_done, pt_ready, pv_done = sem("t_done1"), sem("pt_ready1"), sem("pv_done1")
                pt_ready_act, coef_done = sem("pt_ready_act1"), sem("coef_done")
                c_done, c_left, c_shift, c_exp, ct_done, ct_ready, cv_done, cv_left = (sem(n) for n in (
                    "c_done", "c_left", "c_shift", "c_exp", "ct_done", "ct_ready", "cv_done", "cv_left"))
                o_left, mixed, dve_s, pool_s = sem("o_left"), sem("mixed"), sem("dve_o2"), sem("pool_o2")
                block = ctx.enter_context(nc.Block())
                UNITS = [(3, 0), (0, 0), (3, 1), (0, 1), (2, 0), (1, 0), (2, 1), (1, 1)]
                by_act = (1, 2, 3, 4, 6)
                n_act, n_dve = len(by_act), U - len(by_act)
                keys_of = lambda u: (UNITS[u][0] + 1) * P
                at_of = lambda u: 2 * UNITS[u][0] + UNITS[u][1]

                def heads(eng, step):
                    step(0, 0, False, True)
                    step(1, 1, True, True)
                    with eng.Fori(1, H // 2 - 1) as pair:
                        step(2 * pair, 0, True, True)
                        step(2 * pair + 1, 1, True, True)
                    step(H - 2, 0, True, True)
                    step(H - 1, 1, True, False)

                @block.tensor
                def _(pe):
                    def turn_q(n):
                        pe.wait_ge(q_staged, n + 1)
                        for t in range(NT):
                            last = nc.tensor.transpose(c_bank[0:DK, t * P:(t + 1) * P],
                                                       q_stage[:, t, :], ident[:, :])
                        last.then_inc(x_done, 1)

                    def scores(h, a, u):
                        i, b = UNITS[u]
                        tok, keys = slice(i * P, (i + 1) * P), (i + 1) * P
                        dst = score_bank[u % 3]
                        mm3(nc, dst[:, 0:keys], (qT_hi[a][:, tok], qT_lo[a][:, tok]),
                            (kT_hi[:, b, h // HPG, 0:keys], kT_lo[:, b, h // HPG, 0:keys]), start=True, stop=False)
                        nc.tensor.matmul(dst[:, tok], identb[:, :], causal[:, :], start=False,
                                         stop=True).then_inc(s_done, 1)

                    def compressed_scores(h, a):
                        for i in range(NT):
                            tok = slice(i * P, (i + 1) * P)
                            last = mm3(nc, c_bank[:, i * NC:(i + 1) * NC], (qT_hi[a][:, tok], qT_lo[a][:, tok]),
                                       (kcT_hi[:, h // HPG, :], kcT_lo[:, h // HPG, :]), start=True, stop=True)
                        last.then_inc(c_done, 1)

                    def turn_probs(h, u):
                        pe.wait_ge(exp_done, U * h + u + 1)
                        for j in range(UNITS[u][0] + 1):
                            last = nc.tensor.transpose(pt_bank[u % 2][:, j * P:(j + 1) * P],
                                                       prob[:, u % 3, j * P:(j + 1) * P], ident[:, :])
                        last.then_inc(t_done, 1)

                    def values(h, a, u):
                        i, b = UNITS[u]
                        if u in by_act:
                            pe.wait_ge(pt_ready_act, n_act * h + by_act.index(u) + 1)
                        else:
                            pe.wait_ge(pt_ready, n_dve * h + u + 1 - sum(v < u for v in by_act))
                        if u == 0 and (not isinstance(h, int) or h >= 2):
                            pe.wait_ge(o_left, h - 1)
                        for j in range(i + 1):
                            c0 = (VS, VW)[b]
                            last = nc.tensor.matmul(o_bank[a][:, at_of(u) * DV:(at_of(u) + 1) * DV],
                                                    probT[:, u % 2, j * P:(j + 1) * P],
                                                    kv[:, j, bass.ds(c0 + (h // HPG) * DV, DV)],
                                                    start=j == 0, stop=j == i)
                        last.then_inc(pv_done, 1)

                    def step(h, a, prev, nxt):
                        for k in range(U):
                            if k < U - 2:
                                scores(h, a, k + 2)
                            turn_probs(h, k)
                            if k == 0 and nxt:
                                pe.wait_ge(c_left, h + 1)
                                turn_q(h + 1)
                            if k == 2:
                                if nxt:
                                    pe.wait_ge(q_ready, h + 2)
                                pe.wait_ge(c_exp, h + 1)
                                nc.tensor.transpose(c_bank[:, 0:P], c_e[:, :, :].rearrange("p i n -> p (i n)"),
                                                    ident[:, :]).then_inc(ct_done, 1)
                            if k == 4:
                                pe.wait_ge(ct_ready, h + 1)
                                nc.tensor.matmul(c_bank[:, 0:NT * DV], c_eT[:, :],
                                                 v_diag[:, h // HPG, :, :].rearrange("p i d -> p (i d)"),
                                                 start=True, stop=True).then_inc(cv_done, 1)
                            if k:
                                values(h, a, k - 1)
                            elif prev:
                                values(h - 1, 1 - a, U - 1)
                            if k == U - 2 and nxt:
                                pe.wait_ge(cv_left, h + 1)
                                compressed_scores(h + 1, 1 - a)
                            if k >= U - 2 and nxt:
                                scores(h + 1, 1 - a, k + 2 - U)

                    turn_q(0)
                    pe.wait_ge(q_ready, 1)
                    compressed_scores(0, 0)
                    scores(0, 0, 0)
                    scores(0, 0, 1)
                    heads(pe, step)
                    values(H - 1, 1, U - 1)

                @block.scalar
                def _(act):
                    def high(n, a):
                        act.wait_ge(x_done, n + 1)
                        nc.scalar.activation(qT_hi[a][:, :], c_bank[0:DK, :], ACT.Copy).then_inc(x_hi, 1)

                    def exponential(h, a, u):
                        act.wait_ge(max_done, U * h + u + 1)
                        nc.scalar.activation(prob[:, u % 3, 0:keys_of(u)], score_bank[u % 3][:, 0:keys_of(u)],
                                             ACT.Exp, bias=negmax[:, a, u:u + 1],
                                             accum_out=sums[:, a, at_of(u):at_of(u) + 1]
                                             ).then_inc(exp_done, 1)

                    def step(h, a, prev, nxt):
                        for k in range(U):
                            if k < U - 2:
                                exponential(h, a, k + 2)
                            if k in by_act:
                                act.wait_ge(t_done, U * h + k + 1)
                                nc.scalar.activation(probT[:, k % 2, 0:keys_of(k)], pt_bank[k % 2][:, 0:keys_of(k)],
                                                     ACT.Copy).then_inc(pt_ready_act, 1)
                            if k == 0:
                                if nxt:
                                    high(h + 1, 1 - a)
                            if k == 1:
                                act.wait_ge(c_shift, h + 1)
                                nc.scalar.activation(c_e[:, :, :], c_s[:, :, :], ACT.Exp).then_inc(c_exp, 1)
                            if k >= U - 2 and nxt:
                                exponential(h + 1, 1 - a, k + 2 - U)

                    high(0, 0)
                    exponential(0, 0, 0)
                    exponential(0, 0, 1)
                    heads(act, step)

                @block.gpsimd
                def _(pool):
                    o = Order(pool, pool_s)

                    def stage(n):
                        nc.gpsimd.tensor_copy(q_stage[:, :, :], qs[:, :, bass.ds(n * DK, DK)]).then_inc(q_staged, 1)

                    def mix(h):
                        pool.wait_ge(o_left, h + 1)
                        o.link(nc.gpsimd.tensor_tensor(o_c[:, :, :], o_c[:, :, :], o_sw[:, :, 0, :], ALU.add))
                        o.link(nc.gpsimd.tensor_tensor(o_c[:, :, :], o_c[:, :, :], o_sw[:, :, 1, :], ALU.add))
                        at = z_sb[:, :, bass.ds(h * DV, DV)]
                        nc.gpsimd.tensor_tensor(at, o_c[:, :, :], at, ALU.mult).then_inc(mixed, 1)

                    def step(h, a, prev, nxt):
                        if not isinstance(h, int) or h + 2 < H:
                            pool.wait_ge(x_done, h + 2)
                            stage(h + 2)
                        if prev:
                            o.base, o.n = 2 * (h - 1), 0
                            mix(h - 1)

                    stage(0)
                    pool.wait_ge(x_done, 1)
                    stage(1)
                    heads(pool, step)
                    mix(H - 1)

                @block.vector
                def _(dve):
                    o = Order(dve, dve_s)

                    def low(n, a):
                        dve.wait_ge(x_hi, n + 1)
                        nc.vector.tensor_tensor(qT_lo[a][:, :], c_bank[0:DK, :], qT_hi[a][:, :].bitcast(F32),
                                                ALU.subtract).then_inc(q_ready, 1)

                    def maximum(h, a, u):
                        dve.wait_ge(s_done, U * h + u + 1)
                        nc.vector.tensor_reduce(negmax[:, a, u:u + 1], score_bank[u % 3][:, 0:keys_of(u)],
                                                AX.X, ALU.max, negate=True).then_inc(max_done, 1)

                    def leave(h, a):
                        dve.wait_ge(exp_done, U * h + U)
                        o.link(nc.vector.reciprocal(coef[:, :], sums[:, a, :]))
                        two = coef[:, :].rearrange("p (i b) -> p i b", b=2)
                        nc.vector.tensor_tensor(two, two, gates[:, :, bass.ds(h * 3 + 1, 2)],
                                                ALU.mult).then_inc(coef_done, 1)
                        dve.wait_ge(coef_done, h + 1)
                        dve.wait_ge(pv_done, U * h + U)
                        nc.vector.tensor_tensor(o_sw[:, :, :, :].rearrange("p i b d -> p (i b) d"),
                                                o_bank[a][:, :].rearrange("p (u d) -> p u d", d=DV),
                                                coef[:, :].unsqueeze(2).to_broadcast([P, U, DV]),
                                                ALU.mult).then_inc(o_left, 1)

                    def step(h, a, prev, nxt):
                        o.base, o.n = 7 * h, 0
                        for k in range(U):
                            if k < U - 2:
                                maximum(h, a, k + 2)
                            if k == 0:
                                dve.wait_ge(c_done, h + 1)
                                nc.vector.tensor_tensor(c_s[:, :, :],
                                                        c_bank[:, 0:NT * NC].rearrange("p (i n) -> p i n", n=NC),
                                                        cmask[:, :, :], ALU.add).then_inc(c_left, 1)
                                dve.wait_ge(c_left, h + 1)
                                o.link(nc.vector.tensor_reduce(c_max[:, :], c_s[:, :, :], AX.X, ALU.max))
                                o.link(nc.vector.tensor_scalar(c_max[:, :], c_max[:, :], FLOOR, None, ALU.max))
                                nc.vector.tensor_tensor(c_s[:, :, :], c_s[:, :, :],
                                                        c_max[:, :].unsqueeze(2).to_broadcast([P, NT, NC]),
                                                        ALU.subtract).then_inc(c_shift, 1)
                            if k not in by_act:
                                dve.wait_ge(t_done, U * h + k + 1)
                                nc.vector.tensor_copy(probT[:, k % 2, 0:keys_of(k)],
                                                      pt_bank[k % 2][:, 0:keys_of(k)]).then_inc(pt_ready, 1)
                            if k == 1 and nxt:
                                low(h + 1, 1 - a)
                            if k == 1 and prev:
                                leave(h - 1, 1 - a)
                            elif k == 1:
                                o.link(nc.vector.memset(coef[:, :], 0.0))
                            if k == 2:
                                dve.wait_ge(c_exp, h + 1)
                                o.link(nc.vector.tensor_reduce(c_sum[:, :], c_e[:, :, :], AX.X, ALU.add))
                                o.link(nc.vector.tensor_scalar(c_sum[:, :], c_sum[:, :], 1e-30, None, ALU.max))
                                o.link(nc.vector.reciprocal(c_coef[:, :], c_sum[:, :]))
                                o.link(nc.vector.tensor_tensor(c_coef[:, :], c_coef[:, :],
                                                               gates[:, :, bass.ds(h * 3, 1)].rearrange("p t g -> p (t g)"),
                                                               ALU.mult))
                            if k == 3:
                                dve.wait_ge(ct_done, h + 1)
                                nc.vector.tensor_copy(c_eT[:, :], c_bank[:, 0:P]).then_inc(ct_ready, 1)
                            if k == 5:
                                if prev:
                                    dve.wait_ge(mixed, h)
                                dve.wait_ge(cv_done, h + 1)
                                nc.vector.tensor_tensor(o_c[:, :, :],
                                                        c_bank[:, 0:NT * DV].rearrange("p (i d) -> p i d", d=DV),
                                                        c_coef[:, :].unsqueeze(2).to_broadcast([P, NT, DV]),
                                                        ALU.mult).then_inc(cv_left, 1)
                            if k >= U - 2 and nxt:
                                maximum(h + 1, 1 - a, k + 2 - U)
                        assert o.n == 7, o.n

                    low(0, 0)
                    maximum(0, 0, 0)
                    maximum(0, 0, 1)
                    heads(dve, step)
                    o.base, o.n = 7 * H, 0
                    leave(H - 1, 1)

            mixer.close()

            with ExitStack() as ph:
                o_hi = sb(ph, "o1_hi", [P, Z1 // P, SEQ], F32R)
                o_lo = sb(ph, "o1_lo", [P, Z1 // P, SEQ], F32R)
                with ExitStack() as ctx:
                    transpose_block(ctx, "o1", z_sb, Z1 // P, None, o_hi, o_lo)
                with ExitStack() as ctx:
                    def evacuate(what, t, c0, width, acc):
                        at = x_sb[:, t, bass.ds(c0, width)]
                        return nc.vector.tensor_tensor(at, acc, at, ALU.add)
                    run_stream(ctx, [(nsa_w_out[0], 0, CW, DM // CW, "x")], o_hi, o_lo, evacuate, "dve")
                with ExitStack() as ctx:
                    stored = sem("stored")
                    block = ctx.enter_context(nc.Block())

                    @block.sync
                    def _(sp):
                        for t in range(NT):
                            sp.dma_start(out[0, t * P:(t + 1) * P, :], x_sb[:, t, :]).then_inc(stored, 16)
                        sp.wait_ge(stored, 16 * NT)


_INS = ["x", "positions", "inv_freq", "norm_g", "mla_w_in", "mla_g_cq", "mla_w_uq", "mla_g_ckv", "mla_w_ukv",
        "mla_g_q", "mla_g_k", "mla_w_out", "nsa_w_in", "nsa_g_q", "nsa_g_k", "nsa_pe_k", "nsa_w1_k",
        "nsa_w2_k", "nsa_pe_v", "nsa_w1_v", "nsa_w2_v", "nsa_w_out"]


def kernel(**inputs):
    import concourse.bacc as bacc
    from concourse.bass_utils import run_bass_kernel_spmd

    inputs["inv_freq"] = np.concatenate(
        [THETA ** (-np.arange(half) / half) for half in (HALF0, HALF1)]).astype(np.float32)
    nc = bacc.Bacc("TRN2", target_bir_lowering=False, num_devices=1)
    arrays, args = {}, []
    for name in _INS:
        a = np.ascontiguousarray(inputs[name])
        arrays[f"in_{name}"] = a
        args.append(nc.dram_tensor(f"in_{name}", a.shape, mybir.dt.from_np(a.dtype), kind="ExternalInput").ap())
    out = nc.dram_tensor("out_0", (1, SEQ, DM), F32, kind="ExternalOutput").ap()
    trunk(nc, *args, out)
    r = run_bass_kernel_spmd(nc, [arrays], core_ids=[0])
    return r.results[0]["out_0"]
```

```python
from contextlib import ExitStack

import numpy as np
import concourse.bass as bass
from concourse import mybir

F32 = mybir.dt.float32
F32R = mybir.dt.float32r
BF16 = mybir.dt.bfloat16
I32 = mybir.dt.int32
ACT = mybir.ActivationFunctionType
ALU = mybir.AluOpType
AX = mybir.AxisListType

P = 128
SEQ, DM = 512, 1024
NT = SEQ // P
EPS = 1e-6
THETA = 500000.0
NEG = -1e30
FLOOR = -1e20

H = 16
NOPE, ROPE, DV0 = 128, 64, 128
QK = NOPE + ROPE
HQK = QK // 2
CQ, CKV = 384, 256
KQ, KKV = CQ // P, CKV // P
CC = CQ + CKV + ROPE
ZZ = H * DV0
HALF0 = ROPE // 2
WQ, WKV = QK, NOPE + DV0

G, HPG, DK, DV = 4, 4, 96, 64
ROT = DK // 4
HALF1 = ROT // 2
LCMP, STRIDE = 32, 16
NCMP = (SEQ - LCMP) // STRIDE + 1
NC = 32
QW = H * DK
KVW = 3 * G * (DK + DV)
KC, VC, KS, VS, KW, VW = 0, 384, 640, 1024, 1280, 1664
GW = 3 * H
Z1 = H * DV
FREQS = HALF0 + HALF1

KP = 4
CW = 512
TWO_PI = 2 * np.pi
C1 = 6.28125
C2 = float(np.floor((TWO_PI - C1) * 2**17) / 2**17)
C3 = float(TWO_PI - C1 - C2)
ROUND = 1.5 * 2**23


class Order:

    def __init__(self, eng, sem):
        self.eng, self.sem, self.n, self.base = eng, sem, 0, 0

    def link(self, ins):
        ins.then_inc(self.sem, 1)
        self.n += 1
        self.eng.wait_ge(self.sem, self.base + self.n)

    def enter(self, i, steps):
        self.start, self.steps = self.base + self.n, steps
        self.base, self.n = self.start + i * steps, 0

    def leave(self, trips):
        assert self.n == self.steps, (self.n, self.steps)
        self.base, self.n = self.start + trips * self.steps, 0


def mm3(nc, out, a, b, start, stop):
    nc.tensor.matmul(out, a[0], b[0], start=start, stop=False)
    nc.tensor.matmul(out, a[0], b[1], start=False, stop=False)
    return nc.tensor.matmul(out, a[1], b[0], start=False, stop=stop)


def trunk(nc, x, positions, inv_freq, norm_g, mla_w_in, mla_g_cq, mla_w_uq, mla_g_ckv, mla_w_ukv,
          mla_g_q, mla_g_k, mla_w_out, nsa_w_in, nsa_g_q, nsa_g_k, nsa_pe_k, nsa_w1_k, nsa_w2_k,
          nsa_pe_v, nsa_w1_v, nsa_w2_v, nsa_w_out, out):
    with ExitStack() as whole:
        names = set()

        def sem(name):
            assert name not in names
            names.add(name)
            return whole.enter_context(nc.semaphore(name))

        def sb(ctx, name, shape, dt=F32):
            return ctx.enter_context(nc.sbuf_tensor(name, shape, dt))

        keep = lambda name, shape, dt=F32: sb(whole, name, shape, dt)
        whole.enter_context(nc.allow_non_contiguous_dma(reason="gains and positions are short"))
        bank = [whole.enter_context(nc.psum_tensor(f"bank{b}", [P, 512], F32)) for b in range(8)]

        x_sb = keep("x_sb", [P, NT, DM])
        ident = keep("ident", [P, P])
        identb = keep("identb", [P, P], BF16)
        causal = keep("causal", [P, P], BF16)
        cmask = keep("cmask", [P, NT, NC])
        zeros = keep("zeros", [P, NT * NC])
        minus_half = keep("minus_half", [P, 16])
        tcos = keep("tcos", [P, NT + 1, FREQS])
        tsin = keep("tsin", [P, NT + 1, FREQS])
        g_x = keep("g_x", [P, 2, DM // P])
        g_c = keep("g_c", [P, KQ + KKV])
        gq0 = keep("gq0", [P, QK])
        gk0 = keep("gk0", [P, QK])
        gq1 = keep("gq1", [P, DK])
        gk1 = keep("gk1", [P, 3, DK])

        w_raw = [keep(f"w_raw{s}", [P, KP, CW]) for s in range(2)]
        w_hi = [keep(f"w_hi{s}", [P, KP, CW], F32R) for s in range(2)]
        w_lo = [keep(f"w_lo{s}", [P, KP, CW], F32R) for s in range(2)]
        w_landed = [sem(f"w_landed{s}") for s in range(2)]
        w_hi_made, w_lo_made, w_used = sem("w_hi_made"), sem("w_lo_made"), sem("w_used")
        acc_done, acc_free = sem("acc_done"), sem("acc_free")
        piece_base, acc_base = [0], [0]

        def positive(v):
            return not isinstance(v, int) or v > 0

        def load_piece(sp, g, slot, src):
            if not isinstance(g, int) or g >= 2:
                sp.wait_ge(w_lo_made, g - 1)
            sp.dma_start(w_raw[slot][:, :, 0:src.shape[2]], src).then_inc(w_landed[slot], 16)

        def hi_piece(act, g, slot, round_, width):
            act.wait_ge(w_landed[slot], (round_ + 1) * 16)
            if not isinstance(g, int) or g >= 2:
                act.wait_ge(w_used, g - 1)
            nc.scalar.activation(w_hi[slot][:, :, 0:width], w_raw[slot][:, :, 0:width],
                                 ACT.Copy).then_inc(w_hi_made, 1)

        def lo_piece(pool, g, slot, width):
            pool.wait_ge(w_hi_made, g + 1)
            nc.gpsimd.tensor_tensor(w_lo[slot][:, :, 0:width], w_raw[slot][:, :, 0:width],
                                    w_hi[slot][:, :, 0:width].bitcast(F32), ALU.subtract).then_inc(w_lo_made, 1)

        def first_pieces(w, col0, width):
            rows = w.rearrange("(k p) c -> p k c", p=P)
            return [rows[:, j * KP:(j + 1) * KP, col0:col0 + width] for j in range(2)]

        def stream(ctx, loops, act_hi, act_lo, evacuate, loaded, split, ahead, behind):
            plan = []
            for w, col0, width, chunks, what in loops:
                kt = w.shape[0] // P
                plan.append((w, col0, width, chunks, what, kt // KP, piece_base[0], acc_base[0]))
                piece_base[0] += kt // KP * chunks
                acc_base[0] += NT * chunks
            assert piece_base[0] % 2 == 0

            next0 = piece_base[0]

            def pieces(eng, skip, do):
                for n, entry in enumerate(plan):
                    chunks, ppc = entry[3], entry[5]
                    peel = n == 0 or (behind is not None and entry[4] == behind[0])
                    if peel:
                        for j in range(0 if n else skip, ppc):
                            do(entry, 0, j)
                    if chunks > peel:
                        with eng.Fori(int(peel), chunks) as c:
                            for j in range(ppc):
                                do(entry, c, j)

            def load(sp):
                def one(entry, c, j):
                    w, col0, width, chunks, what, ppc, p0, a0 = entry
                    rows = w.rearrange("(k p) c -> p k c", p=P)
                    load_piece(sp, p0 + c * ppc + j, j % 2,
                               rows[:, j * KP:(j + 1) * KP, bass.ds(col0 + c * width, width)])
                pieces(sp, loaded, one)
                for j, src in enumerate(ahead[0]):
                    load_piece(sp, next0 + j, j, src)

            def split_hi(act):
                def one(entry, c, j):
                    w, col0, width, chunks, what, ppc, p0, a0 = entry
                    hi_piece(act, p0 + c * ppc + j, j % 2, p0 // 2 + c * (ppc // 2) + j // 2, width)
                    if behind and what == behind[0] and j == ppc - 1 and positive(c):
                        act.wait_ge(acc_free, a0 + NT * c)
                        behind[1]((c - 1) * width, width)
                pieces(act, split, one)
                for j in range(ahead[1]):
                    hi_piece(act, next0 + j, j, next0 // 2, ahead[0][j].shape[2])

            def split_lo(pool):
                def one(entry, c, j):
                    w, col0, width, chunks, what, ppc, p0, a0 = entry
                    lo_piece(pool, p0 + c * ppc + j, j % 2, width)
                pieces(pool, split, one)
                for j in range(ahead[1]):
                    lo_piece(pool, next0 + j, j, ahead[0][j].shape[2])

            def products(pe):
                for w, col0, width, chunks, what, ppc, p0, a0 in plan:
                    def chunk(c):
                        for j in range(ppc):
                            pe.wait_ge(w_lo_made, p0 + c * ppc + j + 1)
                            for t in range(NT):
                                a = a0 + c * NT + t
                                if j == 0 and (not isinstance(a, int) or a >= NT):
                                    pe.wait_ge(acc_free, a - NT + 1)
                                for k in range(KP):
                                    kt = j * KP + k
                                    tok = slice(t * P, (t + 1) * P)
                                    last = mm3(nc, bank[t][:, 0:width],
                                               (act_hi[:, kt, tok], act_lo[:, kt, tok]),
                                               (w_hi[j % 2][:, k, 0:width], w_lo[j % 2][:, k, 0:width]),
                                               start=kt == 0, stop=kt == ppc * KP - 1)
                                if j == ppc - 1:
                                    last.then_inc(acc_done, 1)
                            nc.tensor.matmul(bank[4][:, 0:P], identb[:, :], identb[:, :], start=True,
                                             stop=True).then_inc(w_used, 1)
                    first = 1 if a0 == 0 else 0
                    if first:
                        chunk(0)
                    if chunks > first:
                        with pe.Fori(first, chunks) as c:
                            chunk(c)

            def evacuation(eng):
                for w, col0, width, chunks, what, ppc, p0, a0 in plan:
                    with eng.Fori(0, chunks) as c:
                        for t in range(NT):
                            eng.wait_ge(acc_done, a0 + c * NT + t + 1)
                            evacuate(what, t, c * width, width, bank[t][:, 0:width]).then_inc(acc_free, 1)

            return load, split_hi, split_lo, products, evacuation

        with ExitStack() as ctx:
            pos_i = sb(ctx, "pos_i", [P, NT + 1], I32)
            pos_f = sb(ctx, "pos_f", [P, NT + 1])
            freq = sb(ctx, "freq", [P, FREQS])
            ang = sb(ctx, "ang", [P, (NT + 1) * FREQS])
            turns = sb(ctx, "turns", [P, (NT + 1) * FREQS])
            red = sb(ctx, "red", [P, (NT + 1) * FREQS])
            quarter = sb(ctx, "quarter", [P, (NT + 1) * FREQS])
            loaded, pos_loaded, pos_clear = sem("loaded"), sem("pos_loaded"), sem("pos_clear")
            made, table_ready, dve_order = sem("made"), sem("table_ready"), sem("dve_order0")
            pool_order, tables_done = sem("pool_order0"), sem("tables_done")
            block = ctx.enter_context(nc.Block())

            @block.sync
            def _(sp):
                sp.wait_ge(pos_clear, 1)
                row = lambda ap: ap.rearrange("(a d) -> a d", a=1)
                pieces = [
                    (pos_i[:, 0:NT], positions[0].rearrange("(t p) -> p t", p=P)),
                    (pos_i[0:NCMP, NT:NT + 1],
                     positions[0, LCMP - 1:SEQ].rearrange("(n s) -> n s", n=1).rearrange("n s -> s n")[0:SEQ - LCMP + 1:STRIDE, :]),
                    (freq[:, :], row(inv_freq).to_broadcast([P, FREQS])),
                    (g_x[:, :, :], norm_g.rearrange("l (k p) -> p l k", p=P)),
                    (g_c[:, 0:KQ], mla_g_cq[0].rearrange("(k p) -> p k", p=P)),
                    (g_c[:, KQ:KQ + KKV], mla_g_ckv[0].rearrange("(k p) -> p k", p=P)),
                    (gq0[:, :], row(mla_g_q[0]).to_broadcast([P, QK])),
                    (gk0[:, :], row(mla_g_k[0]).to_broadcast([P, QK])),
                    (gq1[:, :], row(nsa_g_q[0]).to_broadcast([P, DK])),
                ] + [(gk1[:, b, :], row(nsa_g_k[0, b]).to_broadcast([P, DK])) for b in range(3)]
                for dst, src in pieces[0:3]:
                    sp.dma_start(dst, src).then_inc(pos_loaded, 16)
                for t in range(NT):
                    sp.dma_start(x_sb[:, t, :], x[0, t * P:(t + 1) * P, :]).then_inc(loaded, 16)
                for dst, src in pieces[3:]:
                    sp.dma_start(dst, src).then_inc(loaded, 16)
                for j, src in enumerate(first_pieces(mla_w_in[0], 0, CC // 2)):
                    load_piece(sp, j, j, src)
                sp.wait_ge(loaded, 16 * (len(pieces) - 3 + NT))

            @block.gpsimd
            def _(pool):
                o = Order(pool, pool_order)
                nc.gpsimd.memset(pos_i[:, :], 0).then_inc(pos_clear, 1)
                nc.gpsimd.memset(minus_half[:, :], -0.5)
                o.link(nc.gpsimd.memset(zeros[:, :], 0.0))
                z = zeros[:, 0:P]
                o.link(nc.gpsimd.affine_select(out=ident[:, :], in_=z, compare_op=ALU.not_equal, fill=1.0,
                                               base=0, pattern=[[-1, P]], channel_multiplier=1))
                nc.gpsimd.affine_select(out=identb[:, :], in_=z, compare_op=ALU.not_equal, fill=1.0,
                                        base=0, pattern=[[-1, P]], channel_multiplier=1)
                nc.gpsimd.affine_select(out=causal[:, :], in_=z, compare_op=ALU.is_ge, fill=NEG,
                                        base=0, pattern=[[-1, P]], channel_multiplier=1)
                nc.gpsimd.affine_select(out=cmask[:, :, :], in_=z.rearrange("p (i n) -> p i n", n=NC),
                                        compare_op=ALU.is_ge, fill=NEG, base=-(LCMP - 1),
                                        pattern=[[P, NT], [-STRIDE, NC]], channel_multiplier=1
                                        ).then_inc(made, 1)

            @block.vector
            def _(dve):
                o = Order(dve, dve_order)
                dve.wait_ge(pos_loaded, 16 * 3)
                o.link(nc.vector.tensor_copy(pos_f[:, :], pos_i[:, :]))
                for t in range(NT + 1):
                    last = nc.vector.tensor_scalar(ang[:, t * FREQS:(t + 1) * FREQS], freq[:, :],
                                                   pos_f[:, t:t + 1], None, ALU.mult)
                o.link(last)
                o.link(nc.vector.tensor_scalar(turns[:, :], ang[:, :], 1 / TWO_PI, ROUND, ALU.mult, ALU.add))
                o.link(nc.vector.tensor_scalar(turns[:, :], turns[:, :], -ROUND, None, ALU.add))
                o.link(nc.vector.scalar_tensor_tensor(ang[:, :], turns[:, :], -C1, ang[:, :], ALU.mult, ALU.add))
                o.link(nc.vector.scalar_tensor_tensor(ang[:, :], turns[:, :], -C2, ang[:, :], ALU.mult, ALU.add))
                o.link(nc.vector.scalar_tensor_tensor(ang[:, :], turns[:, :], -C3, ang[:, :], ALU.mult, ALU.add))
                pi = float(np.nextafter(np.float32(np.pi), np.float32(0)))
                o.link(nc.vector.tensor_scalar(red[:, :], ang[:, :], pi, -pi, ALU.min, ALU.max))
                o.link(nc.vector.scalar_tensor_tensor(quarter[:, :], red[:, :], -1.0, red[:, :], ALU.mult, ALU.max))
                nc.vector.tensor_scalar(quarter[:, :], quarter[:, :], -1.0, float(np.pi / 2), ALU.mult,
                                        ALU.add).then_inc(table_ready, 1)
                dve.wait_ge(loaded, 16 * (9 + NT))
                nc.vector.tensor_scalar(gq0[:, :], gq0[:, :], float(QK) ** -0.5, None, ALU.mult)
                nc.vector.tensor_scalar(gq1[:, :], gq1[:, :], float(DK) ** -0.5, None, ALU.mult)

            @block.scalar
            def _(act):
                act.wait_ge(table_ready, 1)
                nc.scalar.activation(tsin[:, :, :].rearrange("p t f -> p (t f)"), red[:, :], ACT.Sin)
                nc.scalar.activation(tcos[:, :, :].rearrange("p t f -> p (t f)"), quarter[:, :],
                                     ACT.Sin).then_inc(tables_done, 1)
                act.wait_ge(tables_done, 1)

        def transpose_block(ctx, tag, src, kt, gain, dst_hi, dst_lo, norm=None, piece=None):
            norm = norm or []
            normed = sb(ctx, f"normed_{tag}", [P, NT, kt * P]) if norm else src
            junk = sb(ctx, f"junk_{tag}", [P, DM if norm else 2])
            ms = sb(ctx, f"ms_{tag}", [P, NT, 2])
            squared, factor, scaled = sem(f"squared_{tag}"), sem(f"factor_{tag}"), sem(f"scaled_{tag}")
            turned, hi_made, lo_made = sem(f"turned_{tag}"), sem(f"hi_{tag}"), sem(f"lo_{tag}")
            pool_o, act_o = sem(f"pool_o_{tag}"), sem(f"act_o_{tag}")
            block = ctx.enter_context(nc.Block())

            @block.scalar
            def _(act):
                o = Order(act, act_o)
                for t in range(NT if norm else 0):
                    for s, (c0, width) in enumerate(norm):
                        o.link(nc.scalar.activation(junk[:, 0:width], src[:, t, c0:c0 + width], ACT.Square,
                                                    scale=float(width) ** -0.5, accum_out=ms[:, t, s:s + 1]))
                if piece:
                    hi_piece(act, piece_base[0], 0, piece_base[0] // 2, piece)
                for k in range(kt):
                    act.wait_ge(turned, k + 1)
                    nc.scalar.activation(dst_hi[:, k, :], bank[k % 8][:, :], ACT.Copy,
                                         scale=gain[:, k:k + 1] if gain is not None else 1.0
                                         ).then_inc(hi_made, 1)

            @block.gpsimd
            def _(pool):
                o = Order(pool, pool_o)
                for t in range(NT if norm else 0):
                    n = len(norm)
                    pool.wait_ge(act_o, n * (t + 1))
                    o.link(nc.gpsimd.tensor_scalar(ms[:, t, 0:n], ms[:, t, 0:n], EPS, None, ALU.add))
                    nc.gpsimd.tensor_tensor(ms[:, t, 0:n], ms[:, t, 0:n], minus_half[:, 0:n],
                                            ALU.pow).then_inc(factor, 1)
                if piece:
                    lo_piece(pool, piece_base[0], 0, piece)

            @block.vector
            def _(dve):
                for t in range(NT if norm else 0):
                    dve.wait_ge(factor, t + 1)
                    for s, (c0, width) in enumerate(norm):
                        last = nc.vector.tensor_scalar(normed[:, t, c0:c0 + width], src[:, t, c0:c0 + width],
                                                       ms[:, t, s:s + 1], None, ALU.mult)
                    last.then_inc(scaled, 1)
                for k in range(kt):
                    dve.wait_ge(hi_made, k + 1)
                    g = gain[:, k:k + 1] if gain is not None else 1.0
                    nc.vector.scalar_tensor_tensor(dst_lo[:, k, :], bank[k % 8][:, :], g,
                                                   dst_hi[:, k, :].bitcast(F32), ALU.mult,
                                                   ALU.subtract).then_inc(lo_made, 1)

            @block.tensor
            def _(pe):
                if norm:
                    pe.wait_ge(scaled, NT)
                for k in range(kt):
                    if k >= 8:
                        pe.wait_ge(lo_made, k - 7)
                    for t in range(NT):
                        last = nc.tensor.transpose(bank[k % 8][:, t * P:(t + 1) * P],
                                                   normed[:, t, k * P:(k + 1) * P], ident[:, :])
                    last.then_inc(turned, 1)

        def run_stream(ctx, loops, act_hi, act_lo, evacuate, loaded=2, split=1, ahead=((), 0), after=None,
                       behind=None):
            load, split_hi, split_lo, products, evacuation = stream(
                ctx, loops, act_hi, act_lo, evacuate, loaded, split, ahead, behind)
            block = ctx.enter_context(nc.Block())

            @block.sync
            def _(sp):
                load(sp)
                if after:
                    after(sp)

            @block.scalar
            def _(act):
                split_hi(act)

            @block.gpsimd
            def _(pool):
                split_lo(pool)

            @block.tensor
            def _(pe):
                products(pe)

            @block.vector
            def _(dve):
                evacuation(dve)

        with ExitStack() as layer:
            z_sb = sb(layer, "z_sb", [P, NT, ZZ])
            with ExitStack() as proj:
                c_hi = sb(layer, "c_hi", [P, KQ + KKV, SEQ], F32R)
                c_lo = sb(layer, "c_lo", [P, KQ + KKV, SEQ], F32R)
                kpe_sb = sb(layer, "kpe_sb", [P, NT, ROPE])
                kpe_ms = sb(layer, "kpe_ms", [P, NT, 2])
                c_sb = sb(proj, "c_sb", [P, NT, CC])
                with ExitStack() as ph:
                    h_hi = sb(ph, "h_hi", [P, DM // P, SEQ], F32R)
                    h_lo = sb(ph, "h_lo", [P, DM // P, SEQ], F32R)
                    with ExitStack() as ctx:
                        transpose_block(ctx, "x0", x_sb, DM // P, g_x[:, 0, :], h_hi, h_lo, norm=[(0, DM)],
                                        piece=CC // 2)
                    with ExitStack() as ctx:
                        def evacuate(what, t, c0, width, acc):
                            dst = {"c": c_sb, "z": z_sb}[what]
                            return nc.vector.tensor_copy(dst[:, t, bass.ds(c0, width)], acc)

                        def silu_z(c0, width):
                            at = z_sb[:, :, bass.ds(c0, width)]
                            nc.scalar.activation(at, at, ACT.Silu)
                        run_stream(ctx, [(mla_w_in[0], 0, CC // 2, 2, "c"), (mla_w_in[0], CC, CW, ZZ // CW, "z")],
                                   h_hi, h_lo, evacuate,
                                   ahead=(first_pieces(mla_w_out[0], 0, CW)[0:1], 0), behind=("z", silu_z))

                with ExitStack() as ctx:
                    rot = sb(ctx, "rot0", [P, 4, NT, HALF0])
                    junk = sb(ctx, "junk_pe", [P, ROPE])
                    dve_o, kpe_sq = sem("dve_o_pe"), sem("kpe_sq")
                    block = ctx.enter_context(nc.Block())

                    @block.scalar
                    def _(act):
                        for t in range(NT):
                            nc.scalar.activation(junk[:, :], c_sb[:, t, CQ + CKV:CC], ACT.Square,
                                                 scale=float(QK) ** -0.5, accum_out=kpe_ms[:, t, 1:2]
                                                 ).then_inc(kpe_sq, 1)
                            act.wait_ge(kpe_sq, t + 1)
                        last = z_sb[:, :, ZZ - CW:ZZ]
                        nc.scalar.activation(last, last, ACT.Silu)

                    @block.vector
                    def _(dve):
                        o = Order(dve, dve_o)
                        o.link(nc.vector.memset(kpe_ms[:, :, 0:1], EPS))
                        pe_in = c_sb[:, :, CQ + CKV:CC]
                        dve.wait_ge(kpe_sq, NT)
                        for t in range(NT):
                            last = nc.vector.tensor_tensor(pe_in[:, t, :], pe_in[:, t, :], gk0[:, 0:ROPE], ALU.mult)
                        o.link(last)
                        x1, x2 = pe_in[:, :, 0:HALF0], pe_in[:, :, HALF0:ROPE]
                        cos, sin = tcos[:, 0:NT, 0:HALF0], tsin[:, 0:NT, 0:HALF0]
                        nc.vector.tensor_tensor(rot[:, 0], x1, cos, ALU.mult)
                        nc.vector.tensor_tensor(rot[:, 1], x2, sin, ALU.mult)
                        nc.vector.tensor_tensor(rot[:, 2], x2, cos, ALU.mult)
                        o.link(nc.vector.tensor_tensor(rot[:, 3], x1, sin, ALU.mult))
                        nc.vector.tensor_tensor(kpe_sb[:, :, 0:HALF0], rot[:, 0], rot[:, 1], ALU.subtract)
                        nc.vector.tensor_tensor(kpe_sb[:, :, HALF0:ROPE], rot[:, 2], rot[:, 3], ALU.add)
                        nc.vector.tensor_scalar(kpe_ms[:, :, 1:2], kpe_ms[:, :, 1:2], EPS, None, ALU.add)
                with ExitStack() as ctx:
                    transpose_block(ctx, "c", c_sb, KQ + KKV, g_c, c_hi, c_lo, norm=[(0, CQ), (CQ, CKV)])

            with ExitStack() as ctx:
                v_all = sb(ctx, "v_all", [P, NT, ZZ])
                head_w = lambda b: b[:, :, :].rearrange("p k c -> p (k c)")[:, 0:KQ * WQ + KKV * WKV]
                wh_raw, wh_hi, wh_lo = head_w(w_raw[1]), [head_w(b) for b in w_hi], [head_w(b) for b in w_lo]
                qn = sb(ctx, "qn", [P, NT, QK])
                kn = sb(ctx, "kn", [P, NT, QK])
                rot = sb(ctx, "rotq", [P, 4, 2, HALF0])
                sq_junk = sb(ctx, "sq_junk", [P, QK + NOPE])
                ms = sb(ctx, "ms_qk", [P, NT, 2])
                qkT_hi = [sb(ctx, f"qkT_hi{a}", [HQK, 4, SEQ], F32R) for a in range(2)]
                qkT_lo = [sb(ctx, f"qkT_lo{a}", [HQK, 4, SEQ], F32R) for a in range(2)]
                prob = sb(ctx, "prob", [P, 2, SEQ])
                probT = sb(ctx, "probT", [P, 2, SEQ])
                negmax = sb(ctx, "negmax", [P, 2, NT])
                rowsum = sb(ctx, "rowsum", [P, 2, NT])
                rinv = sb(ctx, "rinv", [P, NT])
                score_bank, pt_bank, o_bank = [bank[0], bank[1]], bank[2], bank[3]
                p_bank, x_bank = [bank[4], bank[5]], [bank[6], bank[7]]
                wh_landed, wh_hi_made, wh_ready = sem("wh_landed"), sem("wh_hi_made"), sem("wh_ready")
                p_done, squares, factors = sem("p_done"), sem("squares"), sem("factors")
                qk_scaled, qk_rotated, p_free = sem("qk_scaled"), sem("qk_rotated"), sem("p_free")
                x_free, v_out = sem("x_free"), sem("v_out")
                x_done, x_hi = sem("x_done"), sem("x_hi")
                s_done, max_done, exp_done = sem("s_done"), sem("max_done"), sem("exp_done")
                t_done, pt_ready, pv_done, o_free = sem("t_done"), sem("pt_ready"), sem("pv_done"), sem("o_free")
                act_sem, dve_sem, pool_sem = sem("act_o_mla"), sem("dve_o_mla"), sem("pool_o_mla")
                wq_of = lambda w, k: w[:, k * WQ:(k + 1) * WQ]
                wkv_of = lambda w, k: w[:, KQ * WQ + k * WKV:KQ * WQ + (k + 1) * WKV]
                block = ctx.enter_context(nc.Block())

                @block.sync
                def _(sp):
                    def load(n):
                        if positive(n):
                            sp.wait_ge(wh_ready, n)
                        sp.dma_start(wh_raw[:, 0:KQ * WQ].rearrange("p (k c) -> p k c", k=KQ),
                                     mla_w_uq[0].rearrange("(k p) c -> p k c", p=P)[:, :, bass.ds(n * WQ, WQ)]
                                     ).then_inc(wh_landed, 16)
                        sp.dma_start(wh_raw[:, KQ * WQ:].rearrange("p (k c) -> p k c", k=KKV),
                                     mla_w_ukv[0].rearrange("(k p) c -> p k c", p=P)[:, :, bass.ds(n * WKV, WKV)]
                                     ).then_inc(wh_landed, 16)
                    load(0)
                    with sp.Fori(1, H) as n:
                        load(n)

                def heads(eng, step):
                    with eng.Fori(0, H - 4, 2) as h:
                        step(h, 0, True, True)
                        step(h + 1, 1, True, True)
                    for h in range(H - 4, H):
                        step(h, h % 2, h + 1 < H, h + 2 < H)

                @block.tensor
                def _(pe):
                    def project(n, a, t):
                        if t == 0:
                            pe.wait_ge(wh_ready, n + 1)
                        if positive(4 * n + t - 1):
                            pe.wait_ge(p_free, 4 * n + t - 1)
                        tok = slice(t * P, (t + 1) * P)
                        for k in range(KQ):
                            mm3(nc, p_bank[t % 2][:, 0:WQ], (c_hi[:, k, tok], c_lo[:, k, tok]),
                                (wq_of(wh_hi[a], k), wq_of(wh_lo[a], k)), start=k == 0, stop=k == KQ - 1)
                        for k in range(KKV):
                            last = mm3(nc, p_bank[t % 2][:, WQ:WQ + WKV],
                                       (c_hi[:, KQ + k, tok], c_lo[:, KQ + k, tok]),
                                       (wkv_of(wh_hi[a], k), wkv_of(wh_lo[a], k)), start=k == 0, stop=k == KKV - 1)
                        last.then_inc(p_done, 1)

                    def turn(n, t):
                        if t % 2 == 0:
                            pe.wait_ge(qk_rotated, 2 * n + t // 2 + 1)
                        if positive(4 * n + t - 1):
                            pe.wait_ge(x_free, 4 * n + t - 1)
                        for part in range(4):
                            src = (qn, kn)[part // 2][:, t, (part % 2) * HQK:(part % 2 + 1) * HQK]
                            last = nc.tensor.transpose(x_bank[t % 2][0:HQK, part * P:(part + 1) * P], src, ident[:, :])
                        last.then_inc(x_done, 1)

                    def scores(h, a, i):
                        if i == 0:
                            pe.wait_ge(x_free, 4 * h + 4)
                        tok, keys = slice(i * P, (i + 1) * P), (i + 1) * P
                        dst = score_bank[i % 2]
                        for part in range(2):
                            mm3(nc, dst[:, 0:keys], (qkT_hi[a][:, part, tok], qkT_lo[a][:, part, tok]),
                                (qkT_hi[a][:, 2 + part, 0:keys], qkT_lo[a][:, 2 + part, 0:keys]),
                                start=part == 0, stop=False)
                        nc.tensor.matmul(dst[:, tok], identb[:, :], causal[:, :], start=False,
                                         stop=True).then_inc(s_done, 1)

                    def turn_probs(h, i):
                        pe.wait_ge(exp_done, 4 * h + i + 1)
                        if i == NT - 1:
                            pe.wait_ge(pt_ready, 4 * h + i)
                        for j in range(i + 1):
                            last = nc.tensor.transpose(pt_bank[:, j * P:(j + 1) * P],
                                                       prob[:, i % 2, j * P:(j + 1) * P], ident[:, :])
                        last.then_inc(t_done, 1)

                    def values(h, i):
                        pe.wait_ge(pt_ready, 4 * h + i + 1)
                        pe.wait_ge(o_free, 4 * h + i + 1)
                        for j in range(i + 1):
                            last = nc.tensor.matmul(o_bank[:, 0:DV0], probT[:, i % 2, j * P:(j + 1) * P],
                                                    v_all[:, j, bass.ds(h * DV0, DV0)],
                                                    start=j == 0, stop=j == i)
                        last.then_inc(pv_done, 1)

                    def step(h, a, x, p):
                        for i in range(NT):
                            scores(h, a, i)
                            if x:
                                turn(h + 1, i)
                            if i >= 2:
                                values(h, i - 2)
                            if i >= 1:
                                turn_probs(h, i - 1)
                            if p:
                                project(h + 2, a, i)
                        turn_probs(h, 3)
                        values(h, 2)
                        values(h, 3)

                    for t in range(NT):
                        project(0, 0, t)
                    for t in range(NT):
                        turn(0, t)
                        project(1, 1, t)
                    heads(pe, step)

                @block.scalar
                def _(act):
                    def split_weights(n, a):
                        act.wait_ge(wh_landed, 32 * n + 32)
                        if positive(n - 1):
                            act.wait_ge(p_done, 4 * n - 4)
                        nc.scalar.activation(wh_hi[a][:, :], wh_raw[:, :], ACT.Copy).then_inc(wh_hi_made, 1)

                    def stats(n, t):
                        act.wait_ge(p_done, 4 * n + t + 1)
                        if t or positive(n):
                            act.wait_ge(squares, 4 * n + t)
                        src = p_bank[t % 2]
                        nc.scalar.activation(sq_junk[:, 0:QK], src[:, 0:QK], ACT.Square, scale=float(QK) ** -0.5,
                                             accum_out=ms[:, t, 0:1])
                        nc.scalar.activation(sq_junk[:, QK:], src[:, QK:QK + NOPE], ACT.Square,
                                             scale=float(QK) ** -0.5, accum_out=ms[:, t, 1:2]).then_inc(squares, 1)
                        nc.scalar.activation(v_all[:, t, bass.ds(n * DV0, DV0)], src[:, QK + NOPE:QK + NOPE + DV0],
                                             ACT.Copy).then_inc(v_out, 1)

                    def high(n, a, t):
                        act.wait_ge(x_done, 4 * n + t + 1)
                        nc.scalar.activation(qkT_hi[a][:, :, t * P:(t + 1) * P],
                                             x_bank[t % 2][0:HQK, :].rearrange("p (a t) -> p a t", a=4),
                                             ACT.Copy).then_inc(x_hi, 1)

                    def exponential(h, a, i):
                        act.wait_ge(max_done, 4 * h + i + 1)
                        keys = (i + 1) * P
                        nc.scalar.activation(prob[:, i % 2, 0:keys], score_bank[i % 2][:, 0:keys], ACT.Exp,
                                             bias=negmax[:, a, i:i + 1], accum_out=rowsum[:, a, i:i + 1]
                                             ).then_inc(exp_done, 1)

                    def probs_out(h, i):
                        act.wait_ge(t_done, 4 * h + i + 1)
                        nc.scalar.activation(probT[:, i % 2, 0:(i + 1) * P], pt_bank[:, 0:(i + 1) * P],
                                             ACT.Copy).then_inc(pt_ready, 1)

                    def step(h, a, x, p):
                        for i in range(NT):
                            exponential(h, a, i)
                            if x:
                                high(h + 1, 1 - a, i)
                            if i == 0 and (not isinstance(h, int) or h + 3 < H):
                                split_weights(h + 3, 1 - a)
                            if i >= 2:
                                probs_out(h, i - 1)
                            if p:
                                stats(h + 2, i)

                    split_weights(0, 0)
                    split_weights(1, 1)
                    for t in range(NT):
                        stats(0, t)
                    split_weights(2, 0)
                    for t in range(NT):
                        high(0, 0, t)
                        stats(1, t)
                    heads(act, step)

                @block.gpsimd
                def _(pool):
                    o = Order(pool, pool_sem)

                    def factor(n, t):
                        pool.wait_ge(squares, 4 * n + t + 1)
                        o.link(nc.gpsimd.tensor_tensor(ms[:, t, :], ms[:, t, :], kpe_ms[:, t, :], ALU.add))
                        nc.gpsimd.tensor_tensor(ms[:, t, :], ms[:, t, :], minus_half[:, 0:2],
                                                ALU.pow).then_inc(factors, 1)
                        pool.wait_ge(factors, 4 * n + t + 1)
                        nc.gpsimd.tensor_tensor(kn[:, t, 0:ROPE], kpe_sb[:, t, :],
                                                ms[:, t, 1:2].to_broadcast([P, ROPE]), ALU.mult)

                    def rotate(n, a):
                        pool.wait_ge(qk_scaled, 4 * n + 2 * a + 2)
                        tt = slice(2 * a, 2 * a + 2)
                        x1, x2 = qn[:, tt, 0:HALF0], qn[:, tt, HALF0:ROPE]
                        cos, sin = tcos[:, tt, 0:HALF0], tsin[:, tt, 0:HALF0]
                        nc.gpsimd.tensor_tensor(rot[:, 0], x1, cos, ALU.mult)
                        nc.gpsimd.tensor_tensor(rot[:, 1], x2, sin, ALU.mult)
                        nc.gpsimd.tensor_tensor(rot[:, 2], x2, cos, ALU.mult)
                        o.link(nc.gpsimd.tensor_tensor(rot[:, 3], x1, sin, ALU.mult))
                        nc.gpsimd.tensor_tensor(x1, rot[:, 0], rot[:, 1], ALU.subtract)
                        nc.gpsimd.tensor_tensor(x2, rot[:, 2], rot[:, 3], ALU.add).then_inc(qk_rotated, 1)
                        pool.wait_ge(qk_rotated, 2 * n + a + 1)

                    with pool.Fori(0, H) as n:
                        o.enter(n, 6)
                        for a in range(2):
                            factor(n, 2 * a)
                            factor(n, 2 * a + 1)
                            rotate(n, a)
                        o.leave(H)

                @block.vector
                def _(dve):
                    o = Order(dve, dve_sem)

                    def split_weights(n, a):
                        dve.wait_ge(wh_hi_made, n + 1)
                        nc.vector.tensor_tensor(wh_lo[a][:, :], wh_raw[:, :], wh_hi[a][:, :].bitcast(F32),
                                                ALU.subtract).then_inc(wh_ready, 1)

                    def scale(n, t):
                        dve.wait_ge(v_out, 4 * n + t + 1)
                        dve.wait_ge(factors, 4 * n + t + 1)
                        src = p_bank[t % 2]
                        nc.vector.scalar_tensor_tensor(qn[:, t, :], src[:, 0:QK], ms[:, t, 0:1], gq0[:, :],
                                                       ALU.mult, ALU.mult).then_inc(qk_scaled, 1)
                        nc.vector.scalar_tensor_tensor(kn[:, t, ROPE:QK], src[:, QK:QK + NOPE],
                                                       ms[:, t, 1:2], gk0[:, ROPE:QK], ALU.mult,
                                                       ALU.mult).then_inc(p_free, 1)

                    def low(n, a, t):
                        dve.wait_ge(x_hi, 4 * n + t + 1)
                        at = slice(t * P, (t + 1) * P)
                        nc.vector.tensor_tensor(qkT_lo[a][:, :, at],
                                                x_bank[t % 2][0:HQK, :].rearrange("p (a t) -> p a t", a=4),
                                                qkT_hi[a][:, :, at].bitcast(F32), ALU.subtract).then_inc(x_free, 1)

                    def maximum(h, a, i):
                        dve.wait_ge(s_done, 4 * h + i + 1)
                        nc.vector.tensor_reduce(negmax[:, a, i:i + 1], score_bank[i % 2][:, 0:(i + 1) * P], AX.X,
                                                ALU.max, negate=True).then_inc(max_done, 1)

                    def probs_out(h, i):
                        dve.wait_ge(t_done, 4 * h + i + 1)
                        nc.vector.tensor_copy(probT[:, i % 2, 0:(i + 1) * P],
                                              pt_bank[:, 0:(i + 1) * P]).then_inc(pt_ready, 1)

                    def gate(h, a, i):
                        o.link(nc.vector.reciprocal(rinv[:, i:i + 1], rowsum[:, a, i:i + 1]))
                        dve.wait_ge(pv_done, 4 * h + i + 1)
                        at = z_sb[:, i, bass.ds(h * DV0, DV0)]
                        nc.vector.scalar_tensor_tensor(at, o_bank[:, 0:DV0], rinv[:, i:i + 1], at, ALU.mult,
                                                       ALU.mult).then_inc(o_free, 1)

                    def step(h, a, x, p):
                        for i in range(NT):
                            maximum(h, a, i)
                            if x:
                                low(h + 1, 1 - a, i)
                            if i == 0 and (not isinstance(h, int) or h + 3 < H):
                                split_weights(h + 3, 1 - a)
                            if i == 1:
                                probs_out(h, 0)
                            if i >= 2:
                                gate(h, a, i - 2)
                            if p and i >= 1:
                                scale(h + 2, i - 1)
                        probs_out(h, 3)
                        gate(h, a, 2)
                        if p:
                            scale(h + 2, 3)
                        gate(h, a, 3)

                    nc.vector.memset(rinv[:, :], 1.0).then_inc(o_free, 1)
                    dve.wait_ge(o_free, 1)
                    split_weights(0, 0)
                    split_weights(1, 1)
                    for t in range(NT):
                        scale(0, t)
                    split_weights(2, 0)
                    for t in range(NT):
                        low(0, 0, t)
                        scale(1, t)
                    with dve.Fori(0, H - 4, 2) as h:
                        o.base, o.n = h * NT, 0
                        step(h, 0, True, True)
                        step(h + 1, 1, True, True)
                    o.base, o.n = (H - 4) * NT, 0
                    for h in range(H - 4, H):
                        step(h, h % 2, h + 1 < H, h + 2 < H)

            with ExitStack() as ph:
                o_hi = sb(ph, "o_hi", [P, ZZ // P, SEQ], F32R)
                o_lo = sb(ph, "o_lo", [P, ZZ // P, SEQ], F32R)
                with ExitStack() as ctx:
                    transpose_block(ctx, "o0", z_sb, ZZ // P, None, o_hi, o_lo, piece=CW)
                with ExitStack() as ctx:
                    def evacuate(what, t, c0, width, acc):
                        at = x_sb[:, t, bass.ds(c0, width)]
                        return nc.vector.tensor_tensor(at, acc, at, ALU.add)
                    run_stream(ctx, [(mla_w_out[0], 0, CW, DM // CW, "x")], o_hi, o_lo, evacuate, loaded=1,
                               ahead=(first_pieces(nsa_w_in[0], 0, CW), 1))

        with ExitStack() as layer:
            z_sb = sb(layer, "z1_sb", [P, NT, Z1])
            mixer = ExitStack()
            qs = sb(mixer, "qs", [P, NT, QW])
            kv = sb(mixer, "kv", [P, NT, KVW + GW])
            gates = kv[:, :, KVW:KVW + GW]
            kcT_hi = sb(mixer, "kcT_hi", [DK, G, NC], F32R)
            kcT_lo = sb(mixer, "kcT_lo", [DK, G, NC], F32R)
            vcmp = sb(mixer, "vcmp", [NC, G, DV])
            with ExitStack() as ph:
                h_hi = sb(ph, "h1_hi", [P, DM // P, SEQ], F32R)
                h_lo = sb(ph, "h1_lo", [P, DM // P, SEQ], F32R)
                with ExitStack() as ctx:
                    transpose_block(ctx, "x1", x_sb, DM // P, g_x[:, 1, :], h_hi, h_lo, norm=[(0, DM)])
                with ExitStack() as ctx:
                    def evacuate(what, t, c0, width, acc):
                        dst = {"q": qs, "kv": kv}[what]
                        return nc.vector.tensor_copy(dst[:, t, bass.ds(c0, width)], acc)
                    run_stream(ctx, [(nsa_w_in[0], 0, CW, QW // CW, "q"),
                                     (nsa_w_in[0], QW, (KVW + GW) // 4, 4, "kv")], h_hi, h_lo, evacuate,
                               ahead=(first_pieces(nsa_w_in[0], QW + KVW + GW, CW), 1))

                with ExitStack() as ctx:
                    sq = [sb(ctx, f"sq1_{s}", [P, G * DK]) for s in range(2)]
                    rot = [sb(ctx, f"rot1_{s}", [P, 4, G, HALF1]) for s in range(2)]
                    ct = sb(ctx, "ct", [DK, G, SEQ])
                    w1 = sb(ctx, "w1", [DK, LCMP, DK])
                    w1v = w1[:, :, :].rearrange("d l e -> d (l e)")[0:DV, 0:LCMP * DV].rearrange("d (l e) -> d l e", e=DV)
                    w2k, w2v = sb(ctx, "w2k", [DK, DK]), sb(ctx, "w2v", [DV, DV])
                    pek, pev = sb(ctx, "pek", [LCMP, DK]), sb(ctx, "pev", [LCMP, DV])
                    pekT, pevT = sb(ctx, "pekT", [DK, LCMP]), sb(ctx, "pevT", [DV, LCMP])
                    biask, biasv = sb(ctx, "biask", [DK, 1]), sb(ctx, "biasv", [DV, 1])
                    hidk, hidv = sb(ctx, "hidk", [DK, G, NC]), sb(ctx, "hidv", [DV, G, NC])
                    kcmp = sb(ctx, "kcmp", [NC, G, DK])
                    item = []
                    for t in range(NT):
                        for b, c0 in ((1, KS), (2, KW)):
                            item.append((kv[:, t, c0:c0 + G * DK], gk1[:, b, :], t, P))
                    for t in range(NT):
                        for c0 in range(0, QW, G * DK):
                            item.append((qs[:, t, c0:c0 + G * DK], gq1[:, :], t, P))
                    KCMP = 16
                    item.insert(KCMP, (kcmp[:, :, :].rearrange("p g d -> p (g d)"), gk1[:, 0, :], NT, NC))
                    mean = sb(ctx, "mean1", [P, len(item), G])
                    small_in, w1_in, squared, averaged, factor1 = (sem(n) for n in (
                        "small_in", "w1_in", "squared1", "averaged1", "factor1"))
                    scaled1, multiplied1, pool_s, normed1, turned1, copied1 = (sem(n) for n in (
                        "scaled1", "multiplied1", "pool_o1", "normed1", "turned1", "copied1"))
                    hidden, hid_clear, kc_hi, gate_act, cmp_out = (sem(n) for n in (
                        "hidden", "hid_clear", "kc_hi", "gate_act", "cmp_out"))
                    p0, a0 = piece_base[0], acc_base[0]
                    CHUNKS = Z1 // CW
                    piece_base[0] += 2 * CHUNKS
                    next0 = piece_base[0]
                    acc_base[0] += NT * CHUNKS
                    wz = nsa_w_in[0].rearrange("(k p) c -> p k c", p=P)
                    block = ctx.enter_context(nc.Block())

                    T_KC, T_PE, T_HIDK, T_VC, T_HIDV, T_CMP, T_KCT = 4, 5, 6, 10, 11, 12, 13
                    C_KC, C_PE, C_BIASK, C_VC, C_BIASV = 4, 5, 6, 10, 11

                    @block.sync
                    def _(sp):
                        sp.dma_start(w1[:, :, :], nsa_w1_k[0].rearrange("(l d) e -> d l e", d=DK)).then_inc(w1_in, 16)
                        for dst, src in ((w2k[:, :], nsa_w2_k[0]), (w2v[:, :], nsa_w2_v[0]),
                                         (pek[:, :], nsa_pe_k[0]), (pev[:, :], nsa_pe_v[0])):
                            sp.dma_start(dst, src).then_inc(small_in, 16)
                        for g in range(2, 2 * CHUNKS):
                            c0 = QW + KVW + GW + g // 2 * CW
                            load_piece(sp, p0 + g, g % 2, wz[:, g % 2 * KP:(g % 2 + 1) * KP, c0:c0 + CW])
                        sp.wait_ge(turned1, T_HIDK)
                        sp.dma_start(w1v, nsa_w1_v[0].rearrange("(l d) e -> d l e", d=DV)).then_inc(w1_in, 16)
                        for j, src in enumerate(first_pieces(nsa_w_out[0], 0, CW)):
                            load_piece(sp, next0 + j, j, src)

                    @block.tensor
                    def _(pe):
                        def turn_c(c0, width, g, b):
                            for t in range(NT):
                                last = nc.tensor.transpose(bank[b][0:width, t * P:(t + 1) * P],
                                                           kv[:, t, c0 + g * width:c0 + (g + 1) * width], ident[:, :])
                            last.then_inc(turned1, 1)

                        def turn_kc():
                            for g in range(G):
                                turn_c(KC, DK, g, 4 + g)

                        def turn_pe():
                            pe.wait_ge(small_in, 64)
                            pe.wait_ge(copied1, 1)
                            nc.tensor.transpose(bank[4][0:DK, 0:LCMP], pek[:, :], ident[0:LCMP, 0:LCMP])
                            nc.tensor.transpose(bank[4][0:DV, LCMP:2 * LCMP], pev[:, :],
                                                ident[0:LCMP, 0:LCMP]).then_inc(turned1, 1)

                        def bias(w, peT, d, b, copies):
                            pe.wait_ge(copied1, copies)
                            for l in range(LCMP):
                                nc.tensor.matmul(bank[b][0:d, 0:1], w[:, l, :], peT[:, l:l + 1],
                                                 start=l == 0, stop=l == LCMP - 1)

                        def hidden_layer(w, d, b):
                            for l in range(LCMP):
                                rhs = ct[0:d, :, l:l + (NCMP - 1) * STRIDE + 1:STRIDE]
                                last = nc.tensor.matmul(bank[b][0:d, 0:G * NCMP].rearrange("p (g n) -> p g n", g=G),
                                                        w[:, l, :], rhs, start=l == 0, stop=l == LCMP - 1)
                            last.then_inc(turned1, 1)

                        def bias_k():
                            pe.wait_ge(w1_in, 16)
                            bias(w1, pekT, DK, 5, C_PE)

                        def turn_vc(half):
                            if half:
                                pe.wait_ge(copied1, C_BIASK + 2)
                            turn_c(VC, DV, 2 * half, 4)
                            turn_c(VC, DV, 2 * half + 1, 7)

                        def bias_v():
                            pe.wait_ge(w1_in, 32)
                            bias(w1v, pevT, DV, 4, C_VC)

                        def second_layers():
                            pe.wait_ge(hidden, 2)
                            for g in range(G):
                                nc.tensor.matmul(bank[5][0:NC, g * DK:(g + 1) * DK], hidk[:, g, :], w2k[:, :],
                                                 start=True, stop=True)
                            for g in range(G):
                                last = nc.tensor.matmul(bank[6][0:NC, g * DV:(g + 1) * DV], hidv[:, g, :], w2v[:, :],
                                                        start=True, stop=True)
                            last.then_inc(turned1, 1)

                        def turn_k_cmp():
                            pe.wait_ge(normed1, KCMP + 1)
                            for g in range(G):
                                last = nc.tensor.transpose(bank[7][0:DK, g * NC:(g + 1) * NC], kcmp[:, g, :],
                                                           ident[0:NC, 0:NC])
                            last.then_inc(turned1, 1)

                        beside = {0: turn_kc, 1: turn_pe, 2: bias_k, 3: lambda: hidden_layer(w1, DK, 6),
                                  4: lambda: turn_vc(0), 5: lambda: turn_vc(1), 6: bias_v,
                                  7: lambda: hidden_layer(w1v, DV, 7), 10: second_layers, 15: turn_k_cmp}
                        slot = 0
                        for c in range(CHUNKS):
                            for j in range(2):
                                pe.wait_ge(w_lo_made, p0 + 2 * c + j + 1)
                                for t in range(NT):
                                    if j == 0 and c > 0:
                                        pe.wait_ge(acc_free, a0 + NT * (c - 1) + t + 1)
                                    tok = slice(t * P, (t + 1) * P)
                                    for k in range(KP):
                                        kt = j * KP + k
                                        last = mm3(nc, bank[t][:, :], (h_hi[:, kt, tok], h_lo[:, kt, tok]),
                                                   (w_hi[j][:, k, :], w_lo[j][:, k, :]),
                                                   start=kt == 0, stop=kt == DM // P - 1)
                                    if j:
                                        last.then_inc(acc_done, 1)
                                    elif t == NT - 1:
                                        last.then_inc(w_used, 1)
                                    if slot in beside:
                                        beside[slot]()
                                    slot += 1
                                if j:
                                    nc.tensor.matmul(bank[5][0:1, 0:2], identb[:, 0:1], identb[:, 0:2], start=True,
                                                     stop=True).then_inc(w_used, 1)

                    @block.scalar
                    def _(act):
                        def high(g):
                            hi_piece(act, p0 + g, g % 2, (p0 + g) // 2, CW)

                        def square(n):
                            if n >= 2:
                                act.wait_ge(averaged, n - 1)
                            if n == KCMP:
                                act.wait_ge(cmp_out, 1)
                            src, _, _, rows = item[n]
                            nc.scalar.activation(sq[n % 2][0:rows, :], src, ACT.Square).then_inc(squared, 1)

                        def silu_z(c, t):
                            act.wait_ge(acc_done, a0 + NT * c + t + 1)
                            nc.scalar.activation(z_sb[:, t, c * CW:(c + 1) * CW], bank[t][:, :],
                                                 ACT.Silu).then_inc(acc_free, 1)

                        high(1)
                        nc.scalar.activation(gates[:, :, :], gates[:, :, :], ACT.Tanh, scale=0.5).then_inc(gate_act, 1)
                        for n in range(6):
                            square(n)
                        high(2)
                        for n in range(6, 9):
                            square(n)
                        for t in range(NT):
                            silu_z(0, t)
                            square(9 + t)
                        high(3)
                        act.wait_ge(hid_clear, 1)
                        for hid, bi, d, b, t_at, c_at in ((hidk, biask, DK, 6, T_HIDK, C_BIASK),
                                                          (hidv, biasv, DV, 7, T_HIDV, C_BIASV)):
                            act.wait_ge(turned1, t_at)
                            act.wait_ge(copied1, c_at)
                            nc.scalar.activation(hid[:, :, 0:NCMP],
                                                 bank[b][0:d, 0:G * NCMP].rearrange("p (g n) -> p g n", g=G),
                                                 ACT.Silu, bias=bi[:, 0:1]).then_inc(hidden, 1)
                        for n in range(9 + NT, len(item)):
                            square(n)
                        high(4)
                        for t in range(NT):
                            silu_z(1, t)
                        act.wait_ge(turned1, T_KCT)
                        nc.scalar.activation(kcT_hi[:, :, :], bank[7][0:DK, 0:G * NC].rearrange("p (g n) -> p g n", g=G),
                                             ACT.Copy).then_inc(kc_hi, 1)

                    @block.gpsimd
                    def _(pool):
                        o = Order(pool, pool_s)

                        def low(g):
                            lo_piece(pool, p0 + g, g % 2, CW)

                        def factor(n):
                            pool.wait_ge(averaged, n + 1)
                            m = mean[0:item[n][3], n, :]
                            o.link(nc.gpsimd.tensor_scalar(m, m, 1.0 / DK, EPS, ALU.mult, ALU.add))
                            nc.gpsimd.tensor_tensor(m, m, minus_half[0:item[n][3], 0:G], ALU.pow).then_inc(factor1, 1)

                        low(1)
                        nc.gpsimd.memset(hidk[:, :, :], 0.0)
                        nc.gpsimd.memset(hidv[:, :, :], 0.0).then_inc(hid_clear, 1)
                        for n in range(6):
                            factor(n)
                        low(2)
                        for n in range(6, 12):
                            factor(n)
                        low(3)
                        for n in range(12, len(item)):
                            factor(n)
                        low(4)

                    @block.vector
                    def _(dve):

                        def average(n):
                            rows = item[n][3]
                            dve.wait_ge(squared, n + 1)
                            nc.vector.tensor_reduce(mean[0:rows, n, :], sq[n % 2][0:rows, :].rearrange("p (g d) -> p g d", g=G),
                                                    AX.X, ALU.add).then_inc(averaged, 1)

                        def norm(n):
                            src, gain, t, rows = item[n]
                            dve.wait_ge(factor1, n + 1)
                            for g in range(G):
                                x = src[:, g * DK:(g + 1) * DK]
                                last = nc.vector.scalar_tensor_tensor(x, x, mean[0:rows, n, g:g + 1], gain[0:rows],
                                                                      ALU.mult, ALU.mult)
                            last.then_inc(scaled1, 1)

                        def halves(n):
                            x = item[n][0].rearrange("p (g d) -> p g d", g=G)
                            return x[:, :, 0:HALF1], x[:, :, HALF1:ROT], [rot[n % 2][0:item[n][3], a] for a in range(4)]

                        def products(n):
                            _, _, t, rows = item[n]
                            x1, x2, ro = halves(n)
                            cos = tcos[0:rows, t, HALF0:FREQS].unsqueeze(1).to_broadcast([rows, G, HALF1])
                            sin = tsin[0:rows, t, HALF0:FREQS].unsqueeze(1).to_broadcast([rows, G, HALF1])
                            dve.wait_ge(scaled1, n + 1)
                            if n >= 2:
                                dve.wait_ge(normed1, n - 1)
                            nc.vector.tensor_tensor(ro[0], x1, cos, ALU.mult)
                            nc.vector.tensor_tensor(ro[1], x2, sin, ALU.mult)
                            nc.vector.tensor_tensor(ro[2], x2, cos, ALU.mult)
                            nc.vector.tensor_tensor(ro[3], x1, sin, ALU.mult).then_inc(multiplied1, 1)

                        def rotate(n):
                            x1, x2, ro = halves(n)
                            dve.wait_ge(multiplied1, n + 1)
                            nc.vector.tensor_tensor(x1, ro[0], ro[1], ALU.subtract)
                            nc.vector.tensor_tensor(x2, ro[2], ro[3], ALU.add).then_inc(normed1, 1)

                        def copy_out(dst, b, rows, c0=0, c1=512):
                            nc.vector.tensor_copy(dst, bank[b][0:rows, c0:c1]).then_inc(copied1, 1)

                        def copies_k():
                            for g in range(G):
                                dve.wait_ge(turned1, g + 1)
                                copy_out(ct[:, g, :], 4 + g, DK)
                            dve.wait_ge(turned1, T_PE)
                            nc.vector.tensor_copy(pekT[:, :], bank[4][0:DK, 0:LCMP])
                            copy_out(pevT[:, :], 4, DV, LCMP, 2 * LCMP)

                        def bias_k():
                            dve.wait_ge(turned1, T_HIDK)
                            copy_out(biask[:, :], 5, DK, 0, 1)

                        def copies_v():
                            for g in range(G):
                                dve.wait_ge(turned1, T_HIDK + g + 1)
                                copy_out(ct[0:DV, g, :], (4, 7)[g % 2], DV)

                        def bias_v():
                            dve.wait_ge(turned1, T_HIDV)
                            copy_out(biasv[:, :], 4, DV, 0, 1)

                        def compressed():
                            dve.wait_ge(turned1, T_CMP)
                            nc.vector.tensor_copy(vcmp[:, :, :], bank[6][0:NC, 0:G * DV].rearrange("p (g d) -> p g d", g=G))
                            nc.vector.tensor_copy(kcmp[:, :, :], bank[5][0:NC, 0:G * DK].rearrange("p (g d) -> p g d", g=G)
                                                  ).then_inc(cmp_out, 1)

                        before = {2: copies_k, 8: bias_k, 10: copies_v, 13: bias_v, KCMP: compressed}
                        for n in range(len(item) + 3):
                            if n in before:
                                before[n]()
                            if 3 <= n:
                                rotate(n - 3)
                            if 2 <= n < len(item) + 2:
                                products(n - 2)
                            if n < len(item):
                                average(n)
                            if 1 <= n < len(item) + 1:
                                norm(n - 1)
                        dve.wait_ge(gate_act, 1)
                        nc.vector.tensor_scalar(gates[:, :, :], gates[:, :, :], 0.5, 0.5, ALU.mult, ALU.add)
                        dve.wait_ge(kc_hi, 1)
                        nc.vector.tensor_tensor(kcT_lo[:, :, :], bank[7][0:DK, 0:G * NC].rearrange("p (g n) -> p g n", g=G),
                                                kcT_hi[:, :, :].bitcast(F32), ALU.subtract)

            kT_hi = sb(mixer, "kT_hi", [DK, 2, G, SEQ], F32R)
            kT_lo = sb(mixer, "kT_lo", [DK, 2, G, SEQ], F32R)
            v_diag = sb(mixer, "v_diag", [P, G, NT, DV])

            with ExitStack() as ctx:
                kt_turned, kt_hi, kt_lo, spread, clear = (sem(n) for n in (
                    "kt_turned", "kt_hi", "kt_lo", "spread", "v_clear"))
                block = ctx.enter_context(nc.Block())

                @block.sync
                def _(sp):
                    sp.wait_ge(clear, 1)
                    for i in range(NT):
                        sp.dma_start(v_diag[i * NC:(i + 1) * NC, :, i, :], vcmp[:, :, :]).then_inc(spread, 16)
                    sp.wait_ge(spread, 16 * NT)

                @block.gpsimd
                def _(pool):
                    nc.gpsimd.memset(v_diag[:, :, :, :], 0.0).then_inc(clear, 1)

                @block.tensor
                def _(pe):
                    for u in range(2 * G):
                        c0, g = (KS, KW)[u // G], u % G
                        for t in range(NT):
                            last = nc.tensor.transpose(bank[u][0:DK, t * P:(t + 1) * P],
                                                       kv[:, t, c0 + g * DK:c0 + (g + 1) * DK], ident[:, :])
                        last.then_inc(kt_turned, 1)

                @block.scalar
                def _(act):
                    for u in range(2 * G):
                        act.wait_ge(kt_turned, u + 1)
                        nc.scalar.activation(kT_hi[:, u // G, u % G, :], bank[u][0:DK, :], ACT.Copy).then_inc(kt_hi, 1)

                @block.vector
                def _(dve):
                    for u in range(2 * G):
                        dve.wait_ge(kt_hi, u + 1)
                        nc.vector.tensor_tensor(kT_lo[:, u // G, u % G, :], bank[u][0:DK, :],
                                                kT_hi[:, u // G, u % G, :].bitcast(F32), ALU.subtract).then_inc(kt_lo, 1)

            with ExitStack() as ctx:
                U = 2 * NT
                q_stage = sb(ctx, "q_stage", [P, NT, DK])
                qT_hi = [sb(ctx, f"qT_hi{a}", [DK, SEQ], F32R) for a in range(2)]
                qT_lo = [sb(ctx, f"qT_lo{a}", [DK, SEQ], F32R) for a in range(2)]
                prob = sb(ctx, "prob1", [P, 3, SEQ])
                probT = sb(ctx, "probT1", [P, 2, SEQ])
                negmax = sb(ctx, "negmax1", [P, 2, U])
                sums = sb(ctx, "sums1", [P, 2, U])
                coef = sb(ctx, "coef1", [P, U])
                c_s = sb(ctx, "c_s", [P, NT, NC])
                c_e = sb(ctx, "c_e", [P, NT, NC])
                c_eT = sb(ctx, "c_eT", [P, P])
                c_max = sb(ctx, "c_max", [P, NT])
                c_sum = sb(ctx, "c_sum", [P, NT])
                c_coef = sb(ctx, "c_coef", [P, NT])
                o_sw = sb(ctx, "o_sw", [P, NT, 2, DV])
                o_c = sb(ctx, "o_c", [P, NT, DV])
                score_bank, pt_bank, o_bank, c_bank = bank[0:3], bank[3:5], bank[5:7], bank[7]
                x_done, x_hi, q_ready, q_staged = sem("x_done1"), sem("x_hi1"), sem("q_ready1"), sem("q_staged")
                s_done, max_done, exp_done = sem("s_done1"), sem("max_done1"), sem("exp_done1")
                t_done, pt_ready, pv_done = sem("t_done1"), sem("pt_ready1"), sem("pv_done1")
                pt_ready_act, coef_done = sem("pt_ready_act1"), sem("coef_done")
                c_done, c_left, c_shift, c_exp, ct_done, ct_ready, cv_done, cv_left = (sem(n) for n in (
                    "c_done", "c_left", "c_shift", "c_exp", "ct_done", "ct_ready", "cv_done", "cv_left"))
                o_left, mixed, dve_s, pool_s = sem("o_left"), sem("mixed"), sem("dve_o2"), sem("pool_o2")
                block = ctx.enter_context(nc.Block())
                by_act = (1, 3, 5, 6, 7)
                n_act, n_dve = len(by_act), U - len(by_act)
                keys_of = lambda u: (u // 2 + 1) * P

                def heads(eng, step):
                    step(0, 0, False, True)
                    step(1, 1, True, True)
                    with eng.Fori(1, H // 2 - 1) as pair:
                        step(2 * pair, 0, True, True)
                        step(2 * pair + 1, 1, True, True)
                    step(H - 2, 0, True, True)
                    step(H - 1, 1, True, False)

                @block.tensor
                def _(pe):
                    def turn_q(n):
                        pe.wait_ge(q_staged, n + 1)
                        for t in range(NT):
                            last = nc.tensor.transpose(c_bank[0:DK, t * P:(t + 1) * P],
                                                       q_stage[:, t, :], ident[:, :])
                        last.then_inc(x_done, 1)

                    def scores(h, a, u):
                        i, b = u // 2, u % 2
                        tok, keys = slice(i * P, (i + 1) * P), (i + 1) * P
                        dst = score_bank[u % 3]
                        mm3(nc, dst[:, 0:keys], (qT_hi[a][:, tok], qT_lo[a][:, tok]),
                            (kT_hi[:, b, h // HPG, 0:keys], kT_lo[:, b, h // HPG, 0:keys]), start=True, stop=False)
                        nc.tensor.matmul(dst[:, tok], identb[:, :], causal[:, :], start=False,
                                         stop=True).then_inc(s_done, 1)

                    def compressed_scores(h, a):
                        for i in range(NT):
                            tok = slice(i * P, (i + 1) * P)
                            last = mm3(nc, c_bank[:, i * NC:(i + 1) * NC], (qT_hi[a][:, tok], qT_lo[a][:, tok]),
                                       (kcT_hi[:, h // HPG, :], kcT_lo[:, h // HPG, :]), start=True, stop=True)
                        last.then_inc(c_done, 1)

                    def turn_probs(h, u):
                        pe.wait_ge(exp_done, U * h + u + 1)
                        for j in range(u // 2 + 1):
                            last = nc.tensor.transpose(pt_bank[u % 2][:, j * P:(j + 1) * P],
                                                       prob[:, u % 3, j * P:(j + 1) * P], ident[:, :])
                        last.then_inc(t_done, 1)

                    def values(h, a, u):
                        i, b = u // 2, u % 2
                        if u in by_act:
                            pe.wait_ge(pt_ready_act, n_act * h + by_act.index(u) + 1)
                        else:
                            pe.wait_ge(pt_ready, n_dve * h + u + 1 - sum(v < u for v in by_act))
                        if u == 0 and (not isinstance(h, int) or h >= 2):
                            pe.wait_ge(o_left, h - 1)
                        for j in range(i + 1):
                            c0 = (VS, VW)[b]
                            last = nc.tensor.matmul(o_bank[a][:, u * DV:(u + 1) * DV],
                                                    probT[:, u % 2, j * P:(j + 1) * P],
                                                    kv[:, j, bass.ds(c0 + (h // HPG) * DV, DV)],
                                                    start=j == 0, stop=j == i)
                        last.then_inc(pv_done, 1)

                    def step(h, a, prev, nxt):
                        for k in range(U):
                            if k < U - 2:
                                scores(h, a, k + 2)
                            turn_probs(h, k)
                            if k == 1 and nxt:
                                pe.wait_ge(c_left, h + 1)
                                turn_q(h + 1)
                            if k == 3:
                                if nxt:
                                    pe.wait_ge(q_ready, h + 2)
                                pe.wait_ge(c_exp, h + 1)
                                nc.tensor.transpose(c_bank[:, 0:P], c_e[:, :, :].rearrange("p i n -> p (i n)"),
                                                    ident[:, :]).then_inc(ct_done, 1)
                            if k == 5:
                                pe.wait_ge(ct_ready, h + 1)
                                nc.tensor.matmul(c_bank[:, 0:NT * DV], c_eT[:, :],
                                                 v_diag[:, h // HPG, :, :].rearrange("p i d -> p (i d)"),
                                                 start=True, stop=True).then_inc(cv_done, 1)
                            if k:
                                values(h, a, k - 1)
                            elif prev:
                                values(h - 1, 1 - a, U - 1)
                            if k == U - 1 and nxt:
                                pe.wait_ge(cv_left, h + 1)
                                compressed_scores(h + 1, 1 - a)
                            if k >= U - 2 and nxt:
                                scores(h + 1, 1 - a, k + 2 - U)

                    turn_q(0)
                    pe.wait_ge(q_ready, 1)
                    compressed_scores(0, 0)
                    scores(0, 0, 0)
                    scores(0, 0, 1)
                    heads(pe, step)
                    values(H - 1, 1, U - 1)

                @block.scalar
                def _(act):
                    def high(n, a):
                        act.wait_ge(x_done, n + 1)
                        nc.scalar.activation(qT_hi[a][:, :], c_bank[0:DK, :], ACT.Copy).then_inc(x_hi, 1)

                    def exponential(h, a, u):
                        act.wait_ge(max_done, U * h + u + 1)
                        nc.scalar.activation(prob[:, u % 3, 0:keys_of(u)], score_bank[u % 3][:, 0:keys_of(u)],
                                             ACT.Exp, bias=negmax[:, a, u:u + 1], accum_out=sums[:, a, u:u + 1]
                                             ).then_inc(exp_done, 1)

                    def step(h, a, prev, nxt):
                        for k in range(U):
                            if k < U - 2:
                                exponential(h, a, k + 2)
                            if k in by_act:
                                act.wait_ge(t_done, U * h + k + 1)
                                nc.scalar.activation(probT[:, k % 2, 0:keys_of(k)], pt_bank[k % 2][:, 0:keys_of(k)],
                                                     ACT.Copy).then_inc(pt_ready_act, 1)
                            if k == 1:
                                if nxt:
                                    high(h + 1, 1 - a)
                                act.wait_ge(c_shift, h + 1)
                                nc.scalar.activation(c_e[:, :, :], c_s[:, :, :], ACT.Exp).then_inc(c_exp, 1)
                            if k >= U - 2 and nxt:
                                exponential(h + 1, 1 - a, k + 2 - U)

                    high(0, 0)
                    exponential(0, 0, 0)
                    exponential(0, 0, 1)
                    heads(act, step)

                @block.gpsimd
                def _(pool):
                    o = Order(pool, pool_s)

                    def stage(n):
                        nc.gpsimd.tensor_copy(q_stage[:, :, :], qs[:, :, bass.ds(n * DK, DK)]).then_inc(q_staged, 1)

                    def mix(h):
                        pool.wait_ge(o_left, h + 1)
                        o.link(nc.gpsimd.tensor_tensor(o_c[:, :, :], o_c[:, :, :], o_sw[:, :, 0, :], ALU.add))
                        o.link(nc.gpsimd.tensor_tensor(o_c[:, :, :], o_c[:, :, :], o_sw[:, :, 1, :], ALU.add))
                        at = z_sb[:, :, bass.ds(h * DV, DV)]
                        nc.gpsimd.tensor_tensor(at, o_c[:, :, :], at, ALU.mult).then_inc(mixed, 1)

                    def step(h, a, prev, nxt):
                        if not isinstance(h, int) or h + 2 < H:
                            pool.wait_ge(x_done, h + 2)
                            stage(h + 2)
                        if prev:
                            o.base, o.n = 2 * (h - 1), 0
                            mix(h - 1)

                    stage(0)
                    pool.wait_ge(x_done, 1)
                    stage(1)
                    heads(pool, step)
                    mix(H - 1)

                @block.vector
                def _(dve):
                    o = Order(dve, dve_s)

                    def low(n, a):
                        dve.wait_ge(x_hi, n + 1)
                        nc.vector.tensor_tensor(qT_lo[a][:, :], c_bank[0:DK, :], qT_hi[a][:, :].bitcast(F32),
                                                ALU.subtract).then_inc(q_ready, 1)

                    def maximum(h, a, u):
                        dve.wait_ge(s_done, U * h + u + 1)
                        nc.vector.tensor_reduce(negmax[:, a, u:u + 1], score_bank[u % 3][:, 0:keys_of(u)],
                                                AX.X, ALU.max, negate=True).then_inc(max_done, 1)

                    def leave(h, a):
                        dve.wait_ge(exp_done, U * h + U)
                        o.link(nc.vector.reciprocal(coef[:, :], sums[:, a, :]))
                        two = coef[:, :].rearrange("p (i b) -> p i b", b=2)
                        nc.vector.tensor_tensor(two, two, gates[:, :, bass.ds(h * 3 + 1, 2)],
                                                ALU.mult).then_inc(coef_done, 1)
                        dve.wait_ge(coef_done, h + 1)
                        dve.wait_ge(pv_done, U * h + U)
                        nc.vector.tensor_tensor(o_sw[:, :, :, :].rearrange("p i b d -> p (i b) d"),
                                                o_bank[a][:, :].rearrange("p (u d) -> p u d", d=DV),
                                                coef[:, :].unsqueeze(2).to_broadcast([P, U, DV]),
                                                ALU.mult).then_inc(o_left, 1)

                    def step(h, a, prev, nxt):
                        o.base, o.n = 7 * h, 0
                        for k in range(U):
                            if k < U - 2:
                                maximum(h, a, k + 2)
                            if k == 0:
                                dve.wait_ge(c_done, h + 1)
                                nc.vector.tensor_tensor(c_s[:, :, :],
                                                        c_bank[:, 0:NT * NC].rearrange("p (i n) -> p i n", n=NC),
                                                        cmask[:, :, :], ALU.add).then_inc(c_left, 1)
                                dve.wait_ge(c_left, h + 1)
                                o.link(nc.vector.tensor_reduce(c_max[:, :], c_s[:, :, :], AX.X, ALU.max))
                                o.link(nc.vector.tensor_scalar(c_max[:, :], c_max[:, :], FLOOR, None, ALU.max))
                                nc.vector.tensor_tensor(c_s[:, :, :], c_s[:, :, :],
                                                        c_max[:, :].unsqueeze(2).to_broadcast([P, NT, NC]),
                                                        ALU.subtract).then_inc(c_shift, 1)
                            if k not in by_act:
                                dve.wait_ge(t_done, U * h + k + 1)
                                nc.vector.tensor_copy(probT[:, k % 2, 0:keys_of(k)],
                                                      pt_bank[k % 2][:, 0:keys_of(k)]).then_inc(pt_ready, 1)
                            if k == 1 and prev:
                                leave(h - 1, 1 - a)
                            elif k == 1:
                                o.link(nc.vector.memset(coef[:, :], 0.0))
                            if k == 2:
                                if nxt:
                                    low(h + 1, 1 - a)
                                dve.wait_ge(c_exp, h + 1)
                                o.link(nc.vector.tensor_reduce(c_sum[:, :], c_e[:, :, :], AX.X, ALU.add))
                                o.link(nc.vector.tensor_scalar(c_sum[:, :], c_sum[:, :], 1e-30, None, ALU.max))
                                o.link(nc.vector.reciprocal(c_coef[:, :], c_sum[:, :]))
                                o.link(nc.vector.tensor_tensor(c_coef[:, :], c_coef[:, :],
                                                               gates[:, :, bass.ds(h * 3, 1)].rearrange("p t g -> p (t g)"),
                                                               ALU.mult))
                            if k == 4:
                                dve.wait_ge(ct_done, h + 1)
                                nc.vector.tensor_copy(c_eT[:, :], c_bank[:, 0:P]).then_inc(ct_ready, 1)
                            if k == 6:
                                if prev:
                                    dve.wait_ge(mixed, h)
                                dve.wait_ge(cv_done, h + 1)
                                nc.vector.tensor_tensor(o_c[:, :, :],
                                                        c_bank[:, 0:NT * DV].rearrange("p (i d) -> p i d", d=DV),
                                                        c_coef[:, :].unsqueeze(2).to_broadcast([P, NT, DV]),
                                                        ALU.mult).then_inc(cv_left, 1)
                            if k >= U - 2 and nxt:
                                maximum(h + 1, 1 - a, k + 2 - U)
                        assert o.n == 7, o.n

                    low(0, 0)
                    maximum(0, 0, 0)
                    maximum(0, 0, 1)
                    heads(dve, step)
                    o.base, o.n = 7 * H, 0
                    leave(H - 1, 1)

            mixer.close()

            with ExitStack() as ph:
                o_hi = sb(ph, "o1_hi", [P, Z1 // P, SEQ], F32R)
                o_lo = sb(ph, "o1_lo", [P, Z1 // P, SEQ], F32R)
                with ExitStack() as ctx:
                    transpose_block(ctx, "o1", z_sb, Z1 // P, None, o_hi, o_lo)
                with ExitStack() as ctx:
                    def evacuate(what, t, c0, width, acc):
                        at = x_sb[:, t, bass.ds(c0, width)]
                        return nc.vector.tensor_tensor(at, acc, at, ALU.add)
                    stored, first_left = sem("stored"), acc_base[0]

                    def store(sp):
                        for c in range(DM // CW):
                            for t in range(NT):
                                sp.wait_ge(acc_free, first_left + c * NT + t + 1)
                                cols = slice(c * CW, (c + 1) * CW)
                                sp.dma_start(out[0, t * P:(t + 1) * P, cols], x_sb[:, t, cols]).then_inc(stored, 16)
                        sp.wait_ge(stored, 16 * NT * (DM // CW))
                    run_stream(ctx, [(nsa_w_out[0], 0, CW, DM // CW, "x")], o_hi, o_lo, evacuate, after=store)


_INS = ["x", "positions", "inv_freq", "norm_g", "mla_w_in", "mla_g_cq", "mla_w_uq", "mla_g_ckv", "mla_w_ukv",
        "mla_g_q", "mla_g_k", "mla_w_out", "nsa_w_in", "nsa_g_q", "nsa_g_k", "nsa_pe_k", "nsa_w1_k",
        "nsa_w2_k", "nsa_pe_v", "nsa_w1_v", "nsa_w2_v", "nsa_w_out"]


def kernel(**inputs):
    import concourse.bacc as bacc
    from concourse.bass_utils import run_bass_kernel_spmd

    inputs["inv_freq"] = np.concatenate(
        [THETA ** (-np.arange(half) / half) for half in (HALF0, HALF1)]).astype(np.float32)
    nc = bacc.Bacc("TRN2", target_bir_lowering=False, num_devices=1)
    arrays, args = {}, []
    for name in _INS:
        a = np.ascontiguousarray(inputs[name])
        arrays[f"in_{name}"] = a
        args.append(nc.dram_tensor(f"in_{name}", a.shape, mybir.dt.from_np(a.dtype), kind="ExternalInput").ap())
    out = nc.dram_tensor("out_0", (1, SEQ, DM), F32, kind="ExternalOutput").ap()
    trunk(nc, *args, out)
    r = run_bass_kernel_spmd(nc, [arrays], core_ids=[0])
    return r.results[0]["out_0"]
```
